# Optimizing a Trainium2 kernel written in Bass

```python
import math
import jax, jax.numpy as jnp
from jax import lax
import numpy as np

D_MODEL = 1024
BATCH = 1
SEQ = 512
DEPTH = 1
DEC_BATCH = 8
DEC_SEQ = 1
PAST_LEN = 4096
PAGE_SIZE = 128

GLA_HEADS = 4
GLA_DK = 128
GLA_DV = 256
GLA_GATE_RANK = 16
GLA_GATE_NORMALIZER = 16.0
HGRN_HEADS = 8
HGRN_DK = 128
HGRN_DV = 128
CHUNK = 64
N_EXPERTS = 64
N_GROUPS = 8
TOPK_GROUPS = 4
TOP_K = 8
D_EXPERT = 256
D_SHARED = 256
ROUTED_SCALE = 2.5
DN_ALPHA = (2.0 * DEPTH) ** 0.25
DN_BETA = (8.0 * DEPTH) ** -0.25
EPS = 1e-5

GLA_QK = GLA_HEADS * GLA_DK
GLA_V = GLA_HEADS * GLA_DV
HGRN_K = HGRN_HEADS * HGRN_DK
HGRN_V = HGRN_HEADS * HGRN_DV
IN_SPLITS = (GLA_QK, GLA_QK, GLA_V, GLA_V, GLA_GATE_RANK, HGRN_K, HGRN_K, HGRN_V, HGRN_V, D_MODEL, D_MODEL)
IN_WIDTH = sum(IN_SPLITS)

kernel_name = 'hybrid_gla_hgrn2_moe_deepnorm_adaln_step'

def _split_cols(z):
    out, start = [], 0
    for w in IN_SPLITS:
        out.append(z[..., start:start + w])
        start += w
    return out

def _rmsnorm(x, w):
    xf = x.astype(jnp.float32)
    return xf * lax.rsqrt(jnp.mean(xf * xf, axis=-1, keepdims=True) + EPS) * w.astype(jnp.float32)

def _layernorm(x, g, b):
    xf = x.astype(jnp.float32)
    mu = jnp.mean(xf, axis=-1, keepdims=True)
    var = jnp.mean(jnp.square(xf - mu), axis=-1, keepdims=True)
    return ((xf - mu) * lax.rsqrt(var + EPS) * g.astype(jnp.float32) + b.astype(jnp.float32)).astype(x.dtype)

def _gated_linear_recurrence(q, k, v, log_a, s0):
    B, L, H, K = q.shape
    V = v.shape[-1]
    C = math.gcd(CHUNK, L)
    N = L // C

    def to_chunks(t):
        return t.astype(jnp.float32).reshape(B, N, C, H, t.shape[-1]).transpose(1, 0, 3, 2, 4)

    qc, kc, vc, gc = to_chunks(q), to_chunks(k), to_chunks(v), to_chunks(log_a)
    mask = jnp.tril(jnp.ones((C, C), dtype=bool))[:, :, None]

    def step(s, inp):
        qi, ki, vi, gi = inp
        b = jnp.cumsum(gi, axis=2)
        diff = b[:, :, :, None, :] - b[:, :, None, :, :]
        decay = jnp.exp(jnp.where(mask, diff, -jnp.inf))
        scores = jnp.einsum('bhik,bhjk,bhijk->bhij', qi, ki, decay)
        o = jnp.einsum('bhij,bhjv->bhiv', scores, vi) + jnp.einsum('bhik,bhkv->bhiv', qi * jnp.exp(b), s)
        b_last = b[:, :, -1:, :]
        s_new = s * jnp.exp(b_last[:, :, 0, :, None]) + jnp.einsum('bhjk,bhjv->bhkv', ki * jnp.exp(b_last - b), vi)
        return s_new, o

    s_final, o = lax.scan(step, s0.astype(jnp.float32), (qc, kc, vc, gc))
    o = o.transpose(1, 0, 3, 2, 4).reshape(B, L, H, V)
    return o, s_final.astype(s0.dtype)

def _token_mixer(h, s_gla, s_hgrn, layer, w_in, w_gk2, b_gk, hgrn_lb, gla_norm_w, hgrn_norm_w, w_proj_a, w_proj_b, w_out):
    B, L, _ = h.shape
    z = jnp.einsum('bld,de->ble', h, w_in)
    qa, ka, va, ga, gk_lr, qb, fb, ib, gb, ua, ub = _split_cols(z)
    f32 = jnp.float32
    log_a = jax.nn.log_sigmoid((jnp.einsum('blr,rk->blk', gk_lr, w_gk2) + b_gk).astype(f32)) / GLA_GATE_NORMALIZER
    oa, s_gla_new = _gated_linear_recurrence(
        qa.reshape(B, L, GLA_HEADS, GLA_DK).astype(f32) * GLA_DK ** -0.5,
        ka.reshape(B, L, GLA_HEADS, GLA_DK),
        va.reshape(B, L, GLA_HEADS, GLA_DV),
        log_a.reshape(B, L, GLA_HEADS, GLA_DK), s_gla)
    oa = _rmsnorm(oa, gla_norm_w) * jax.nn.silu(ga.reshape(B, L, GLA_HEADS, GLA_DV).astype(f32))
    lb = jnp.cumsum(jax.nn.softmax(hgrn_lb.astype(f32), axis=0), axis=0)[layer]
    forget = lb + (1.0 - lb) * jax.nn.sigmoid(fb.astype(f32))
    ob, s_hgrn_new = _gated_linear_recurrence(
        jax.nn.silu(qb.astype(f32)).reshape(B, L, HGRN_HEADS, HGRN_DK) * HGRN_DK ** -0.5,
        (1.0 - forget).reshape(B, L, HGRN_HEADS, HGRN_DK),
        ib.reshape(B, L, HGRN_HEADS, HGRN_DV),
        jnp.log(forget).reshape(B, L, HGRN_HEADS, HGRN_DK), s_hgrn)
    ob = _rmsnorm(ob, hgrn_norm_w) * jax.nn.sigmoid(gb.reshape(B, L, HGRN_HEADS, HGRN_DV).astype(f32))
    ya = jnp.einsum('ble,ed->bld', oa.reshape(B, L, GLA_V).astype(h.dtype), w_proj_a)
    yb = jnp.einsum('ble,ed->bld', ob.reshape(B, L, HGRN_V).astype(h.dtype), w_proj_b)
    merged = jax.nn.sigmoid(ua) * ya + jax.nn.sigmoid(ub) * yb
    return jnp.einsum('bld,de->ble', merged, w_out), s_gla_new, s_hgrn_new

def _moe(h, w_router, router_bias, w_exp_gate, w_exp_up, w_exp_down, w_sh_gate, w_sh_up, w_sh_down):
    B, L, D = h.shape
    t = h.reshape(B * L, D)
    scores = jax.nn.sigmoid(jnp.einsum('nd,de->ne', t, w_router).astype(jnp.float32))
    biased = scores + router_bias.astype(jnp.float32)
    grouped = biased.reshape(-1, N_GROUPS, N_EXPERTS // N_GROUPS)
    group_score = jnp.sum(lax.top_k(grouped, 2)[0], axis=-1)
    _, top_groups = lax.top_k(group_score, TOPK_GROUPS)
    group_mask = jnp.sum(jax.nn.one_hot(top_groups, N_GROUPS, dtype=jnp.float32), axis=1) > 0
    expert_mask = jnp.repeat(group_mask, N_EXPERTS // N_GROUPS, axis=1)
    _, idx = lax.top_k(jnp.where(expert_mask, biased, -jnp.inf), TOP_K)
    w = jnp.take_along_axis(scores, idx, axis=1)
    w = w / jnp.sum(w, axis=-1, keepdims=True) * ROUTED_SCALE
    gates = jnp.einsum('nk,nke->ne', w, jax.nn.one_hot(idx, N_EXPERTS, dtype=jnp.float32)).astype(h.dtype)

    def expert(acc, p):
        wg, wu, wd, g = p
        a = jax.nn.silu(t @ wg) * (t @ wu)
        return acc + g[:, None] * (a @ wd), None

    routed, _ = lax.scan(expert, jnp.zeros_like(t), (w_exp_gate, w_exp_up, w_exp_down, gates.T))
    shared = (jax.nn.silu(t @ w_sh_gate) * (t @ w_sh_up)) @ w_sh_down
    return (routed + shared).reshape(B, L, D)

def _trunk(x, c, s_gla, s_hgrn, w_ada, b_ada, w_in, w_gk2, b_gk, hgrn_lb, gla_norm_w, hgrn_norm_w,
           w_proj_a, w_proj_b, w_out, ln1_g, ln1_b, w_router, router_bias, w_exp_gate, w_exp_up,
           w_exp_down, w_sh_gate, w_sh_up, w_sh_down, ln2_g, ln2_b):
    new_gla, new_hgrn = [], []
    for l in range(DEPTH):
        mod = jnp.einsum('bd,de->be', jax.nn.silu(c), w_ada[l]) + b_ada[l]
        sh1, sc1, g1, sh2, sc2, g2 = [m[:, None, :] for m in jnp.split(mod, 6, axis=-1)]
        h = x * (1.0 + sc1) + sh1
        mix, sg, shh = _token_mixer(h, s_gla[l], s_hgrn[l], l, w_in[l], w_gk2[l], b_gk[l], hgrn_lb,
                                    gla_norm_w[l], hgrn_norm_w[l], w_proj_a[l], w_proj_b[l], w_out[l])
        x = _layernorm(DN_ALPHA * x + g1 * mix, ln1_g[l], ln1_b[l])
        h = x * (1.0 + sc2) + sh2
        ffn = _moe(h, w_router[l], router_bias[l], w_exp_gate[l], w_exp_up[l], w_exp_down[l],
                   w_sh_gate[l], w_sh_up[l], w_sh_down[l])
        x = _layernorm(DN_ALPHA * x + g2 * ffn, ln2_g[l], ln2_b[l])
        new_gla.append(sg)
        new_hgrn.append(shh)
    return x, jnp.stack(new_gla), jnp.stack(new_hgrn)

def setup_inputs(seed: int = 0) -> dict:
    key = jax.random.key(seed)
    ks = iter(jax.random.split(key, 40))
    nrm = lambda shape, s: jax.random.normal(next(ks), shape, jnp.float32) * s
    D = D_MODEL
    return {
        'x_prompt': nrm((BATCH, SEQ, D), 1.0),
        'x_sample': nrm((DEC_BATCH, DEC_SEQ, D), 1.0),
        'state_gla': nrm((DEPTH, DEC_BATCH, GLA_HEADS, GLA_DK, GLA_DV), 1.0),
        'state_hgrn': nrm((DEPTH, DEC_BATCH, HGRN_HEADS, HGRN_DK, HGRN_DV), 1.0),
        'c_prompt': nrm((BATCH, D), 1.0),
        'c_sample': nrm((DEC_BATCH, D), 1.0),
        'w_ada': nrm((DEPTH, D, 6 * D), 0.5 * D ** -0.5),
        'b_ada': nrm((DEPTH, 6 * D), 0.02),
        'w_in': nrm((DEPTH, D, IN_WIDTH), D ** -0.5),
        'w_gk2': nrm((DEPTH, GLA_GATE_RANK, GLA_QK), GLA_GATE_RANK ** -0.5),
        'b_gk': nrm((DEPTH, GLA_QK), 0.1),
        'hgrn_lb': nrm((DEPTH + 1, HGRN_K), 1.0),
        'gla_norm_w': 1.0 + nrm((DEPTH, GLA_DV), 0.02),
        'hgrn_norm_w': 1.0 + nrm((DEPTH, HGRN_DV), 0.02),
        'w_proj_a': nrm((DEPTH, GLA_V, D), GLA_V ** -0.5),
        'w_proj_b': nrm((DEPTH, HGRN_V, D), HGRN_V ** -0.5),
        'w_out': nrm((DEPTH, D, D), DN_BETA * D ** -0.5),
        'ln1_g': 1.0 + nrm((DEPTH, D), 0.02),
        'ln1_b': nrm((DEPTH, D), 0.02),
        'w_router': nrm((DEPTH, D, N_EXPERTS), D ** -0.5),
        'router_bias': nrm((DEPTH, N_EXPERTS), 0.01),
        'w_exp_gate': nrm((DEPTH, N_EXPERTS, D, D_EXPERT), D ** -0.5),
        'w_exp_up': nrm((DEPTH, N_EXPERTS, D, D_EXPERT), D ** -0.5),
        'w_exp_down': nrm((DEPTH, N_EXPERTS, D_EXPERT, D), DN_BETA * D_EXPERT ** -0.5),
        'w_sh_gate': nrm((DEPTH, D, D_SHARED), D ** -0.5),
        'w_sh_up': nrm((DEPTH, D, D_SHARED), D ** -0.5),
        'w_sh_down': nrm((DEPTH, D_SHARED, D), DN_BETA * D_SHARED ** -0.5),
        'ln2_g': 1.0 + nrm((DEPTH, D), 0.02),
        'ln2_b': nrm((DEPTH, D), 0.02),
    }

def reference(x_prompt, x_sample, state_gla, state_hgrn, c_prompt, c_sample, w_ada, b_ada, w_in, w_gk2, b_gk,
              hgrn_lb, gla_norm_w, hgrn_norm_w, w_proj_a, w_proj_b, w_out, ln1_g, ln1_b, w_router, router_bias,
              w_exp_gate, w_exp_up, w_exp_down, w_sh_gate, w_sh_up, w_sh_down, ln2_g, ln2_b):
    b_prompt = x_prompt.shape[0]
    zero_gla = jnp.zeros((DEPTH, b_prompt, GLA_HEADS, GLA_DK, GLA_DV), state_gla.dtype)
    zero_hgrn = jnp.zeros((DEPTH, b_prompt, HGRN_HEADS, HGRN_DK, HGRN_DV), state_hgrn.dtype)
    y_prompt, gla_prompt, hgrn_prompt = _trunk(
        x_prompt, c_prompt, zero_gla, zero_hgrn, w_ada, b_ada, w_in, w_gk2, b_gk, hgrn_lb, gla_norm_w,
        hgrn_norm_w, w_proj_a, w_proj_b, w_out, ln1_g, ln1_b, w_router, router_bias, w_exp_gate, w_exp_up,
        w_exp_down, w_sh_gate, w_sh_up, w_sh_down, ln2_g, ln2_b)
    y_sample, gla_sample, hgrn_sample = _trunk(
        x_sample, c_sample, state_gla, state_hgrn, w_ada, b_ada, w_in, w_gk2, b_gk, hgrn_lb, gla_norm_w,
        hgrn_norm_w, w_proj_a, w_proj_b, w_out, ln1_g, ln1_b, w_router, router_bias, w_exp_gate, w_exp_up,
        w_exp_down, w_sh_gate, w_sh_up, w_sh_down, ln2_g, ln2_b)
    return (y_prompt, y_sample, gla_prompt, hgrn_prompt, gla_sample, hgrn_sample)


_drawn_inputs = setup_inputs


def setup_inputs(seed=0):
    import zlib

    import numpy as np

    out = dict(_drawn_inputs(seed))
    spreads = {}
    factors = {'gla_norm_w': 97.698, 'hgrn_norm_w': 108.869, 'ln2_g': 28.643, 'ln2_b': 26.118}
    for name, (base, spread) in spreads.items():
        noise = np.random.default_rng([zlib.crc32(name.encode()), seed]).standard_normal(out[name].shape)
        drawn = base * np.exp(spread * noise) if base else spread * noise
        out[name] = __import__('jax').numpy.asarray(drawn.astype(out[name].dtype))
    for name, factor in factors.items():
        out[name] = (out[name] * factor).astype(out[name].dtype)
    return out
```

```python
from contextlib import ExitStack

import numpy as np
import concourse.bass as bass
from concourse import mybir

P = 128
D = 1024
KC = D // P
SEQ = 512
DEC = 8
NT = SEQ + DEC
HALF = NT // 2
CH = 128
NCH = SEQ // CH
LEV = 7
GH, GV = 4, 256
HH, HV = 8, 128
RANK = 16
NE, NG, TOPG, TOPK = 64, 8, 4, 8
FE = 256
TT = 5
MAXT = 96
TRASH = TT * P
ROWS = TRASH + P
ALPHA = 2.0 ** 0.25
EPS = 1e-5
RSCALE = 2.5
NCOND = 1 + DEC
BIG = 1e30

F32 = mybir.dt.float32
I32 = mybir.dt.int32
U32 = mybir.dt.uint32
ALU = mybir.AluOpType
ACT = mybir.ActivationFunctionType
AX = mybir.AxisListType.X

Q_ADA, Q_VA, Q_QA, Q_KA = 0, 12, 14, 15
Q_H = [(16, 17, 18), (19, 20, 21)]
Q_GA, Q_GB, Q_P, Q_O = 22, 24, 26, 34
NQ = 36

def columns(widths):
    at, out = 0, {}
    for name, w in widths:
        out[name] = (at, w)
        at += w
    return out, at

SMALL, NSMALL = columns([("cond", KC * NCOND), ("b_ada", 48), ("b_gk", GH), ("lb", 2 * HH), ("gla_w", 2),
                         ("hgrn_w", 1), ("ln1_g", KC), ("ln1_b", KC), ("ln2_g", KC), ("ln2_b", KC),
                         ("wgk1", KC * RANK)])
CONST, NCONST = columns([("ident", P), ("ones", P), ("mean", P), ("masks", 8 * P), ("reset", NT), ("mhalf", 1)])
ROUTE, NROUTE = columns([("tri", P), ("iota", P), ("group", NG), ("quads", MAXT // 4), ("part", 1),
                         ("trash", 1), ("token", TT), ("bias", NE), ("w", KC * NE)])


def constants():
    c = np.zeros((P, NCONST), np.float32)
    def put(table, arr, name, v):
        a, w = table[name]
        arr[:, a:a + w] = v
    j, i = np.arange(P)[:, None], np.arange(P)[None, :]
    put(CONST, c, "ident", np.eye(P))
    put(CONST, c, "ones", 1.0)
    put(CONST, c, "mean", 1.0 / D)
    masks = []
    for l in range(LEV):
        s = CH >> (l + 1)
        masks.append((j // (2 * s) == i // (2 * s)) & (j % (2 * s) < s) & (i % (2 * s) >= s))
    masks.append(j == i)
    put(CONST, c, "masks", np.stack(masks, 1).reshape(P, 8 * P))
    t = np.arange(NT)
    put(CONST, c, "reset", ((t % CH != 0) & (t < SEQ))[None, :])
    put(CONST, c, "mhalf", -0.5)
    r = np.zeros((P, NROUTE), np.float32)
    put(ROUTE, r, "tri", j < i)
    put(ROUTE, r, "iota", i)
    put(ROUTE, r, "group", np.arange(NG)[None, :])
    put(ROUTE, r, "quads", 4 * np.arange(MAXT // 4)[None, :])
    put(ROUTE, r, "part", j)
    put(ROUTE, r, "trash", TRASH + j)
    put(ROUTE, r, "token", j + P * np.arange(TT)[None, :])
    return c, r


def decoder_step(nc, xT, small, wgk2, const, route, wq, wexp, st_in, yT, st_prompt, st_out):
    with ExitStack() as ctx:
        def sb(name, n, dt=F32, p=P):
            return ctx.enter_context(nc.sbuf_tensor(name, [p, n], dt))

        def sem(name):
            return ctx.enter_context(nc.semaphore(name))

        h2rows = nc.dram_tensor("h2rows", [ROWS, D], F32, kind="Internal").ap()
        ffrows = nc.dram_tensor("ffrows", [ROWS, D], F32, kind="Internal").ap()
        etab_d = nc.dram_tensor("etab", [P, 1], F32, kind="Internal").ap()

        W = sb("W", 4 * 4096)
        Xb = sb("Xb", KC * NT)
        Hb = sb("Hb", KC * NT)
        OA = sb("OA", KC * NT)
        OB = sb("OB", KC * NT)
        work = sb("work", 16480)
        cst = sb("cst", NCONST)
        sml = sb("sml", NSMALL)
        gk2 = sb("gk2", GH * P, p=RANK)
        mod = sb("mod", 48 * NCOND)
        tiny = sb("tiny", 256)
        ints = sb("ints", 256, I32)
        ps = ctx.enter_context(nc.psum_tensor("ps", [P, 8, 512], F32))

        def view(buf, first, n, pattern=None, **kw):
            v = buf[:, first:first + n]
            return v.rearrange(pattern, **kw) if pattern else v

        def C(name):
            a, w = CONST[name]
            return cst[:, a:a + w]

        def S(name):
            a, w = SMALL[name]
            return sml[:, a:a + w]

        ident, ones = C("ident"), C("ones")
        ring = W[:, :].rearrange("p (s u c m) -> p s u c m", s=4, u=4, c=KC)
        X = Xb[:, :].rearrange("p (c t) -> p c t", c=KC)
        H = Hb[:, :].rearrange("p (c t) -> p c t", c=KC)
        oa = OA[:, :].rearrange("p (c t) -> p c t", c=KC)
        ob = OB[:, :].rearrange("p (c t) -> p c t", c=KC)
        md = mod[:, :].rearrange("p (e n) -> p e n", n=NCOND)
        SH1, SC1, G1, SH2, SC2, G2 = range(0, 48, 8)
        conds = S("cond").rearrange("p (c n) -> p c n", c=KC)
        V = view(work, 0, 4096, "p (t n) -> p t n", t=NCH)
        Qb, Kb, Gb = (view(work, 4096 + k * 4 * NT, 4 * NT) for k in range(3))
        q4, k4, g4 = (v.rearrange("p (h t) -> p h t", h=4) for v in (Qb, Kb, Gb))
        M = view(work, 10336, 5120, "p (b l t) -> p b l t", b=2, l=10)
        state = view(work, 15456, 768, "p (b v) -> p b v", b=3)
        Vs = Xb[0:DEC, 0:2048]
        sq_, sk_, sa_ = (view(Xb, 2048 + 96 * k, 96, "p (h b) -> p h b", b=DEC) for k in range(3))
        Pm = view(Xb, 2336, 1024)
        ST = view(Xb, 3360, 256, "p (b t) -> p b t", b=2)
        kdT = view(Xb, 3616, 256, "p (b t) -> p b t", b=2)
        gkl = Xb[0:RANK, 3640:3640 + NT]
        on = view(work, 16224, 256)
        elast = view(tiny, 0, 4, "p (b c) -> p b c", b=2)
        ssum = view(tiny, 4, 2)
        rstd = view(tiny, 6, 2)
        lbt = view(tiny, 16, 8)
        omlb = view(tiny, 24, 8)
        lbx = view(tiny, 40, 16, "p (r h) -> p r h", r=2)
        lbm = view(tiny, 56, 8)

        s_small, s_x, s_x2, s_route = sem("small_loaded"), sem("x_loaded"), sem("x_again"), sem("route_loaded")
        s_w = [sem(f"quad_loaded_{k}") for k in range(4)]
        s_wfree = sem("quad_used")
        s_cs = sem("cond_silu")
        s_mod, s_h = sem("mod_ready"), sem("h_ready")
        s_z, s_zev = sem("proj_done"), sem("proj_taken")
        s_lb = sem("lb_steps")
        s_gk = sem("gk_steps")
        s_kf, s_fk = sem("forget_ready"), sem("hgrn_k_ready")
        s_in, s_cum = sem("gates_in"), sem("cumsum_done")
        s_D, s_E, s_Mq, s_Mk = sem("diff_done"), sem("exp_done"), sem("mq_done"), sem("mk_done")
        s_kdt, s_kdc = sem("kd_transposed"), sem("kd_copied")
        s_sc, s_pm, s_st = sem("scores_done"), sem("scores_masked"), sem("scores_summed")
        s_o, s_ss, s_rs, s_rstd = sem("o_done"), sem("o_squares"), sem("o_ms"), sem("o_rstd")
        s_on, s_ot, s_oc = sem("o_scaled"), sem("o_transposed"), sem("o_copied")
        s_u, s_state, s_sout = sem("update_done"), sem("state_done"), sem("state_stored")
        s_rec = sem("group_done")
        s_smp = sem("sample_saved")
        paced = {e: sem(f"paced_{e}") for e in ("sp", "pe", "act", "dve", "pool")}

        def gate(eng, name, s, value):
            eng.wait_ge(s, value)
            eng.sem_inc(paced[name], 1)

        s_si, s_so = [sem("sin0"), sem("sin1")], [sem("sout0"), sem("sout1")]
        s_vm, s_vb, s_sa, s_sn, s_sop = sem("v_row"), sem("v_bcast"), sem("s_scaled"), sem("s_new"), sem("s_o")
        s_sn2 = sem("sample_norm")
        s_g1, s_g2, s_g3 = sem("gate_proj"), sem("gate_act"), sem("gate_mul")
        s_p1, s_p2, s_p3, s_p3a = sem("merge_proj"), sem("merge_act"), sem("merged"), sem("merge_parts")
        s_o1, s_o2 = sem("out_proj"), sem("resid")
        s_ln = sem("ln_steps")
        s_lnp = sem("ln_sums")
        s_lna = sem("ln_squares")
        s_lng = sem("ln_rstd")
        s_r1, s_r2, s_rv = sem("router_proj"), sem("router_sigmoid"), sem("route_steps")
        s_rp = sem("route_counts")
        s_tab = sem("table_sums")
        s_ab, s_abp = sem("onehots"), sem("onehots_used")
        s_row, s_et, s_T = sem("etab_stored"), sem("etab_back"), sem("etab_ready")
        s_ht, s_hc, s_hd = sem("h2_transposed"), sem("h2_copied"), [sem("h2_stored_0"), sem("h2_stored_1")]
        s_zero, s_hz = sem("zeroed"), sem("zeros_stored")
        s_shw, s_shd = sem("shared_gu"), sem("shared_down")
        s_gu = [sem(f"gu_loaded_{k}") for k in range(4)]
        s_dn = [sem(f"dn_loaded_{k}") for k in range(4)]
        s_guf, s_dnf = sem("gu_used"), sem("dn_used")
        s_ic, s_gc, s_xt, s_xc = sem("idx_col"), sem("gate_col"), sem("x_transposed"), sem("x_copied")
        s_hh, s_sg, s_a, s_at, s_ac = sem("hidden"), sem("hidden_silu"), sem("act_ready"), sem("act_transposed"), sem("act_copied")
        s_y, s_yc, s_add = sem("y_done"), sem("y_copied"), sem("y_added")
        s_ga = [sem("gathered_0"), sem("gathered_1")]
        t_hh, t_sg, t_a, t_at, t_ac = sem("sh_hidden"), sem("sh_silu"), sem("sh_act"), sem("sh_act_t"), sem("sh_act_c")
        t_y, t_yc, t_st = sem("sh_y"), sem("sh_y_copied"), [sem("sh_stored_0"), sem("sh_stored_1")]
        s_f1, s_f2, s_f3, s_f4 = sem("ff_loaded"), sem("ff_transposed"), sem("ff_resid"), sem("y_stored")
        s_fx, s_fy, s_msk = sem("x_scaled"), sem("decode_resid"), sem("mask_ready")

        block = ctx.enter_context(nc.Block())

        R0 = KC * NT - NROUTE - 8
        assert R0 > 2900
        rt = view(OB, R0, NROUTE)

        def R(name):
            a, w = ROUTE[name]
            return rt[:, a:a + w]

        scores = view(OB, 0, TT * NE, "p (t e) -> p t e", t=TT)
        biased = view(OB, 320, TT * NE, "p (t e) -> p t e", t=TT)
        msk = view(OB, 640, TT * NE, "p (t e) -> p t e", t=TT)
        pos = view(OB, 960, TT * NE, "p (t e) -> p t e", t=TT)
        gates = view(OB, 1280, TT * NE, "p (t e) -> p t e", t=TT)
        tmp = view(OB, 1600, TT * NE, "p (t e) -> p t e", t=TT)
        g8 = view(OB, 1920, TT * NG * 8, "p (t g k) -> p t g k", t=TT, g=NG)
        grp = view(OB, 2240, TT * NG, "p (t g) -> p t g", t=TT)
        gm = view(OB, 2280, TT * NG, "p (t g) -> p t g", t=TT)
        top = view(OB, 2320, TT * 8, "p (t k) -> p t k", t=TT)
        idxf = view(OB, 2360, TT * 8, "p (t k) -> p t k", t=TT)
        posk = view(OB, 2400, TT * 8, "p (t k) -> p t k", t=TT)
        gk = view(OB, 2440, TT * 8, "p (t k) -> p t k", t=TT)
        tilek = view(OB, 2480, TT * 8, "p (t k) -> p t k", t=TT)
        slotk = view(OB, 2520, TT * 8, "p (t k) -> p t k", t=TT)
        cnt = view(OB, 2560, NE)
        nti = view(OB, 2624, NE)
        incl = view(OB, 2688, NE)
        excl = view(OB, 2752, NE)
        cmp_ = view(OB, 2816, NE)
        gsum = view(tiny, 32, TT)
        ecol = view(tiny, 37, 1)
        erow = tiny[0:1, 64:64 + MAXT + 4]
        ui = ints[:, 0:TT * 8].bitcast(U32).rearrange("p (t k) -> p t k", t=TT)
        posi = ints[:, 40:80]
        hi_i, lo_i = ints[:, 80:120], ints[:, 120:160]
        idxt = view(OB, 2880, MAXT + 4)
        quadn = tiny[:, 180:181]
        oh = view(work, 0, TT * 8 * NE, "p (t k e) -> p t k e", t=TT, k=8)
        prod = view(work, 2560, TT * 8 * NE, "p (t k e) -> p t k e", t=TT, k=8)
        Aoh = view(work, 5120, 2 * P, "p (b s) -> p b s", b=2)
        Boh = view(work, 5376, 2 * 3 * MAXT, "p (b c t) -> p b c t", b=2, c=3)
        hrow = view(work, 6400, 2 * D, "p (b d) -> p b d", b=2)
        zrow = view(work, 8448, D)
        assert 8448 + D <= 10240
        WD = view(work, 0, 8192, "p (s f d) -> p s f d", s=4, f=2)
        GU = W[:, :].rearrange("p (s c f) -> p s c f", s=4, c=KC)
        xg = view(work, 8192, 2048, "p (b d) -> p b d", b=2)
        xe = view(work, 10240, 2048, "p (b c n) -> p b c n", b=2, c=KC)
        yb = view(work, 12288, 2048, "p (b d) -> p b d", b=2)
        av = view(work, 14336, 512, "p (b f) -> p b f", b=2)
        aT = view(work, 14848, 512, "p (b f n) -> p b f n", b=2, f=2)
        sg = view(work, 15360, 512, "p (b f) -> p b f", b=2)
        idx_i = view(work, 15872, MAXT + 4).bitcast(I32)
        gtabs = view(work, 15972, MAXT + 4)
        eti = work[0:1, 16072:16072 + MAXT + 4].bitcast(I32)
        qni = view(work, 16172, 1).bitcast(I32)
        idg = view(work, 16176, 4).bitcast(I32)
        ida = view(work, 16180, 4).bitcast(I32)
        gcol = view(work, 16184, 4)

        LSQ = view(work, 0, KC * NT, "p (c t) -> p c t", c=KC)
        lnr = view(work, 4160, 2 * NT)
        mg = view(work, 6000, KC * NT, "p (c t) -> p c t", c=KC)
        gtmp = view(work, 10200, 4 * HALF, "p (b t) -> p b t", b=4)
        sin = view(work, 0, 4096, "p (b n) -> p b n", b=2)
        snew = view(work, 4096, 4096, "p (b n) -> p b n", b=2)
        vm = view(work, 8192, 4096, "p (b n) -> p b n", b=2)
        oS = view(work, 12288, 128, "p (j b) -> p j b", b=DEC)
        oS2 = view(work, 12416, 128, "p (j b) -> p j b", b=DEC)
        oms = view(work, 12544, 128, "p (j b) -> p j b", b=DEC)

        GROUPS = [dict(heads=GH, v=GV, out=oa, first=0, kind="gla", qs=Q_QA, fs=Q_KA),
                  dict(heads=4, v=HV, out=ob, first=0, kind="hgrn", qs=Q_H[0][1], fs=Q_H[0][2]),
                  dict(heads=4, v=HV, out=ob, first=4, kind="hgrn", qs=Q_H[1][1], fs=Q_H[1][2])]
        halves = [(0, HALF), (HALF, NT)]

        def z_items():
            out = []
            for gi in range(3):
                nv = 2 if gi == 0 else 1
                for b in range(nv):
                    for t in range(TT):
                        out.append((gi, "v", b, t))
                if gi == 0:
                    for hf in range(2):
                        out.append((gi, "gl", 0, hf))
                    for h in range(4):
                        for hf in range(2):
                            out.append((gi, "g", h, hf))
                for what in ("q", "k"):
                    for h in range(4):
                        for hf in range(2):
                            out.append((gi, what, h, hf))
            return out

        ITEMS = z_items()


        def rows_stored(eng):
            eng.wait_ge(s_hd[0], 48)
            eng.wait_ge(s_hd[1], 32)
            eng.wait_ge(s_hz, 64)

        def used(q):
            if q < 12:
                return s_wfree, q + 1
            if q < Q_GA:
                n, last = 0, 0
                for gi, what, a, b in ITEMS:
                    n += 1
                    own = {"v": (Q_VA + a) if gi == 0 else Q_H[gi - 1][0], "q": GROUPS[gi]["qs"],
                           "k": GROUPS[gi]["fs"]}.get(what)
                    if own == q:
                        last = n
                return s_z, last
            if q < Q_P:
                return s_g1, 8 * (q - Q_GA + 1)
            if q < Q_O:
                return s_p1, 8 * (q - Q_P + 1)
            return s_o1, 8 * (q - Q_O + 1)

        LN0, LN1 = 0, 23

        def layer_norm_pe(pe, which):
            for what in range(2):
                if what:
                    pe.wait_ge(s_lna, 2 * which + 2)
                src = LSQ if what else X
                for hf, (lo, hi) in enumerate(halves):
                    for c in range(KC):
                        mm = pe.matmul(ps[:, 2 + 2 * what + hf, 0:HALF], C("mean"), src[:, c, lo:hi],
                                       start=(c == 0), stop=(c == KC - 1))
                    mm.then_inc(s_lnp, 1)

        def recurrence_pe(pe, gi):
            g = GROUPS[gi]
            v, base = g["v"], 16 * gi
            with pe.Fori(0, 4) as h:
                def at(s, value):
                    gate(pe, "pe", s, value)

                def scores_of(cc):
                    p, c = cc // 2, cc % 2
                    col_ = slice(c * CH, (c + 1) * CH)
                    at(s_Mk, h * 2 + (8 * gi + p + 1))
                    at(s_Mq, h * 2 + (8 * gi + p + 1))
                    at(s_kdc, h * 4 + (base + cc))
                    pe.transpose(ps[:, 2, 0:CH], M[:, p, 7, col_], ident).then_inc(s_kdt, 1)
                    at(s_pm, h * 4 + (base + cc))
                    for l in range(LEV):
                        pe.matmul(ps[:, l // 4, (l % 4) * CH:(l % 4 + 1) * CH], M[:, p, l, col_], M[:, p, l, col_],
                                  start=True, stop=True)
                    pe.matmul(ps[:, 1, 3 * CH:4 * CH], M[:, p, 9, col_], q4[:, bass.ds(h, 1), cc * CH:(cc + 1) * CH].rearrange("p a t -> p (a t)"),
                              start=True, stop=True).then_inc(s_sc, 1)

                def values(cc):
                    return V[:, cc, bass.ds(h * v, v)]

                def update(cc):
                    at(s_kdc, h * 4 + (base + cc + 1))
                    at(s_state, h * 4 + (base + cc))
                    pe.matmul(ps[:, 3, 0:v], kdT[:, cc % 2, :], values(cc), start=True, stop=True).then_inc(s_u, 1)

                def output(cc):
                    p, c = cc // 2, cc % 2
                    at(s_st, h * 4 + (base + cc + 1))
                    at(s_on, h * 4 + max(base + cc - 1, 0))
                    mm = pe.matmul(ps[:, 4 + cc % 2, 0:v], ST[:, cc % 2, :], values(cc), start=True, stop=(cc == 0))
                    if cc:
                        at(s_state, h * 4 + (base + cc))
                        mm = pe.matmul(ps[:, 4 + cc % 2, 0:v], M[:, p, 8, c * CH:(c + 1) * CH], state[:, cc % 2, 0:v],
                                       start=False, stop=True)
                    mm.then_inc(s_o, 1)

                def turn(cc):
                    at(s_on, h * 4 + (base + cc + 1))
                    at(s_oc, h * 4 + (base + cc))
                    for j in range(v // P):
                        mm = pe.transpose(ps[:, 6, j * P:(j + 1) * P], on[:, j * P:(j + 1) * P], ident)
                    mm.then_inc(s_ot, 1)

                scores_of(0)
                for cc in range(NCH):
                    update(cc)
                    if cc + 1 < NCH:
                        scores_of(cc + 1)
                    output(cc)
                    turn(cc)

        def layer_norm_act(act, which):
            for hf, (lo, hi) in enumerate(halves):
                act.wait_ge(s_ln, (LN0, LN1)[which] + 1 + hf)
                act.activation(LSQ[:, :, lo:hi], X[:, :, lo:hi], ACT.Square).then_inc(s_lna, 1)

        def recurrence_act(act, gi):
            g = GROUPS[gi]
            v, base = g["v"], 16 * gi
            act.wait_ge(s_cum, 4 * gi + 4)
            act.activation(sa_[:, 4 * gi:4 * gi + 4, :], g4[:, :, SEQ:NT], ACT.Exp).then_inc(s_smp, 1)
            if gi:
                act.wait_ge(s_kf, 4 * gi)
                act.wait_ge(s_fk, 2 * gi)
            with act.Fori(0, 4) as h:
                def at(s, value):
                    gate(act, "act", s, value)

                def factors(p):
                    at(s_D, h * 2 + (8 * gi + p + 1))
                    act.activation(M[:, p, 0:8, :], M[:, p, 0:8, :], ACT.Abs).then_inc(s_E, 1)
                    at(s_E, h * 10 + (40 * gi + 5 * p + 1))
                    act.activation(M[:, p, 0:8, :], M[:, p, 0:8, :], ACT.Exp, scale=-1.0).then_inc(s_E, 1)
                    gsrc = g4[:, bass.ds(h, 1), p * 256:(p + 1) * 256].rearrange("p a t -> p (a t)")
                    act.activation(M[:, p, 8, :], gsrc, ACT.Exp).then_inc(s_E, 1)
                    act.activation(M[:, p, 9, :], k4[:, bass.ds(h, 1), p * 256:(p + 1) * 256].rearrange("p a t -> p (a t)"), ACT.Copy).then_inc(s_E, 1)
                    act.activation(elast[:, p, :], g4[:, bass.ds(h, 1), p * 256 + 127:(p + 1) * 256:128].rearrange("p a t -> p (a t)"), ACT.Exp).then_inc(s_E, 1)

                def copy_kd(cc):
                    at(s_kdt, h * 4 + (base + cc + 1))
                    at(s_u, h * 4 + (base + max(cc - 1, 0)))
                    act.activation(kdT[:, cc % 2, :], ps[:, 2, 0:CH], ACT.Copy).then_inc(s_kdc, 1)

                def norm(cc):
                    at(s_o, h * 4 + (base + cc + 1))
                    at(s_ot, h * 4 + (base + cc))
                    act.activation(on[:, 0:v], ps[:, 4 + cc % 2, 0:v], ACT.Square, accum_out=ssum[:, cc % 2:cc % 2 + 1]).then_inc(s_ss, 1)
                    at(s_rstd, h * 4 + (base + cc + 1))
                    act.activation(on[:, 0:v], ps[:, 4 + cc % 2, 0:v], ACT.Copy, scale=rstd[:, cc % 2:cc % 2 + 1]).then_inc(s_on, 1)

                factors(0)
                copy_kd(0)
                factors(1)
                for cc in range(NCH):
                    if cc + 1 < NCH:
                        copy_kd(cc + 1)
                    norm(cc)

        def layer_norm_pool(pool, which):
            pool.wait_ge(s_ln, (LN0, LN1)[which] + 4)
            pool.tensor_tensor(lnr[:, NT:2 * NT], lnr[:, 0:NT], C("mhalf").broadcast_to([P, NT]), ALU.pow).then_inc(s_lng, 1)

        def layer_norm_dve(dve, which):
            base = (LN0, LN1)[which]
            g, b = S(f"ln{which + 1}_g"), S(f"ln{which + 1}_b")

            def wide(v):
                return v.rearrange("p (a t) -> p a t", a=1).broadcast_to([P, KC, v.shape[1]])

            for hf, (lo, hi) in enumerate(halves):
                dve.wait_ge(s_lnp, 4 * which + hf + 1)
                dve.tensor_tensor(X[:, :, lo:hi], X[:, :, lo:hi], wide(ps[:, 2 + hf, 0:HALF]), ALU.subtract).then_inc(s_ln, 1)
            for hf, (lo, hi) in enumerate(halves):
                dve.wait_ge(s_lnp, 4 * which + hf + 3)
                dve.tensor_scalar(lnr[:, lo:hi], ps[:, 4 + hf, 0:HALF], EPS, None, ALU.add).then_inc(s_ln, 1)
            dve.wait_ge(s_lng, 2 + which)
            dve.tensor_tensor(X, X, wide(lnr[:, NT:2 * NT]), ALU.mult).then_inc(s_ln, 1)
            dve.wait_ge(s_ln, base + 5)
            for c in range(KC):
                dve.tensor_scalar(X[:, c, :], X[:, c, :], g[:, c:c + 1], b[:, c:c + 1], ALU.mult, ALU.add).then_inc(s_ln, 1)
            dve.wait_ge(s_ln, base + 13)

        @block.sync
        def _(sp):
            sp.dma_start(sml[:, :], small).then_inc(s_small, 16)
            sp.dma_start(cst[:, :], const).then_inc(s_small, 16)
            sp.dma_start(gk2[:, :], wgk2).then_inc(s_small, 16)

            def load(q, slot):
                return sp.dma_start(W[:, slot * 4096:(slot + 1) * 4096].rearrange("p (u n) -> p u n", u=4),
                                    wq[4 * q:4 * q + 4].rearrange("u p n -> p u n"))

            for q in range(4):
                load(q, q).then_inc(s_w[q], 16)
            sp.dma_start(Xb[:, :], xT).then_inc(s_x, 16)
            with sp.Fori(1, 4) as i:
                for k in range(4):
                    gate(sp, "sp", s_wfree, i * 4 + (k - 3))
                    sp.dma_start(W[:, k * 4096:(k + 1) * 4096].rearrange("p (u n) -> p u n", u=4),
                                 wq[bass.ds(i * 16 + 4 * k, 4)].rearrange("u p n -> p u n")).then_inc(s_w[k], 16)

            def stream(a, b):
                for q in range(a, b):
                    sp.wait_ge(*used(q - 4))
                    load(q, q % 4).then_inc(s_w[q % 4], 16)

            def store_states(gi):
                g = GROUPS[gi]
                v = g["v"]
                with sp.Fori(0, 4) as h:
                    gate(sp, "sp", s_state, h * 4 + (16 * gi + 4))
                    at = (0, 1024, 1536)[gi]
                    sp.dma_start(st_prompt[:, bass.ds(h * v + at, v)], state[:, 2, 0:v]).then_inc(s_sout, 16)

            stream(16, 20)
            store_states(0)
            stream(20, 22)
            stream(22, 23)
            store_states(1)
            stream(23, 26)
            store_states(2)
            for b in range(2):
                sp.wait_ge(s_rec, 3)
                sp.dma_start(sin[:, b, :], st_in[b]).then_inc(s_si[b], 16)
            with sp.Fori(0, 3) as i:
                for b in range(2):
                    gate(sp, "sp", s_sn, i * 24 + (12 * b + 12))
                    sp.dma_start(st_out[bass.ds(i * 2 + b, 1)].rearrange("a p n -> (a p) n"), snew[:, b, :])\
                      .then_inc(s_so[b], 16)
                    sp.dma_start(sin[:, b, :], st_in[bass.ds(i * 2 + (b + 2), 1)].rearrange("a p n -> (a p) n"))\
                      .then_inc(s_si[b], 16)
            for b in range(2):
                sp.wait_ge(s_sn, 12 * (7 + b))
                sp.dma_start(st_out[6 + b], snew[:, b, :]).then_inc(s_so[b], 16)
            for b in range(2):
                sp.wait_ge(s_so[b], 64)
            sp.wait_ge(s_sn2, 6)
            sp.dma_start(Xb[:, :], xT).then_inc(s_x2, 16)
            stream(26, NQ)
            sp.wait_ge(s_p1, 64)
            sp.dma_start(rt, route).then_inc(s_route, 16)
            sp.wait_ge(*used(NQ - 1))
            sp.dma_start(W[:, 3 * 4096:4 * 4096], wexp[NE, :, 0:4096]).then_inc(s_shw, 16)
            sp.wait_ge(s_zero, 1)
            for rows in (h2rows, ffrows):
                sp.dma_start(rows[TRASH:ROWS, :], zrow).then_inc(s_hz, 16)
                sp.dma_start(rows[NT:TRASH, :], zrow[0:TRASH - NT, :]).then_inc(s_hz, 16)
            for t in range(TT):
                n = min(P, NT - t * P)
                sp.wait_ge(s_hc, 2 * t + 2)
                sp.dma_start(h2rows[t * P:t * P + n, :], hrow[0:n, t % 2, :]).then_inc(s_hd[t % 2], 16)
            rows_stored(sp)
            sp.dma_start(work[:, 3 * 2048:4 * 2048], wexp[NE, :, 4096:6144]).then_inc(s_shd, 16)
            for t in range(TT):
                n = min(P, NT - t * P)
                sp.wait_ge(t_yc, 2 * t + 2)
                sp.dma_start(ffrows[t * P:t * P + n, :], yb[0:n, t % 2, :]).then_inc(t_st[t % 2], 16)
            sp.wait_ge(s_row, 1)
            sp.dma_start(etab_d, ecol).then_inc(s_et, 16)
            sp.wait_ge(s_et, 16)
            sp.dma_start(erow, etab_d[0:MAXT + 4, :].rearrange("t a -> a t")).then_inc(s_et, 16)
            sp.wait_ge(s_T, 3)
            sp.wait_ge(t_y, 2 * TT)
            sp.wait_ge(s_abp, 40)
            nq = sp.value_load(qni[0:1, 0:1], min_val=1, max_val=MAXT // 4)

            def load_tile(t, slot, what, sems):
                lo, hi = (0, 4096) if what == "gu" else (4096, 6144)
                e = sp.value_load(eti[0:1, bass.ds(t, 1)], min_val=0, max_val=NE - 1)
                dst = W if what == "gu" else work
                w = hi - lo
                sp.dma_start(dst[:, slot * w:(slot + 1) * w],
                             wexp[bass.ds(e, 1), :, lo:hi].rearrange("a p n -> (a p) n")).then_inc(sems[slot], 16)

            load_tile(0, 0, "gu", s_gu)
            with sp.Fori(0, nq) as i:
                for k in range(4):
                    gate(sp, "sp", s_hh, i * 4 + (k + 2))
                    load_tile(i * 4 + (k + 1), (k + 1) % 4, "gu", s_gu)
                    gate(sp, "sp", s_y, i * 8 + (2 * k + 2))
                    load_tile(i * 4 + k, k, "dn", s_dn)
            gate(sp, "sp", s_add, nq * 64)
            for t in range(TT):
                n = min(P, NT - t * P)
                sp.dma_start(work[0:n, t * D:(t + 1) * D], ffrows[t * P:t * P + n, :]).then_inc(s_f1, 16)
            sp.wait_ge(s_ln, LN1 + 13)
            sp.dma_start(yT, Xb[:, :]).then_inc(s_f4, 16)
            sp.wait_ge(s_f4, 16)
            sp.wait_ge(s_sout, 192)

        @block.tensor
        def _(pe):
            pe.wait_ge(s_small, 48)
            pe.wait_ge(s_cs, 1)
            with pe.Fori(0, 3) as i:
                for k in range(4):
                    gate(pe, "pe", s_w[k], i * 16 + 16)
                    for u in range(4):
                        for c in range(KC):
                            mm = pe.matmul(ps[:, 0, bass.ds(i * (16 * NCOND) + (4 * k + u) * NCOND, NCOND)],
                                           ring[:, k, u, c, :], conds[:, c, :], start=(c == 0), stop=(c == KC - 1))
                    mm.then_inc(s_wfree, 1)
            pe.wait_ge(s_h, 9)

            def quad_ready(q):
                pe.wait_ge(s_w[q % 4], 16 * (q // 4 + 1))

            n = 0
            for gi, what, a, b in ITEMS:
                g = GROUPS[gi]
                if (what, a, b) == ("v", 0, 0):
                    if gi:
                        recurrence_pe(pe, gi - 1)
                    pe.wait_ge(s_mod, 1)
                bank = n % 2
                if n >= 2:
                    pe.wait_ge(s_zev, n - 1)
                if what == "v":
                    q = (Q_VA + a) if gi == 0 else Q_H[gi - 1][0]
                    rows = min(P, NT - b * P)
                    quad_ready(q)
                    for c in range(KC):
                        mm = pe.matmul(ps[0:rows, bank, :], H[:, c, b * P:b * P + rows], ring[:, q % 4, :, c, :],
                                       start=(c == 0), stop=(c == KC - 1))
                elif what == "gl":
                    w = S("wgk1").rearrange("p (c r) -> p c r", c=KC)
                    for c in range(KC):
                        mm = pe.matmul(ps[0:RANK, bank, 0:HALF], w[:, c, :], H[:, c, halves[b][0]:halves[b][1]],
                                       start=(c == 0), stop=(c == KC - 1))
                elif what == "g":
                    pe.wait_ge(s_zev, 12)
                    mm = pe.matmul(ps[:, bank, 0:HALF], gk2[:, a * P:(a + 1) * P], gkl[:, halves[b][0]:halves[b][1]],
                                   start=True, stop=True)
                else:
                    q = g["qs"] if what == "q" else g["fs"]
                    quad_ready(q)
                    for c in range(KC):
                        mm = pe.matmul(ps[:, bank, 0:HALF], ring[:, q % 4, a, c, :],
                                       H[:, c, halves[b][0]:halves[b][1]], start=(c == 0), stop=(c == KC - 1))
                mm.then_inc(s_z, 1)
                n += 1
            recurrence_pe(pe, 2)

            with pe.Fori(0, 4) as i:
                for b in range(2):
                    gate(pe, "pe", s_vm, i * 2 + (b + 1))
                    gate(pe, "pe", s_sn, i * 24 + 12 * b)
                    for j in range(4):
                        mm = pe.matmul(ps[:, j, :], ones[0:DEC, :], vm[0:DEC, b, j * 512:(j + 1) * 512],
                                       start=True, stop=True)
                    mm.then_inc(s_vb, 1)
                    gate(pe, "pe", s_sn, i * 24 + (12 * b + 12))
                    for j in range(16):
                        h = j // 2 if j < 8 else j - 4
                        mm = pe.matmul(ps[:, 4, bass.ds(i * 2 + (DEC * j + b), 1)], snew[:, b, j * P:(j + 1) * P],
                                       sq_[:, h, bass.ds(i * 2 + b, 1)], start=True, stop=True)
                    mm.then_inc(s_sop, 1)
            pe.wait_ge(s_sn2, 2)
            pe.matmul(ps[:, 5, 0:128], ones, oS2.rearrange("p j b -> p (j b)"), start=True, stop=True).then_inc(s_sop, 1)
            pe.wait_ge(s_sn2, 6)

            n = 0
            for q in range(Q_GA, Q_GB + 2):
                quad_ready(q)
                for u in range(4):
                    for lo, hi in halves:
                        if n >= 2:
                            pe.wait_ge(s_g2, n - 1)
                        for c in range(KC):
                            mm = pe.matmul(ps[:, n % 2, 0:HALF], ring[:, q % 4, u, c, :], H[:, c, lo:hi],
                                           start=(c == 0), stop=(c == KC - 1))
                        mm.then_inc(s_g1, 1)
                        n += 1
            pe.wait_ge(s_g3, 32)
            pe.wait_ge(s_g2, 32)
            n = 0
            for m in range(KC):
                q = Q_P + m
                quad_ready(q)
                for hf, (lo, hi) in enumerate(halves):
                    if n >= 2:
                        pe.wait_ge(s_p3a, 2 * (n - 1))
                    for u, rhs in enumerate((H, oa, H, ob)):
                        for c in range(KC):
                            mm = pe.matmul(ps[:, 4 * hf + u, 0:HALF], ring[:, q % 4, u, c, :], rhs[:, c, lo:hi],
                                           start=(c == 0), stop=(c == KC - 1))
                        mm.then_inc(s_p1, 1)
                    n += 1
            pe.wait_ge(s_p3, 16)
            n = 0
            for q in range(Q_O, NQ):
                quad_ready(q)
                for u in range(4):
                    for lo, hi in halves:
                        if n >= 2:
                            pe.wait_ge(s_o2, n - 1)
                        for c in range(KC):
                            mm = pe.matmul(ps[:, n % 2, 0:HALF], ring[:, q % 4, u, c, :], mg[:, c, lo:hi],
                                           start=(c == 0), stop=(c == KC - 1))
                        mm.then_inc(s_o1, 1)
                        n += 1
            pe.wait_ge(s_o2, 16)
            layer_norm_pe(pe, 0)
            pe.wait_ge(s_ln, LN1)

            pe.wait_ge(s_route, 16)
            wr = R("w").rearrange("p (c e) -> p c e", c=KC)
            for t in range(TT):
                rows = min(P, NT - t * P)
                for c in range(KC):
                    mm = pe.matmul(ps[0:rows, 0, t * NE:(t + 1) * NE], H[:, c, t * P:t * P + rows], wr[:, c, :],
                                   start=(c == 0), stop=(c == KC - 1))
            mm.then_inc(s_r1, 1)
            for t in range(TT):
                rows = min(P, NT - t * P)
                for hf in range(2):
                    n = 2 * t + hf
                    if n >= 2:
                        pe.wait_ge(s_hc, n - 1)
                    for c in range(4):
                        mm = pe.transpose(ps[0:rows, 1 + n % 2, c * P:(c + 1) * P],
                                          H[:, 4 * hf + c, t * P:t * P + rows], ident)
                    mm.then_inc(s_ht, 1)
            pe.wait_ge(s_shw, 16)
            pe.wait_ge(s_hc, 2 * TT)
            for t in range(TT):
                rows = min(P, NT - t * P)
                if t >= 1:
                    pe.wait_ge(t_sg, 2 * t)
                for c in range(KC):
                    mm = pe.matmul(ps[0:rows, 1, :], H[:, c, t * P:t * P + rows], GU[:, 3, c, :],
                                   start=(c == 0), stop=(c == KC - 1))
                mm.then_inc(t_hh, 1)
                pe.wait_ge(t_a, t + 1)
                if t >= 1:
                    pe.wait_ge(t_ac, t)
                for f in range(2):
                    mm = pe.transpose(ps[:, 2, f * P:f * P + rows], av[0:rows, t % 2, f * P:(f + 1) * P], ident[0:rows, 0:rows])
                mm.then_inc(t_at, 1)
                pe.wait_ge(t_ac, t + 1)
                pe.wait_ge(s_shd, 16)
                if t >= 1:
                    pe.wait_ge(t_yc, 2 * t)
                for hf in range(2):
                    for f in range(2):
                        mm = pe.matmul(ps[0:rows, 6 + hf, :], aT[:, t % 2, f, 0:rows], WD[:, 3, f, hf * 512:(hf + 1) * 512],
                                       start=(f == 0), stop=(f == 1))
                    mm.then_inc(t_y, 1)
            pe.wait_ge(s_msk, 1)
            for t in range(TT):
                rows = min(P, NT - t * P)
                pe.matmul(ps[:, 3, 0:NE], ones[0:rows, :], msk[0:rows, t, :], start=(t == 0), stop=(t == TT - 1))
            for t in range(TT):
                rows = min(P, NT - t * P)
                for t2 in range(t + 1):
                    k = P if t2 < t else rows
                    lhs = ones[0:k, 0:rows] if t2 < t else R("tri")[0:k, 0:rows]
                    mm = pe.matmul(ps[0:rows, 4, t * NE:(t + 1) * NE], lhs, msk[0:k, t2, :],
                                   start=(t2 == 0), stop=(t2 == t))
            mm.then_inc(s_rp, 1)
            n = 0
            for t in range(TT):
                rows = min(P, NT - t * P)
                for k in range(TOPK):
                    pe.wait_ge(s_ab, 4 * n + 4)
                    pe.matmul(ps[:, 5, 0:3 * MAXT], Aoh[0:rows, n % 2, :],
                              Boh[0:rows, n % 2, :, :].rearrange("p c t -> p (c t)"),
                              start=(n == 0), stop=(n == 39)).then_inc(s_abp, 1)
                    n += 1
            pe.wait_ge(s_T, 3)
            pe.wait_ge(t_yc, 2 * TT)
            pe.sem_inc(s_hh, 4)
            pe.sem_inc(s_y, 8)
            pe.sem_inc(s_xt, 4)
            nq = pe.value_load(qni[0:1, 0:1], min_val=1, max_val=MAXT // 4)

            def turn(t, k, gathered):
                gate(pe, "pe", s_ga[k % 2], gathered)
                gate(pe, "pe", s_xc, t * 2)
                for hf in range(2):
                    for c in range(4):
                        mm = pe.transpose(ps[:, 6 + hf, c * P:(c + 1) * P],
                                          xg[:, k % 2, (4 * hf + c) * P:(4 * hf + c + 1) * P], ident)
                    mm.then_inc(s_xt, 1)

            def gate_up(t, k, loaded):
                gate(pe, "pe", s_xc, t * 2 + 2)
                gate(pe, "pe", s_gu[k % 4], loaded)
                gate(pe, "pe", s_a, t + 1)
                for c in range(KC):
                    mm = pe.matmul(ps[:, k % 2, :], xe[:, k % 2, c, :], GU[:, k % 4, c, :],
                                   start=(c == 0), stop=(c == KC - 1))
                mm.then_inc(s_hh, 1)

            turn(0, 0, 16)
            gate_up(0, 0, 16)
            turn(1, 1, 16)
            with pe.Fori(0, nq) as i:
                for k in range(4):
                    t = i * 4 + k
                    gate(pe, "pe", s_a, i * 4 + (k + 3))
                    gate(pe, "pe", s_ac, t)
                    for f in range(2):
                        mm = pe.transpose(ps[:, 2, f * P:(f + 1) * P], av[:, k % 2, f * P:(f + 1) * P], ident)
                    mm.then_inc(s_at, 1)
                    gate_up(i * 4 + (k + 1), k + 1, i * 16 + (16 if k < 3 else 32))
                    gate(pe, "pe", s_ac, i * 4 + (k + 1))
                    gate(pe, "pe", s_dn[k], i * 16 + 16)
                    for hf in range(2):
                        gate(pe, "pe", s_yc, i * 8 + (2 * k + hf + 1))
                        for f in range(2):
                            mm = pe.matmul(ps[:, 4 + hf, :], aT[:, k % 2, f, :], WD[:, k, f, hf * 512:(hf + 1) * 512],
                                           start=(f == 0), stop=(f == 1))
                        mm.then_inc(s_y, 1)
                    turn(i * 4 + (k + 2), k, i * 32 + 16 * (k // 2 + 2))

            for t in range(TT):
                rows = min(P, NT - t * P)
                pe.wait_ge(s_f1, 16 * TT)
                for hf in range(2):
                    n = 2 * t + hf
                    if n >= 2:
                        pe.wait_ge(s_f3, n - 1)
                    for c in range(4):
                        mm = pe.transpose(ps[:, n % 2, c * P:c * P + rows],
                                          work[0:rows, t * D + (4 * hf + c) * P:t * D + (4 * hf + c + 1) * P],
                                          ident[0:rows, 0:rows])
                    mm.then_inc(s_f2, 1)
            pe.wait_ge(s_f3, 2 * TT)
            layer_norm_pe(pe, 1)

        @block.scalar
        def _(act):
            act.wait_ge(s_small, 48)
            act.activation(conds, conds, ACT.Silu).then_inc(s_cs, 1)
            act.wait_ge(s_lb, 3)
            act.activation(lbx, lbx, ACT.Exp).then_inc(s_lb, 1)
            n = 0
            for gi, what, a, b in ITEMS:
                g = GROUPS[gi]
                if (what, a, b) == ("v", 0, 0) and gi:
                    recurrence_act(act, gi - 1)
                bank = n % 2
                act.wait_ge(s_z, n + 1)
                lo, hi = halves[b] if what != "v" else (0, 0)
                if what == "v":
                    rows = min(P, NT - b * P)
                    if n == 0:
                        act.wait_ge(s_h, 9)
                    at = {0: a * 512, 1: 1024, 2: 1536}[gi]
                    dst = V[:, b, a * 512:(a + 1) * 512] if b < 4 else Vs[:, at:at + 512]
                    act.activation(dst, ps[0:rows, bank, :], ACT.Copy).then_inc(s_zev, 1)
                elif what == "gl":
                    act.activation(gkl[:, lo:hi], ps[0:RANK, bank, 0:HALF], ACT.Copy).then_inc(s_zev, 1)
                elif what == "g":
                    act.activation(g4[:, a, lo:hi], ps[:, bank, 0:HALF], ACT.Identity, bias=S("b_gk")[:, a:a + 1]).then_inc(s_zev, 1)
                elif what == "q":
                    if gi == 0:
                        act.activation(q4[:, a, lo:hi], ps[:, bank, 0:HALF], ACT.Copy, scale=P ** -0.5).then_inc(s_zev, 1)
                    else:
                        act.activation(q4[:, a, lo:hi], ps[:, bank, 0:HALF], ACT.Silu).then_inc(s_zev, 1)
                else:
                    if gi == 0:
                        act.activation(k4[:, a, lo:hi], ps[:, bank, 0:HALF], ACT.Copy).then_inc(s_zev, 1)
                    else:
                        act.activation(k4[:, a, lo:hi], ps[:, bank, 0:HALF], ACT.Sigmoid).then_inc(s_zev, 1)
                n += 1
                if what == "g" and (a, b) == (3, 1):
                    tmp_ = view(work, 10336, 4 * NT)
                    act.wait_ge(s_zev, n)
                    act.activation(tmp_, Gb, ACT.Abs).then_inc(s_gk, 1)
                    act.wait_ge(s_gk, 1)
                    act.activation(tmp_, tmp_, ACT.Exp, scale=-1.0).then_inc(s_gk, 1)
                    act.wait_ge(s_gk, 2)
                    act.activation(tmp_, tmp_, ACT.Ln, bias=1.0).then_inc(s_gk, 1)
                if gi and what == "k" and (a, b) == (3, 1):
                    act.wait_ge(s_kf, 4 * gi)
                    act.activation(Gb, Kb, ACT.Ln).then_inc(s_in, 1)
            recurrence_act(act, 2)

            with act.Fori(0, 4) as i:
                for b in range(2):
                    gate(act, "act", s_si[b], i * 16 + 16)
                    for h in range(12):
                        lo, hi = (h * GV, (h + 1) * GV) if h < GH else (1024 + (h - 4) * HV, 1024 + (h - 3) * HV)
                        act.activation(sin[:, b, lo:hi], sin[:, b, lo:hi], ACT.Copy,
                                       scale=sa_[:, h, bass.ds(i * 2 + b, 1)]).then_inc(s_sa, 1)

            n = 0
            for q in range(4):
                for u in range(4):
                    for lo, hi in halves:
                        act.wait_ge(s_g1, n + 1)
                        if n >= 4:
                            act.wait_ge(s_g3, n - 3)
                        act.activation(gtmp[:, n % 4, :], ps[:, n % 2, 0:HALF], ACT.Silu if q < 2 else ACT.Sigmoid)\
                           .then_inc(s_g2, 1)
                        n += 1
            act.wait_ge(s_g3, 32)
            n = 0
            for m in range(KC):
                for hf in range(2):
                    if n >= 2:
                        act.wait_ge(s_p3, n - 1)
                    for u in (0, 2):
                        act.wait_ge(s_p1, 4 * n + u + 1)
                        act.activation(gtmp[:, u // 2 + 2 * hf, :], ps[:, 4 * hf + u, 0:HALF], ACT.Sigmoid).then_inc(s_p2, 1)
                    n += 1
            layer_norm_act(act, 0)
            act.wait_ge(s_r1, 1)
            act.activation(OB[:, 0:4 * NE], ps[:, 0, 0:4 * NE], ACT.Sigmoid).then_inc(s_r2, 1)
            act.activation(scores[0:DEC, 4, :], ps[0:DEC, 0, 4 * NE:5 * NE], ACT.Sigmoid).then_inc(s_r2, 1)
            for t in range(TT):
                rows = min(P, NT - t * P)
                for hf in range(2):
                    n = 2 * t + hf
                    act.wait_ge(s_ht, n + 1)
                    if t >= 2:
                        act.wait_ge(s_hd[t % 2], 16 * (t // 2))
                    act.activation(hrow[0:rows, t % 2, hf * 512:(hf + 1) * 512], ps[0:rows, 1 + n % 2, :], ACT.Copy)\
                       .then_inc(s_hc, 1)
            for t in range(TT):
                rows = min(P, NT - t * P)
                act.wait_ge(t_hh, t + 1)
                if t >= 1:
                    act.wait_ge(t_a, t)
                act.activation(sg[0:rows, 0, :], ps[0:rows, 1, 0:FE], ACT.Silu).then_inc(t_sg, 1)
                act.activation(sg[0:rows, 1, :], ps[0:rows, 1, FE:2 * FE], ACT.Copy).then_inc(t_sg, 1)
                act.wait_ge(t_at, t + 1)
                act.activation(aT[:, t % 2, :, 0:rows], ps[:, 2, 0:2 * P].rearrange("p (f n) -> p f n", f=2)[:, :, 0:rows], ACT.Copy)\
                   .then_inc(t_ac, 1)
                if t >= 2:
                    act.wait_ge(t_st[t % 2], 16 * (t // 2))
                for hf in range(2):
                    act.wait_ge(t_y, 2 * t + hf + 1)
                    act.activation(yb[0:rows, t % 2, hf * 512:(hf + 1) * 512], ps[0:rows, 6 + hf, :], ACT.Copy)\
                       .then_inc(t_yc, 1)
            act.wait_ge(s_T, 3)
            nq = act.value_load(qni[0:1, 0:1], min_val=1, max_val=MAXT // 4)

            def take_x(t, k):
                gate(act, "act", s_hh, t + 3)
                for hf in range(2):
                    gate(act, "act", s_xt, t * 2 + (5 + hf))
                    act.activation(xe[:, k % 2, 4 * hf:4 * hf + 4, :].rearrange("p c n -> p (c n)"), ps[:, 6 + hf, :],
                                   ACT.Copy).then_inc(s_xc, 1)

            def silu(t, k):
                gate(act, "act", s_hh, t + 5)
                gate(act, "act", s_a, t + 1)
                act.activation(sg[:, k % 2, :], ps[:, k % 2, 0:FE], ACT.Silu).then_inc(s_sg, 1)

            take_x(0, 0)
            silu(0, 0)
            take_x(1, 1)
            with act.Fori(0, nq) as i:
                for k in range(4):
                    gate(act, "act", s_at, i * 4 + (k + 1))
                    gate(act, "act", s_y, i * 8 + (2 * k + 6))
                    act.activation(aT[:, k % 2, :, :].rearrange("p f n -> p (f n)"), ps[:, 2, 0:2 * P], ACT.Copy)\
                       .then_inc(s_ac, 1)
                    silu(i * 4 + (k + 1), k + 1)
                    take_x(i * 4 + (k + 2), k)
            layer_norm_act(act, 1)

        @block.gpsimd
        def _(pool):
            pool.wait_ge(s_small, 48)
            for gi in range(3):
                g = GROUPS[gi]
                v, base = g["v"], 16 * gi
                with pool.Fori(0, 4) as h:
                    def at(s, value):
                        gate(pool, "pool", s, value)

                    def mk(p):
                        at(s_E, h * 10 + (40 * gi + 5 * p + 5))
                        kk = k4[:, bass.ds(h, 1), p * 256:(p + 1) * 256].rearrange("p a t -> p (a t)")
                        for l in range(LEV):
                            s = CH >> (l + 1)
                            e = M[:, p, l, :].rearrange("p (n s) -> p n s", s=2 * s)[:, :, 0:s]
                            pool.tensor_tensor(e, e, kk.rearrange("p (n s) -> p n s", s=2 * s)[:, :, 0:s], ALU.mult)
                        pool.tensor_tensor(M[:, p, 7, :], M[:, p, 7, :], kk, ALU.mult).then_inc(s_Mk, 1)

                    def rs(cc):
                        at(s_ss, h * 4 + (base + cc + 1))
                        pool.tensor_scalar(ssum[:, cc % 2:cc % 2 + 1], ssum[:, cc % 2:cc % 2 + 1], 1.0 / v, EPS, ALU.mult, ALU.add).then_inc(s_rs, 1)
                        at(s_rs, h * 4 + (base + cc + 1))
                        pool.tensor_tensor(rstd[:, cc % 2:cc % 2 + 1], ssum[:, cc % 2:cc % 2 + 1], C("mhalf"), ALU.pow).then_inc(s_rstd, 1)

                    mk(0)
                    mk(1)
                    for cc in range(NCH):
                        rs(cc)
            pool.wait_ge(s_sn2, 4)
            pool.tensor_tensor(oms.rearrange("p j b -> p (j b)"), oms.rearrange("p j b -> p (j b)"),
                               C("mhalf").broadcast_to([P, 128]), ALU.pow).then_inc(s_lng, 1)
            layer_norm_pool(pool, 0)
            pool.memset(zrow, 0.0).then_inc(s_zero, 1)
            for t in range(TT):
                rows = min(P, NT - t * P)
                pool.wait_ge(t_sg, 2 * t + 2)
                if t >= 2:
                    pool.wait_ge(t_at, t - 1)
                pool.tensor_tensor(av[0:rows, t % 2, :], sg[0:rows, 0, :], sg[0:rows, 1, :], ALU.mult).then_inc(t_a, 1)
            pool.wait_ge(s_T, 3)
            pool.wait_ge(t_st[0], 48)
            pool.wait_ge(t_st[1], 32)
            rows_stored(pool)
            nq = pool.value_load(qni[0:1, 0:1], min_val=1, max_val=MAXT // 4)

            def gather(t, k, copied):
                gate(pool, "pool", s_xt, t * 2 + 2)
                pool.tensor_copy(idg[:, k:k + 1], idx_i[:, bass.ds(t, 1)]).then_inc(s_ic, 1)
                gate(pool, "pool", s_ic, copied)
                pool.indirect_dma_start(out=xg[:, k % 2, :], out_offset=None, in_=h2rows,
                                        in_offset=bass.IndirectOffsetOnAxis(ap=idg[:, k:k + 1], axis=0)).then_inc(s_ga[k % 2], 16)

            gather(0, 0, 1)
            gather(1, 1, 2)
            with pool.Fori(0, nq) as i:
                for k in range(4):
                    gather(i * 4 + (k + 2), (k + 2) % 4, i * 8 + (2 * k + 3))
                    gate(pool, "pool", s_add, i * 64 + 16 * k)
                    pool.tensor_copy(ida[:, k:k + 1], idx_i[:, bass.ds(i * 4 + k, 1)]).then_inc(s_ic, 1)
                    gate(pool, "pool", s_yc, i * 8 + (2 * k + 4))
                    gate(pool, "pool", s_ic, i * 8 + (2 * k + 4))
                    pool.indirect_dma_start(out=ffrows, out_offset=bass.IndirectOffsetOnAxis(ap=ida[:, k:k + 1], axis=0),
                                            in_=yb[:, k % 2, :], in_offset=None, compute_op=ALU.add).then_inc(s_add, 16)
            for p in range(2):
                gate(pool, "pool", s_ga[p], nq * 32 + 16)
            layer_norm_pool(pool, 1)

        @block.vector
        def _(dve):
            dve.wait_ge(s_small, 48)
            lb = S("lb").rearrange("p (r h) -> p r h", r=2)
            def lstep(ins, c=[0]):
                c[0] += 1
                ins.then_inc(s_lb, 1)
                dve.wait_ge(s_lb, c[0])
            lstep(dve.tensor_tensor(lbm, lb[:, 0, :], lb[:, 1, :], ALU.max))
            lstep(dve.tensor_tensor(lbx[:, 0, :], lb[:, 0, :], lbm, ALU.subtract))
            lstep(dve.tensor_tensor(lbx[:, 1, :], lb[:, 1, :], lbm, ALU.subtract))
            dve.wait_ge(s_wfree, 12)
            dve.tensor_tensor(md, ps[:, 0, 0:48 * NCOND].rearrange("p (e n) -> p e n", n=NCOND),
                              S("b_ada").rearrange("p (e a) -> p e a", a=1).broadcast_to([P, 48, NCOND]), ALU.add).then_inc(s_mod, 1)
            dve.wait_ge(s_mod, 1)
            for e in (SC1, SC2):
                dve.tensor_scalar(md[:, e:e + 8, :], md[:, e:e + 8, :], 1.0, None, ALU.add).then_inc(s_mod, 1)
            dve.wait_ge(s_mod, 3)
            dve.wait_ge(s_x, 16)
            for c in range(KC):
                dve.tensor_scalar(H[:, c, 0:SEQ], X[:, c, 0:SEQ], md[:, SC1 + c, 0:1], md[:, SH1 + c, 0:1],
                                  ALU.mult, ALU.add).then_inc(s_h, 1)
            dve.tensor_tensor(H[:, :, SEQ:NT], X[:, :, SEQ:NT], md[:, SC1:SC1 + 8, 1:NCOND], ALU.mult).then_inc(s_mod, 1)
            dve.wait_ge(s_mod, 4)
            dve.tensor_tensor(H[:, :, SEQ:NT], H[:, :, SEQ:NT], md[:, SH1:SH1 + 8, 1:NCOND], ALU.add).then_inc(s_h, 1)

            for gi in range(3):
                g = GROUPS[gi]
                v, base = g["v"], 16 * gi
                if gi == 0:
                    dve.wait_ge(s_gk, 3)
                    dve.tensor_scalar(Gb, Gb, 0.0, None, ALU.min).then_inc(s_in, 1)
                    dve.wait_ge(s_in, 1)
                    dve.tensor_tensor(Gb, Gb, view(work, 10336, 4 * NT), ALU.subtract).then_inc(s_in, 1)
                    dve.wait_ge(s_in, 2)
                    dve.tensor_scalar(Gb, Gb, 1.0 / 16.0, None, ALU.mult).then_inc(s_in, 1)
                    dve.wait_ge(s_in, 3)
                    dve.wait_ge(s_lb, 4)
                    dve.tensor_tensor(lbm, lbx[:, 0, :], lbx[:, 1, :], ALU.add).then_inc(s_lb, 1)
                    dve.wait_ge(s_lb, 5)
                    dve.reciprocal(lbm, lbm).then_inc(s_lb, 1)
                    dve.wait_ge(s_lb, 6)
                    dve.tensor_tensor(lbt, lbx[:, 0, :], lbm, ALU.mult).then_inc(s_lb, 1)
                    dve.wait_ge(s_lb, 7)
                    dve.tensor_scalar(omlb, lbt, -1.0, 1.0, ALU.mult, ALU.add).then_inc(s_lb, 1)
                    dve.wait_ge(s_lb, 8)
                else:
                    zend = sum(1 for it in ITEMS if it[0] <= gi)
                    dve.wait_ge(s_zev, zend)
                    for h in range(4):
                        hd = 4 * (gi - 1) + h
                        dve.tensor_scalar(k4[:, h, :], k4[:, h, :], omlb[:, hd:hd + 1], lbt[:, hd:hd + 1],
                                          ALU.mult, ALU.add).then_inc(s_kf, 1)
                    dve.tensor_scalar(Qb, Qb, P ** -0.5, None, ALU.mult).then_inc(s_fk, 1)
                    dve.wait_ge(s_kf, 4 * gi)
                    dve.wait_ge(s_in, 3 + gi)
                    dve.tensor_scalar(Kb, Kb, -1.0, 1.0, ALU.mult, ALU.add).then_inc(s_fk, 1)
                for h in range(4):
                    dve.tensor_tensor_scan(g4[:, h, :], C("reset"), g4[:, h, :], 0.0, ALU.mult, ALU.add).then_inc(s_cum, 1)
                dve.wait_ge(s_cum, 4 * gi + 4)
                if gi:
                    dve.wait_ge(s_fk, 2 * gi)
                else:
                    dve.wait_ge(s_zev, sum(1 for it in ITEMS if it[0] == 0))
                dve.tensor_copy(sq_[:, 4 * gi:4 * gi + 4, :], q4[:, :, SEQ:NT]).then_inc(s_smp, 1)
                dve.tensor_copy(sk_[:, 4 * gi:4 * gi + 4, :], k4[:, :, SEQ:NT]).then_inc(s_smp, 1)

                with dve.Fori(0, 4) as h:
                    def at(s, value):
                        gate(dve, "dve", s, value)

                    def diffs(p):
                        at(s_o, h * 4 + base)
                        b = g4[:, bass.ds(h, 1), p * 256:(p + 1) * 256].rearrange("p a t -> p (a t)")
                        for l in range(LEV + 1):
                            s = CH >> (l + 1)
                            w = 2 * s if l < LEV else CH
                            r = s - 1 if l < LEV else CH - 1
                            bb = b.rearrange("p (n s) -> p n s", s=w)
                            ins = dve.tensor_tensor(M[:, p, l, :].rearrange("p (n s) -> p n s", s=w), bb,
                                                    bb[:, :, r:r + 1].broadcast_to([P, 256 // w, w]), ALU.subtract)
                        ins.then_inc(s_D, 1)

                    def mq(p):
                        at(s_E, h * 10 + (40 * gi + 5 * p + 5))
                        qq = q4[:, bass.ds(h, 1), p * 256:(p + 1) * 256].rearrange("p a t -> p (a t)")
                        for l in range(LEV):
                            s = CH >> (l + 1)
                            e = M[:, p, l, :].rearrange("p (n s) -> p n s", s=2 * s)[:, :, s:2 * s]
                            dve.tensor_tensor(e, e, qq.rearrange("p (n s) -> p n s", s=2 * s)[:, :, s:2 * s], ALU.mult)
                        dve.tensor_tensor(M[:, p, 8, :], M[:, p, 8, :], qq, ALU.mult).then_inc(s_Mq, 1)

                    def mask(cc):
                        at(s_sc, h * 4 + (base + cc + 1))
                        at(s_st, h * 4 + (base + cc))
                        dve.tensor_tensor(Pm, ps[:, 0:2, :].rearrange("p b t -> p (b t)"), C("masks"), ALU.mult).then_inc(s_pm, 1)
                        at(s_pm, h * 4 + (base + cc + 1))
                        at(s_o, h * 4 + (base + max(cc - 1, 0)))
                        dve.tensor_reduce(ST[:, cc % 2, :], Pm.rearrange("p (l t) -> p t l", l=8), AX, ALU.add).then_inc(s_st, 1)

                    def new_state(cc):
                        at(s_u, h * 4 + (base + cc + 1))
                        dst = state[:, (cc + 1) % 2 if cc < 3 else 2, 0:v]
                        if cc == 3:
                            at(s_sout, h * 16 + 64 * gi)
                        if cc:
                            at(s_o, h * 4 + (base + cc - 1))
                            at(s_state, h * 4 + (base + cc))
                            dve.scalar_tensor_tensor(out=dst, in0=state[:, cc % 2, 0:v], scalar=elast[:, cc // 2, cc % 2:cc % 2 + 1],
                                                     in1=ps[:, 3, 0:v], op0=ALU.mult, op1=ALU.add).then_inc(s_state, 1)
                        else:
                            dve.tensor_copy(dst, ps[:, 3, 0:v]).then_inc(s_state, 1)

                    def take_o(cc):
                        at(s_ot, h * 4 + (base + cc + 1))
                        nj = v // P
                        dst = g["out"][:, bass.ds(h * nj + g["first"], nj), cc * CH:(cc + 1) * CH]
                        dve.tensor_copy(dst, ps[:, 6, 0:v].rearrange("p (j t) -> p j t", t=CH)).then_inc(s_oc, 1)

                    diffs(0)
                    diffs(1)
                    mq(0)
                    mq(1)
                    mask(0)
                    for cc in range(NCH):
                        new_state(cc)
                        if cc + 1 < NCH:
                            mask(cc + 1)
                        take_o(cc)
                dve.wait_ge(s_oc, base + 16)
                dve.sem_inc(s_rec, 1)

            dve.wait_ge(s_smp, 9)
            dve.wait_ge(s_zev, len(ITEMS))
            with dve.Fori(0, 4) as i:
                def row(b):
                    gate(dve, "dve", s_vb, i * 2)
                    dve.tensor_scalar(vm[0:DEC, b, :], Vs, ident[0:DEC, bass.ds(i * 2 + b, 1)], None, ALU.mult).then_inc(s_vm, 1)
                row(0)
                row(1)
                for b in range(2):
                    gate(dve, "dve", s_vb, i * 2 + (b + 1))
                    gate(dve, "dve", s_so[b], i * 16)
                    gate(dve, "dve", s_sop, i * 2)
                    for h in range(12):
                        lo, hi = (h * GV, (h + 1) * GV) if h < GH else (1024 + (h - 4) * HV, 1024 + (h - 3) * HV)
                        gate(dve, "dve", s_sa, i * 24 + (12 * b + h + 1))
                        dve.scalar_tensor_tensor(out=snew[:, b, lo:hi], in0=ps[:, lo // 512, lo % 512:lo % 512 + hi - lo],
                                                 scalar=sk_[:, h, bass.ds(i * 2 + b, 1)], in1=sin[:, b, lo:hi],
                                                 op0=ALU.mult, op1=ALU.add).then_inc(s_sn, 1)
            dve.wait_ge(s_sop, 8)
            dve.tensor_copy(oS.rearrange("p j b -> p (j b)"), ps[:, 4, 0:128]).then_inc(s_sn2, 1)
            dve.wait_ge(s_sn2, 1)
            dve.tensor_tensor(oS2, oS, oS, ALU.mult).then_inc(s_sn2, 1)
            dve.wait_ge(s_sop, 9)
            sums = ps[:, 5, 0:128].rearrange("p (j b) -> p j b", b=DEC)
            dve.tensor_copy(oms, sums).then_inc(s_sn2, 1)
            dve.wait_ge(s_sn2, 3)
            pair = oms[:, 0:8, :].rearrange("p (h k) b -> p h k b", k=2)
            both = oS2[:, 0:8, :].rearrange("p (h k) b -> p h k b", k=2)
            for k in range(2):
                ins = dve.tensor_tensor(both[:, :, k, :], pair[:, :, 0, :], pair[:, :, 1, :], ALU.add)
            ins.then_inc(s_mod, 1)
            dve.wait_ge(s_mod, 5)
            dve.tensor_scalar(oms[:, 0:8, :], oS2[:, 0:8, :], 1.0 / GV, EPS, ALU.mult, ALU.add).then_inc(s_mod, 1)
            dve.tensor_scalar(oms[:, 8:16, :], oms[:, 8:16, :], 1.0 / HV, EPS, ALU.mult, ALU.add).then_inc(s_sn2, 1)
            dve.wait_ge(s_mod, 6)
            dve.wait_ge(s_lng, 1)
            dve.tensor_tensor(oa[:, :, SEQ:NT], oS[:, 0:8, :], oms[:, 0:8, :], ALU.mult).then_inc(s_sn2, 1)
            dve.tensor_tensor(ob[:, :, SEQ:NT], oS[:, 8:16, :], oms[:, 8:16, :], ALU.mult).then_inc(s_sn2, 1)
            dve.wait_ge(s_sn2, 6)

            n = 0
            for q in range(4):
                for u in range(4):
                    m = 4 * (q % 2) + u
                    o = oa if q < 2 else ob
                    w = S("gla_w")[:, m % 2:m % 2 + 1] if q < 2 else S("hgrn_w")
                    for lo, hi in halves:
                        dve.wait_ge(s_g2, n + 1)
                        dve.scalar_tensor_tensor(out=o[:, m, lo:hi], in0=gtmp[:, n % 4, :], scalar=w, in1=o[:, m, lo:hi],
                                                 op0=ALU.mult, op1=ALU.mult).then_inc(s_g3, 1)
                        n += 1
            n = 0
            for m in range(KC):
                for hf, (lo, hi) in enumerate(halves):
                    dve.wait_ge(s_p2, 2 * n + 2)
                    dve.wait_ge(s_p1, 4 * n + 4)
                    for u in range(2):
                        dve.tensor_tensor(gtmp[:, u + 2 * hf, :], gtmp[:, u + 2 * hf, :], ps[:, 4 * hf + 2 * u + 1, 0:HALF],
                                          ALU.mult).then_inc(s_p3a, 1)
                    dve.wait_ge(s_p3a, 2 * n + 2)
                    dve.tensor_tensor(mg[:, m, lo:hi], gtmp[:, 2 * hf, :], gtmp[:, 1 + 2 * hf, :], ALU.add).then_inc(s_p3, 1)
                    n += 1
            dve.wait_ge(s_x2, 16)
            dve.tensor_scalar(Xb[:, :], Xb[:, :], ALPHA, None, ALU.mult).then_inc(s_fx, 1)
            dve.wait_ge(s_fx, 1)
            for m in range(KC):
                for hf, (lo, hi) in enumerate(halves):
                    n = 2 * m + hf
                    dve.wait_ge(s_o1, n + 1)
                    w = min(hi, SEQ) - lo
                    ins = dve.scalar_tensor_tensor(out=X[:, m, lo:lo + w], in0=ps[:, n % 2, 0:w], scalar=md[:, G1 + m, 0:1],
                                                   in1=X[:, m, lo:lo + w], op0=ALU.mult, op1=ALU.add)
                    if hi > SEQ:
                        dec = view(tiny, 200, DEC)
                        dve.tensor_tensor(dec, ps[:, n % 2, w:w + DEC], md[:, G1 + m, 1:NCOND], ALU.mult).then_inc(s_fx, 1)
                        dve.wait_ge(s_fx, m + 2)
                        ins = dve.tensor_tensor(X[:, m, SEQ:NT], X[:, m, SEQ:NT], dec, ALU.add)
                    ins.then_inc(s_o2, 1)
            dve.wait_ge(s_o2, 16)
            layer_norm_dve(dve, 0)
            for c in range(KC):
                dve.tensor_scalar(H[:, c, 0:SEQ], X[:, c, 0:SEQ], md[:, SC2 + c, 0:1], md[:, SH2 + c, 0:1],
                                  ALU.mult, ALU.add).then_inc(s_ln, 1)
            dve.tensor_tensor(H[:, :, SEQ:NT], X[:, :, SEQ:NT], md[:, SC2:SC2 + 8, 1:NCOND], ALU.mult).then_inc(s_ln, 1)
            dve.wait_ge(s_ln, LN1 - 1)
            dve.tensor_tensor(H[:, :, SEQ:NT], H[:, :, SEQ:NT], md[:, SH2:SH2 + 8, 1:NCOND], ALU.add).then_inc(s_ln, 1)

            dve.wait_ge(s_ln, LN1)
            dve.tensor_scalar(Xb[:, :], Xb[:, :], ALPHA, None, ALU.mult).then_inc(s_fx, 1)

            count = [0]

            def step(ins):
                ins.then_inc(s_rv, 1)
                count[0] += 1
                return ins

            def settled():
                dve.wait_ge(s_rv, count[0])

            dve.wait_ge(s_route, 16)
            dve.wait_ge(s_r2, 2)
            grouped = "p t (g k) -> p (t g) k"
            step(dve.tensor_tensor(biased, scores, R("bias").rearrange("p (a e) -> p a e", a=1).broadcast_to([P, TT, NE]), ALU.add))
            settled()
            for t in range(TT):
                for g in range(NG):
                    step(dve.max(g8[:, t, g, :], biased[:, t, g * 8:(g + 1) * 8]))
            settled()
            step(dve.tensor_tensor(grp, g8[:, :, :, 0], g8[:, :, :, 1], ALU.add))
            settled()
            for t in range(TT):
                step(dve.max(top[:, t, :], grp[:, t, :]))
            settled()
            for t in range(TT):
                step(dve.max_index(ui[:, t, :], top[:, t, :], grp[:, t, :]))
            settled()
            step(dve.tensor_copy(idxf, ui))
            settled()
            g4h = view(work, 0, TT * TOPG * NG, "p (t k g) -> p t k g", t=TT, k=TOPG)
            step(dve.tensor_tensor(g4h, R("group").rearrange("p (a b g) -> p a b g", a=1, b=1).broadcast_to([P, TT, TOPG, NG]),
                                   idxf[:, :, 0:TOPG].rearrange("p t (k a) -> p t k a", a=1).broadcast_to([P, TT, TOPG, NG]),
                                   ALU.is_equal))
            settled()
            step(dve.tensor_reduce(gm, g4h.rearrange("p t k g -> p t g k"), AX, ALU.add))
            settled()
            gmf = gm.rearrange("p t g -> p (t g)")
            gmx = gm.rearrange("p t (g a) -> p (t g) a", a=1)
            step(dve.tensor_tensor(tmp.rearrange(grouped, k=8), biased.rearrange(grouped, k=8),
                                   gmx.broadcast_to([P, TT * NG, 8]), ALU.mult))
            settled()
            step(dve.tensor_scalar(gmf, gmf, -1.0, BIG, ALU.add, ALU.mult))
            settled()
            step(dve.tensor_tensor(tmp.rearrange(grouped, k=8), tmp.rearrange(grouped, k=8),
                                   gmx.broadcast_to([P, TT * NG, 8]), ALU.add))
            settled()
            for t in range(TT):
                step(dve.max(top[:, t, :], tmp[:, t, :]))
            settled()
            for t in range(TT):
                step(dve.max_index(ui[:, t, :], top[:, t, :], tmp[:, t, :]))
            settled()
            step(dve.tensor_copy(idxf, ui))
            settled()
            step(dve.tensor_tensor(oh, R("iota")[:, 0:NE].rearrange("p (a b e) -> p a b e", a=1, b=1).broadcast_to([P, TT, TOPK, NE]),
                                   idxf.rearrange("p t (k a) -> p t k a", a=1).broadcast_to([P, TT, TOPK, NE]), ALU.is_equal))
            settled()
            dve.tensor_reduce(msk, oh.rearrange("p t k e -> p t e k"), AX, ALU.add).then_inc(s_msk, 1)
            dve.wait_ge(s_msk, 1)
            step(dve.tensor_tensor(tmp, scores, msk, ALU.mult))
            settled()
            step(dve.tensor_reduce(gsum, tmp, AX, ALU.add))
            settled()
            step(dve.reciprocal(gsum, gsum))
            settled()
            step(dve.tensor_scalar(gsum, gsum, RSCALE, None, ALU.mult))
            settled()
            step(dve.tensor_tensor(gates, scores, gsum.rearrange("p (t a) -> p t a", a=1).broadcast_to([P, TT, NE]), ALU.mult))
            dve.wait_ge(s_rp, 1)
            step(dve.tensor_copy(cnt, ps[:, 3, 0:NE]))
            settled()
            step(dve.tensor_scalar(nti, cnt, 0.0, None, ALU.is_gt))
            settled()
            for k in range(1, TT):
                step(dve.scalar_tensor_tensor(out=nti, in0=cnt, scalar=float(P * k), in1=nti, op0=ALU.is_gt, op1=ALU.add))
                settled()
            step(dve.tensor_tensor_scan(incl, ones[:, 0:NE], nti, 0.0, ALU.mult, ALU.add))
            settled()
            step(dve.tensor_scalar(cmp_, incl, R("part"), None, ALU.is_le))
            step(dve.tensor_tensor(excl, incl, nti, ALU.subtract))
            settled()
            step(dve.tensor_reduce(ecol, cmp_, AX, ALU.add))
            settled()
            dve.tensor_scalar(ecol, ecol, float(NE - 1), None, ALU.min).then_inc(s_row, 1)
            step(dve.tensor_scalar(cmp_[:, 0:MAXT // 4], R("quads"), incl[:, NE - 1:NE], None, ALU.is_lt))
            settled()
            step(dve.tensor_reduce(quadn, cmp_[:, 0:MAXT // 4], AX, ALU.add))
            settled()
            dve.tensor_copy(qni[0:1, 0:1], quadn[0:1, :]).then_inc(s_T, 1)
            for t, r in ((slice(0, 4), P), (slice(4, 5), DEC)):
                n = t.stop - t.start
                step(dve.scalar_tensor_tensor(out=pos[0:r, t, :], in0=excl[0:r, :].rearrange("p (a e) -> p a e", a=1).broadcast_to([r, n, NE]),
                                              scalar=float(P), op0=ALU.mult, op1=ALU.add,
                                              in1=ps[0:r, 4, t.start * NE:t.stop * NE].rearrange("p (t e) -> p t e", t=n)))
            settled()
            for dst, src in ((posk, pos), (gk, gates)):
                step(dve.tensor_tensor(prod, oh, src.rearrange("p t (a e) -> p t a e", a=1).broadcast_to([P, TT, TOPK, NE]), ALU.mult))
                settled()
                step(dve.tensor_reduce(dst, prod, AX, ALU.add))
                settled()
            step(dve.tensor_copy(posi, posk.rearrange("p t k -> p (t k)")))
            settled()
            step(dve.tensor_scalar(hi_i, posi, 7, None, ALU.arith_shift_right))
            step(dve.tensor_scalar(lo_i, posi, P - 1, None, ALU.bitwise_and))
            settled()
            step(dve.tensor_copy(tilek.rearrange("p t k -> p (t k)"), hi_i))
            step(dve.tensor_copy(slotk.rearrange("p t k -> p (t k)"), lo_i))
            settled()
            n = 0
            for t in range(TT):
                for k in range(TOPK):
                    if n >= 2:
                        dve.wait_ge(s_abp, n - 1)
                    slot, tile = slotk[:, t, k:k + 1], tilek[:, t, k:k + 1]
                    i96 = R("iota")[:, 0:MAXT]
                    dve.tensor_scalar(Aoh[:, n % 2, :], R("iota"), slot, None, ALU.is_equal).then_inc(s_ab, 1)
                    dve.tensor_scalar(Boh[:, n % 2, 0, :], i96, tile, R("token")[:, t:t + 1], ALU.is_equal, ALU.mult).then_inc(s_ab, 1)
                    dve.tensor_scalar(Boh[:, n % 2, 1, :], i96, tile, gk[:, t, k:k + 1], ALU.is_equal, ALU.mult).then_inc(s_ab, 1)
                    dve.tensor_scalar(Boh[:, n % 2, 2, :], i96, tile, None, ALU.is_equal).then_inc(s_ab, 1)
                    n += 1
            dve.wait_ge(s_et, 32)
            dve.tensor_copy(eti[0:1, 0:MAXT + 4], erow).then_inc(s_T, 1)
            dve.wait_ge(s_abp, 40)
            tok, gat, use = (ps[:, 5, c * MAXT:(c + 1) * MAXT] for c in range(3))
            step(dve.tensor_copy(gtabs[:, 0:MAXT], gat))
            step(dve.memset(gtabs[:, MAXT:MAXT + 4], 0.0))
            step(dve.memset(idxt[:, MAXT:MAXT + 4], 1.0))
            step(dve.tensor_scalar(idxt[:, 0:MAXT], use, -1.0, 1.0, ALU.mult, ALU.add))
            settled()
            step(dve.tensor_scalar(idxt, idxt, R("trash"), None, ALU.mult))
            settled()
            step(dve.tensor_tensor(idxt[:, 0:MAXT], idxt[:, 0:MAXT], tok, ALU.add))
            settled()
            dve.tensor_copy(idx_i[:, :], idxt).then_inc(s_T, 1)

            dve.sem_inc(s_a, 2)
            dve.sem_inc(s_yc, 2)
            dve.wait_ge(s_T, 3)
            nq = dve.value_load(qni[0:1, 0:1], min_val=1, max_val=MAXT // 4)

            def gated(t, k, copied):
                dve.tensor_copy(gcol[:, k % 4:k % 4 + 1], gtabs[:, bass.ds(t, 1)]).then_inc(s_gc, 1)
                gate(dve, "dve", s_gc, copied)
                gate(dve, "dve", s_sg, t + 1)
                dve.scalar_tensor_tensor(out=av[:, k % 2, :], in0=ps[:, k % 2, FE:2 * FE], scalar=gcol[:, k % 4:k % 4 + 1],
                                         in1=sg[:, k % 2, :], op0=ALU.mult, op1=ALU.mult).then_inc(s_a, 1)

            gated(0, 0, 1)
            with dve.Fori(0, nq) as i:
                for k in range(4):
                    gated(i * 4 + (k + 1), k + 1, i * 4 + (k + 2))
                    gate(dve, "dve", s_add, i * 64 + 16 * max(k - 1, 0))
                    for hf in range(2):
                        gate(dve, "dve", s_y, i * 8 + (2 * k + hf + 9))
                        dve.tensor_copy(yb[:, k % 2, hf * 512:(hf + 1) * 512], ps[:, 4 + hf, :]).then_inc(s_yc, 1)

            for t in range(TT):
                rows = min(P, NT - t * P)
                for hf in range(2):
                    n = 2 * t + hf
                    dve.wait_ge(s_f2, n + 1)
                    if t < 4:
                        for c in range(4):
                            m = 4 * hf + c
                            ins = dve.scalar_tensor_tensor(out=X[:, m, t * P:(t + 1) * P], in0=ps[:, n % 2, c * P:(c + 1) * P],
                                                           scalar=md[:, G2 + m, 0:1], in1=X[:, m, t * P:(t + 1) * P],
                                                           op0=ALU.mult, op1=ALU.add)
                    else:
                        four = slice(4 * hf, 4 * hf + 4)
                        dec = view(tiny, 184 + 32 * hf, 4 * DEC, "p (c b) -> p c b", c=4)
                        dve.tensor_tensor(dec, ps[:, n % 2, :].rearrange("p (c t) -> p c t", c=4)[:, :, 0:DEC],
                                          md[:, G2 + 4 * hf:G2 + 4 * hf + 4, 1:NCOND], ALU.mult).then_inc(s_fy, 1)
                        dve.wait_ge(s_fy, hf + 1)
                        ins = dve.tensor_tensor(X[:, four, SEQ:NT], X[:, four, SEQ:NT], dec, ALU.add)
                    ins.then_inc(s_f3, 1)
            dve.wait_ge(s_f3, 2 * TT)
            layer_norm_dve(dve, 1)


def kernel(**inputs):
    import concourse.bacc as bacc
    from concourse.bass_utils import run_bass_kernel_spmd as run

    a = {k: np.asarray(v) for k, v in inputs.items()}

    def rows(x):
        return x.reshape(-1, KC, P).transpose(2, 1, 0)

    def blocks(w):
        return w.reshape(KC, P, -1, P).transpose(2, 1, 0, 3).reshape(-1, P, KC * P)

    xT = rows(np.concatenate([a["x_prompt"][0], a["x_sample"][:, 0]])).reshape(P, KC * NT)
    w_in = a["w_in"][0]
    cuts = np.cumsum([0, 512, 512, 1024, 1024, 16, 1024, 1024, 1024, 1024, 1024, 1024])
    qa, ka, va, ga, gk, qb, fb, ib, gb, ua, ub = (w_in[:, cuts[i]:cuts[i + 1]] for i in range(11))
    B = blocks
    merge = np.stack([B(ua), B(a["w_proj_a"][0]), B(ub), B(a["w_proj_b"][0])], 1).reshape(4 * KC, P, KC * P)
    wq = np.concatenate([B(a["w_ada"][0]), B(va), B(qa), B(ka),
                         B(ib[:, :512]), B(qb[:, :512]), B(fb[:, :512]),
                         B(ib[:, 512:]), B(qb[:, 512:]), B(fb[:, 512:]),
                         B(ga), B(gb), merge, B(a["w_out"][0])])
    col = lambda x: x.reshape(-1, P).T
    small = np.concatenate([
        rows(np.concatenate([a["c_prompt"], a["c_sample"]])).reshape(P, -1), col(a["b_ada"][0]), col(a["b_gk"][0]),
        col(a["hgrn_lb"]), col(a["gla_norm_w"][0]), col(a["hgrn_norm_w"][0]), col(a["ln1_g"][0]), col(a["ln1_b"][0]),
        col(a["ln2_g"][0]), col(a["ln2_b"][0]), gk.reshape(KC, P, RANK).transpose(1, 0, 2).reshape(P, -1)], 1)
    const, route = constants()
    at, n = ROUTE["bias"]
    route[:, at:at + n] = np.broadcast_to(a["router_bias"][0], (P, NE))
    at, n = ROUTE["w"]
    route[:, at:at + n] = a["w_router"][0].reshape(KC, P, NE).transpose(1, 0, 2).reshape(P, -1)

    def expert(g, u, d):
        gu = np.concatenate([g.reshape(-1, KC, P, FE), u.reshape(-1, KC, P, FE)], 3)
        return np.concatenate([gu.transpose(0, 2, 1, 3).reshape(-1, P, 4096),
                               d.reshape(-1, 2, P, D).transpose(0, 2, 1, 3).reshape(-1, P, 2048)], 2)

    wexp = np.concatenate([expert(a["w_exp_gate"][0], a["w_exp_up"][0], a["w_exp_down"][0]),
                           expert(a["w_sh_gate"], a["w_sh_up"], a["w_sh_down"])])
    st_in = np.concatenate([a["state_gla"][0].transpose(0, 2, 1, 3).reshape(DEC, P, GH * GV),
                            a["state_hgrn"][0].transpose(0, 2, 1, 3).reshape(DEC, P, HH * HV)], 2)
    ins = dict(xT=xT, small=small, wgk2=a["w_gk2"][0], const=const, route=route, wq=wq, wexp=wexp, st_in=st_in)
    ins = {k: np.ascontiguousarray(v) for k, v in ins.items()}

    nc = bacc.Bacc("TRN2", target_bir_lowering=False, num_devices=1)
    aps = {k: nc.dram_tensor(k, v.shape, F32, kind="ExternalInput").ap() for k, v in ins.items()}
    outs = dict(yT=(P, KC * NT), st_prompt=(P, 2048), st_out=(DEC, P, 2048))
    aps.update({k: nc.dram_tensor(k, s, F32, kind="ExternalOutput").ap() for k, s in outs.items()})
    decoder_step(nc, **aps)
    r = run(nc, [ins], core_ids=[0]).results[0]
    y = r["yT"].reshape(P, KC, NT).transpose(2, 1, 0).reshape(NT, D)
    sp, so = r["st_prompt"], r["st_out"]
    gla = lambda s: s[..., :1024].reshape(-1, P, GH, GV).transpose(0, 2, 1, 3)[None]
    hgrn = lambda s: s[..., 1024:].reshape(-1, P, HH, HV).transpose(0, 2, 1, 3)[None]
    c = np.ascontiguousarray
    return (c(y[None, :SEQ]), c(y[SEQ:, None]), c(gla(sp[None])), c(hgrn(sp[None])), c(gla(so)), c(hgrn(so)))
```

```python
from contextlib import ExitStack

import numpy as np
import concourse.bass as bass
from concourse import mybir

P = 128
D = 1024
KC = D // P
SEQ = 512
DEC = 8
NT = SEQ + DEC
HALF = NT // 2
CH = 128
NCH = SEQ // CH
LEV = 7
GH, GV = 4, 256
HH, HV = 8, 128
RANK = 16
NE, NG, TOPG, TOPK = 64, 8, 4, 8
FE = 256
TT = 5
TS = 128
MAXT = 96
TRASH = TT * P
ROWS = TRASH + P
ALPHA = 2.0 ** 0.25
EPS = 1e-5
RSCALE = 2.5
NCOND = 1 + DEC
BIG = 1e30
assert MAXT % 4 == 0 and MAXT >= NT * TOPK // TS + NE - 1 and TS == 1 << 7


F32 = mybir.dt.float32
I32 = mybir.dt.int32
U32 = mybir.dt.uint32
ALU = mybir.AluOpType
ACT = mybir.ActivationFunctionType
AX = mybir.AxisListType.X

Q_ADA = [0, 1, 2, 3, 8, 9, 10, 11, 12, 13, 14, 15]
Q_QA, Q_KA, Q_VA = 4, 5, 6
Q_H = [(18, 17, 16), (23, 22, 21)]
Q_G = [19, 20, 24, 25]
Q_P, Q_O = 26, 34
NQ = 36

def columns(widths):
    at, out = 0, {}
    for name, w in widths:
        out[name] = (at, w)
        at += w
    return out, at

SMALL, NSMALL = columns([("cond", KC * NCOND), ("b_ada", 48), ("b_gk", GH), ("lb", 2 * HH), ("gla_w", 2),
                         ("hgrn_w", 1), ("ln1_g", KC), ("ln1_b", KC), ("ln2_g", KC), ("ln2_b", KC),
                         ("wgk1", KC * RANK)])
CONST, NCONST = columns([("ident", P), ("ones", P), ("mean", P), ("masks", 8 * P), ("reset", NT), ("mhalf", 1), ("eps", 1)])
ROUTE, NROUTE = columns([("tri", P), ("iota", P), ("group", NG), ("quads", MAXT // 4), ("part", 1),
                         ("trash", 1), ("token", TT), ("bias", NE), ("w", KC * NE)])


def constants():
    c = np.zeros((P, NCONST), np.float32)
    def put(table, arr, name, v):
        a, w = table[name]
        arr[:, a:a + w] = v
    j, i = np.arange(P)[:, None], np.arange(P)[None, :]
    put(CONST, c, "ident", np.eye(P))
    put(CONST, c, "ones", 1.0)
    put(CONST, c, "mean", 1.0 / D)
    masks = []
    for l in range(LEV):
        s = CH >> (l + 1)
        masks.append((j // (2 * s) == i // (2 * s)) & (j % (2 * s) < s) & (i % (2 * s) >= s))
    masks.append(j == i)
    put(CONST, c, "masks", np.stack(masks, 1).reshape(P, 8 * P))
    t = np.arange(NT)
    put(CONST, c, "reset", ((t % CH != 0) & (t < SEQ))[None, :])
    put(CONST, c, "mhalf", -0.5)
    put(CONST, c, "eps", EPS)
    r = np.zeros((P, NROUTE), np.float32)
    put(ROUTE, r, "tri", j < i)
    put(ROUTE, r, "iota", i)
    put(ROUTE, r, "group", np.arange(NG)[None, :])
    put(ROUTE, r, "quads", 4 * np.arange(MAXT // 4)[None, :])
    put(ROUTE, r, "part", j)
    put(ROUTE, r, "trash", TRASH + j)
    put(ROUTE, r, "token", j + P * np.arange(TT)[None, :])
    return c, r


def decoder_step(nc, xT, small, wgk2, const, route, wq, wexp, st_in, yT, st_prompt, st_out):
    with ExitStack() as ctx:
        def sb(name, n, dt=F32, p=P):
            return ctx.enter_context(nc.sbuf_tensor(name, [p, n], dt))

        def sem(name):
            return ctx.enter_context(nc.semaphore(name))

        h2rows = nc.dram_tensor("h2rows", [ROWS, D], F32, kind="Internal").ap()
        ffrows = nc.dram_tensor("ffrows", [ROWS, D], F32, kind="Internal").ap()
        etab_d = nc.dram_tensor("etab", [P, 1], F32, kind="Internal").ap()

        W = sb("W", 4 * 4096)
        Xb = sb("Xb", KC * NT)
        Hb = sb("Hb", KC * NT)
        OA = sb("OA", KC * NT)
        OB = sb("OB", KC * NT)
        work = sb("work", 16480)
        cst = sb("cst", NCONST)
        sml = sb("sml", NSMALL)
        gk2 = sb("gk2", GH * P, p=RANK)
        mod = sb("mod", 48 * NCOND)
        tiny = sb("tiny", 256)
        ints = sb("ints", 256, I32)
        ps = ctx.enter_context(nc.psum_tensor("ps", [P, 8, 512], F32))

        def view(buf, first, n, pattern=None, **kw):
            v = buf[:, first:first + n]
            return v.rearrange(pattern, **kw) if pattern else v

        def C(name):
            a, w = CONST[name]
            return cst[:, a:a + w]

        def S(name):
            a, w = SMALL[name]
            return sml[:, a:a + w]

        ident, ones = C("ident"), C("ones")
        ring = W[:, :].rearrange("p (s u c m) -> p s u c m", s=4, u=4, c=KC)
        X = Xb[:, :].rearrange("p (c t) -> p c t", c=KC)
        H = Hb[:, :].rearrange("p (c t) -> p c t", c=KC)
        oa = OA[:, :].rearrange("p (c t) -> p c t", c=KC)
        ob = OB[:, :].rearrange("p (c t) -> p c t", c=KC)
        md = mod[:, :].rearrange("p (e n) -> p e n", n=NCOND)
        SH1, SC1, G1, SH2, SC2, G2 = range(0, 48, 8)
        conds = S("cond").rearrange("p (c n) -> p c n", c=KC)
        V = view(work, 0, 4096, "p (t n) -> p t n", t=NCH)
        Qb, Kb, Gb = (view(work, 4096 + k * 4 * NT, 4 * NT) for k in range(3))
        q4, k4, g4 = (v.rearrange("p (h t) -> p h t", h=4) for v in (Qb, Kb, Gb))
        M = view(work, 10336, 5120, "p (b l t) -> p b l t", b=2, l=10)
        state = view(work, 15456, 768, "p (b v) -> p b v", b=3)
        Vs = Xb[0:DEC, 0:2048]
        sq_, sk_, sa_ = (view(Xb, 2048 + 96 * k, 96, "p (h b) -> p h b", b=DEC) for k in range(3))
        Pm = view(Xb, 2336, 1024)
        ST = view(Xb, 3360, 256, "p (b t) -> p b t", b=2)
        kdT = view(Xb, 3616, 256, "p (b t) -> p b t", b=2)
        gkl = Xb[0:RANK, 3640:3640 + NT]
        on = (view(work, 16224, 256), view(Xb, 3872, 256))
        gdec = view(tiny, 64, 16 * DEC, "p (j b) -> p j b", b=DEC)
        elast = view(tiny, 0, 4, "p (b c) -> p b c", b=2)
        ssum = view(tiny, 4, 2)
        rstd = view(tiny, 6, 2)
        lbt = view(tiny, 16, 8)
        omlb = view(tiny, 24, 8)
        lbx = view(tiny, 40, 16, "p (r h) -> p r h", r=2)
        lbm = view(tiny, 56, 8)

        s_small, s_x, s_x2, s_route = sem("small_loaded"), sem("x_loaded"), sem("x_again"), sem("route_loaded")
        s_w = [sem(f"quad_loaded_{k}") for k in range(4)]
        s_wfree = sem("quad_used")
        s_cs = sem("cond_silu")
        s_md, s_mod, s_h = sem("modulation"), sem("sample_sums"), sem("h_ready")
        s_z, s_zev = sem("proj_done"), sem("proj_taken")
        s_lb = sem("lb_steps")
        s_gk = sem("gk_steps")
        s_kf, s_fk = sem("forget_ready"), sem("hgrn_k_ready")
        s_in, s_cum = sem("gates_in"), sem("cumsum_done")
        s_D, s_E, s_Mq, s_Mk = sem("diff_done"), sem("exp_done"), sem("mq_done"), sem("mk_done")
        s_kdt, s_kdc = sem("kd_transposed"), sem("kd_copied")
        s_sc, s_pm, s_st = sem("scores_done"), sem("scores_masked"), sem("scores_summed")
        s_o, s_ss, s_rs, s_rstd = sem("o_done"), sem("o_squares"), sem("o_ms"), sem("o_rstd")
        s_on, s_ot, s_oc = sem("o_scaled"), sem("o_transposed"), sem("o_copied")
        s_u, s_state, s_sout = sem("update_done"), sem("state_done"), sem("state_stored")
        s_rec = sem("group_done")
        s_smp = sem("sample_saved")
        paced = {e: sem(f"paced_{e}") for e in ("sp", "pe", "act", "dve", "pool")}

        def gate(eng, name, s, value):
            eng.wait_ge(s, value)
            eng.sem_inc(paced[name], 1)

        s_si, s_so = [sem("sin0"), sem("sin1")], [sem("sout0"), sem("sout1")]
        s_vm, s_vb, s_sa, s_sn, s_sop = sem("v_row"), sem("v_bcast"), sem("s_scaled"), sem("s_new"), sem("s_o")
        s_sn2 = sem("sample_norm")
        s_g1, s_g2, s_g3 = sem("gate_proj"), sem("gate_act"), sem("gate_mul")
        s_p1, s_p2, s_p3, s_p3a = sem("merge_proj"), sem("merge_act"), sem("merged"), sem("merge_parts")
        s_o1, s_o2 = sem("out_proj"), sem("resid")
        s_ln = sem("ln_steps")
        s_lnp = sem("ln_sums")
        s_lna = sem("ln_squares")
        s_lng, s_laf = sem("deviation"), sem("ln_affine")
        s_r1, s_r2, s_rv = sem("router_proj"), sem("router_sigmoid"), sem("route_steps")
        s_rp = sem("route_counts")
        s_tab = sem("table_sums")
        s_ab, s_abq, s_abp = sem("tile_onehots"), sem("slot_onehots"), sem("onehots_used")
        s_slots, s_eti = sem("slots_ready"), sem("tile_experts")
        s_row, s_et, s_T = sem("etab_stored"), sem("etab_back"), sem("etab_ready")
        s_ht, s_hc, s_hd = sem("h2_transposed"), sem("h2_copied"), [sem("h2_stored_0"), sem("h2_stored_1")]
        s_zero, s_hz = sem("zeroed"), sem("zeros_stored")
        s_shw, s_shd = sem("shared_gu"), sem("shared_down")
        s_gu = [sem(f"gu_loaded_{k}") for k in range(4)]
        s_dn = [sem(f"dn_loaded_{k}") for k in range(4)]
        s_guf, s_dnf = sem("gu_used"), sem("dn_used")
        s_ic, s_gc, s_xt, s_xc = sem("idx_col"), sem("gate_col"), sem("x_transposed"), sem("x_copied")
        s_hh, s_sg, s_a, s_at, s_ac = sem("hidden"), sem("hidden_silu"), sem("act_ready"), sem("act_transposed"), sem("act_copied")
        s_y, s_yc, s_add = sem("y_done"), sem("y_copied"), sem("y_added")
        s_ga = [sem("gathered_0"), sem("gathered_1")]
        t_hh, t_sg, t_a = sem("sh_hidden"), sem("sh_factors"), sem("sh_act")
        t_y, t_yc, t_st = sem("sh_y"), sem("sh_y_copied"), [sem("sh_stored_0"), sem("sh_stored_1")]
        s_f1, s_f2, s_f3, s_f4 = sem("ff_loaded"), sem("ff_transposed"), sem("ff_resid"), sem("y_stored")
        s_fx, s_fy, s_msk = sem("x_scaled"), sem("decode_resid"), sem("mask_ready")

        block = ctx.enter_context(nc.Block())

        R0 = KC * NT - NROUTE - 8
        assert R0 > 2900
        rt = view(OB, R0, NROUTE)

        def R(name):
            a, w = ROUTE[name]
            return rt[:, a:a + w]

        scores = view(OB, 0, TT * NE, "p (t e) -> p t e", t=TT)
        biased = view(OB, 320, TT * NE, "p (t e) -> p t e", t=TT)
        msk = view(OB, 640, TT * NE, "p (t e) -> p t e", t=TT)
        pos = view(OB, 960, TT * NE, "p (t e) -> p t e", t=TT)
        gates = view(OB, 1280, TT * NE, "p (t e) -> p t e", t=TT)
        tmp = view(OB, 1600, TT * NE, "p (t e) -> p t e", t=TT)
        g8 = view(OB, 1920, TT * NG * 8, "p (t g k) -> p t g k", t=TT, g=NG)
        grp = view(OB, 2240, TT * NG, "p (t g) -> p t g", t=TT)
        gm = view(OB, 2280, TT * NG, "p (t g) -> p t g", t=TT)
        top = view(OB, 2320, TT * 8, "p (t k) -> p t k", t=TT)
        idxf = view(OB, 2360, TT * 8, "p (t k) -> p t k", t=TT)
        posk = view(OB, 2400, TT * 8, "p (t k) -> p t k", t=TT)
        gk = view(OB, 2440, TT * 8, "p (t k) -> p t k", t=TT)
        tilek = view(OB, 2480, TT * 8, "p (t k) -> p t k", t=TT)
        slotk = view(OB, 2520, TT * 8, "p (t k) -> p t k", t=TT)
        cnt = view(OB, 2560, NE)
        nti = view(OB, 2624, NE)
        incl = view(OB, 2688, NE)
        excl = view(OB, 2752, NE)
        cmp_ = view(OB, 2816, NE)
        gsum = view(tiny, 32, TT)
        ecol = view(tiny, 37, 1)
        erow = tiny[0:1, 64:64 + MAXT + 4]
        ui = ints[:, 0:TT * 8].bitcast(U32).rearrange("p (t k) -> p t k", t=TT)
        posi = ints[:, 40:80]
        hi_i = ints[:, 80:120]
        idxt = view(OB, 2880, MAXT + 4)
        assert 2880 + MAXT + 4 <= R0
        quadn = tiny[:, 180:181]
        oh = view(work, 0, TT * 8 * NE, "p (t k e) -> p t k e", t=TT, k=8)
        prod = view(work, 2560, TT * 8 * NE, "p (t k e) -> p t k e", t=TT, k=8)
        Aoh = view(work, 5120, 2 * TS, "p (b s) -> p b s", b=2)
        Boh = view(work, 5376, 2 * 3 * MAXT, "p (b c t) -> p b c t", b=2, c=3)
        hrow = view(work, 6400, 2 * D, "p (b d) -> p b d", b=2)
        zrow = view(work, 8448, D)
        assert 8448 + D <= 10240
        WD = view(work, 0, 8192, "p (s f d) -> p s f d", s=4, f=2)
        GU = W[:, :].rearrange("p (s c f) -> p s c f", s=4, c=KC)
        xg = view(work, 8192, 2048, "p (b d) -> p b d", b=2)
        xe = view(work, 10240, 2 * KC * TS, "p (b c n) -> p b c n", b=2, c=KC)
        yb = view(work, 12288, 2048, "p (b d) -> p b d", b=2)
        av = view(work, 14336, 512, "p (b f) -> p b f", b=2)
        aT = view(work, 14848, 512, "p (b f n) -> p b f n", b=2, f=2)
        sg = view(work, 15360, 512, "p (b f) -> p b f", b=2)
        shT = view(work, 10240, 2 * NT, "p (f t) -> p f t", f=2)
        shg = view(work, 11280, 2 * HALF, "p (k t) -> p k t", k=2)
        idx_i = view(work, 15872, MAXT + 4).bitcast(I32)
        gtabs = view(work, 15984, MAXT + 4)
        eti = work[0:1, 16096:16096 + MAXT + 4].bitcast(I32)
        qni = view(work, 16208, 1).bitcast(I32)
        idg = view(work, 16212, 4).bitcast(I32)
        ida = view(work, 16216, 4).bitcast(I32)
        gcol = view(work, 16220, 4)

        LSQ = view(work, 0, KC * NT, "p (c t) -> p c t", c=KC)
        lnr = view(work, 4160, 2 * NT)
        mg = view(work, 6000, KC * NT, "p (c t) -> p c t", c=KC)
        gtmp = view(work, 10200, 4 * HALF, "p (b t) -> p b t", b=4)
        sin = view(work, 0, 4096, "p (b n) -> p b n", b=2)
        snew = view(work, 4096, 4096, "p (b n) -> p b n", b=2)
        vm = view(work, 8192, 4096, "p (b n) -> p b n", b=2)
        oS = view(work, 12288, 128, "p (j b) -> p j b", b=DEC)
        oS2 = view(work, 12416, 128, "p (j b) -> p j b", b=DEC)
        oms = view(work, 12544, 128, "p (j b) -> p j b", b=DEC)

        GROUPS = [dict(heads=GH, v=GV, out=oa, first=0, kind="gla", qs=Q_QA, fs=Q_KA),
                  dict(heads=4, v=HV, out=ob, first=0, kind="hgrn", qs=Q_H[0][1], fs=Q_H[0][2]),
                  dict(heads=4, v=HV, out=ob, first=4, kind="hgrn", qs=Q_H[1][1], fs=Q_H[1][2])]
        halves = [(0, HALF), (HALF, NT)]

        def z_items():
            out = []
            for gi in range(3):
                def heads(what):
                    return [(gi, what, h, hf) for h in range(4) for hf in range(2)]

                if gi == 0:
                    out += [(gi, "gl", 0, hf) for hf in range(2)] + heads("g") + heads("q") + heads("k")
                else:
                    out += heads("k") + heads("q")
                for b in range(2 if gi == 0 else 1):
                    out += [(gi, "v", b, t) for t in range(TT)]
            return out

        ITEMS = z_items()


        def rows_stored(eng):
            eng.wait_ge(s_hd[0], 48)
            eng.wait_ge(s_hd[1], 32)
            eng.wait_ge(s_hz, 32)

        def used(q):
            if q in Q_ADA:
                return s_wfree, Q_ADA.index(q) + 1
            if q in Q_G:
                return s_g1, 8 * Q_G.index(q) + 8
            if q < Q_P:
                n, last = 0, 0
                for gi, what, a, b in ITEMS:
                    n += 1
                    own = {"v": (Q_VA + a) if gi == 0 else Q_H[gi - 1][0], "q": GROUPS[gi]["qs"],
                           "k": GROUPS[gi]["fs"]}.get(what)
                    if own == q:
                        last = n
                return s_z, last
            if q < Q_O:
                return s_p1, 8 * (q - Q_P + 1)
            return s_o1, 8 * (q - Q_O + 1)

        def taken(gi, what):
            return 1 + max(n for n, it in enumerate(ITEMS) if it[:2] == (gi, what))

        def since(eng, s, value):
            if value > 0:
                eng.wait_ge(s, value)

        def gate_unit(n):
            lo, hi = halves[n % 2]
            return 4 * (n // 8 % 2) + n // 2 % 4, lo, min(hi, SEQ), (7 if n < 24 else 6 + n % 2)

        FILL = [{c: ("mod", 3 + c) for c in range(1, 9)}, {c: ("gate", c) for c in range(16)},
                {2 * c: ("gate", 16 + c) for c in range(8)}]

        LN0, LN1 = 0, 24

        def mean_pe(pe, c, hf):
            lo, hi = halves[hf]
            mm = pe.matmul(ps[:, 2 + hf, 0:HALF], C("mean"), X[:, c, lo:hi], start=(c == 0), stop=(c == KC - 1))
            if c == KC - 1:
                mm.then_inc(s_lnp, 1)

        def variance_pe(pe, which):
            for hf, (lo, hi) in enumerate(halves):
                pe.wait_ge(s_lna, 2 * which + hf + 1)
                for c in range(KC):
                    mm = pe.matmul(ps[:, 4 + hf, 0:HALF], C("mean"), LSQ[:, c, lo:hi], start=(c == 0), stop=(c == KC - 1))
                mm.then_inc(s_lnp, 1)

        def recurrence_pe(pe, gi, fill):
            v, base = GROUPS[gi]["v"], 16 * gi

            def scores_of(n):
                pair, p, c, h, cc = n // 2, n // 2 % 2, n % 2, n // 4 % 4, n % 4
                col_ = slice(c * CH, (c + 1) * CH)
                pe.wait_ge(s_Mk, pair + 1)
                pe.wait_ge(s_Mq, pair + 1)
                since(pe, s_kdc, n)
                pe.transpose(ps[:, 2, 0:CH], M[:, p, 7, col_], ident).then_inc(s_kdt, 1)
                since(pe, s_pm, n)
                for l in range(LEV):
                    pe.matmul(ps[:, l // 4, (l % 4) * CH:(l % 4 + 1) * CH], M[:, p, l, col_], M[:, p, l, col_],
                              start=True, stop=True)
                pe.matmul(ps[:, 1, 3 * CH:4 * CH], M[:, p, 9, col_], q4[:, h, cc * CH:(cc + 1) * CH],
                          start=True, stop=True).then_inc(s_sc, 1)

            def values(n):
                return V[:, n % 4, n // 4 % 4 * v:(n // 4 % 4 + 1) * v]

            def update(n):
                pe.wait_ge(s_kdc, n + 1)
                since(pe, s_state, n)
                pe.matmul(ps[:, 3, 0:v], kdT[:, n % 2, :], values(n), start=True, stop=True).then_inc(s_u, 1)

            def output(n):
                o = ps[:, 4 + n % 2, 0:v]
                pe.wait_ge(s_st, n + 1)
                since(pe, s_on, n - 1)
                mm = pe.matmul(o, ST[:, n % 2, :], values(n), start=True, stop=(n % 4 == 0))
                if n % 4:
                    pe.wait_ge(s_state, n)
                    mm = pe.matmul(o, M[:, n // 2 % 2, 8, n % 2 * CH:(n % 2 + 1) * CH], state[:, n % 4 % 2, 0:v],
                                   start=False, stop=True)
                mm.then_inc(s_o, 1)

            def turn(n):
                pe.wait_ge(s_on, n + 1)
                since(pe, s_oc, n)
                for j in range(v // P):
                    mm = pe.transpose(ps[:, 6, j * P:(j + 1) * P], on[n % 2][:, j * P:(j + 1) * P], ident)
                mm.then_inc(s_ot, 1)

            scores_of(base)
            for c in range(17):
                if c < 16:
                    update(base + c)
                    if c in FILL[gi]:
                        fill(*FILL[gi][c])
                if c + 1 < 16:
                    scores_of(base + c + 1)
                if c < 16:
                    output(base + c)
                if c:
                    turn(base + c - 1)

        def layer_norm_act(act, which):
            base = (LN0, LN1)[which]
            g, b = S(f"ln{which + 1}_g"), S(f"ln{which + 1}_b")
            for hf, (lo, hi) in enumerate(halves):
                act.wait_ge(s_ln, base + 1 + hf)
                act.activation(LSQ[:, :, lo:hi], X[:, :, lo:hi], ACT.Square).then_inc(s_lna, 1)
            for hf, (lo, hi) in enumerate(halves):
                act.wait_ge(s_lnp, 4 * which + hf + 3)
                act.activation(lnr[:, lo:hi], ps[:, 4 + hf, 0:HALF], ACT.Sqrt, bias=C("eps")).then_inc(s_lng, 1)
            act.wait_ge(s_ln, base + 5)
            for c in range(KC):
                act.activation(X[:, c, 0:HALF], X[:, c, 0:HALF], ACT.Identity, scale=g[:, c:c + 1],
                               bias=b[:, c:c + 1]).then_inc(s_laf, 1)

        def gate_act(act, n):
            m, lo, hi, bank = gate_unit(n)
            fn = ACT.Silu if n < 16 else ACT.Sigmoid
            act.wait_ge(s_g1, n + 1)
            if n % 2:
                act.activation(gdec[:, 8 * (n // 16) + m, :], ps[:, bank, hi - lo:HALF], fn)
            act.activation(ps[:, bank, 0:hi - lo], ps[:, bank, 0:hi - lo], fn).then_inc(s_g2, 1)

        def gate_mul(dve, n):
            m, lo, hi, bank = gate_unit(n)
            o, w = (oa, S("gla_w")[:, m % 2:m % 2 + 1]) if n < 16 else (ob, S("hgrn_w"))
            dve.wait_ge(s_g2, n + 1)
            dve.scalar_tensor_tensor(out=o[:, m, lo:hi], in0=ps[:, bank, 0:hi - lo], scalar=w, in1=o[:, m, lo:hi],
                                     op0=ALU.mult, op1=ALU.mult).then_inc(s_g3, 1)

        def filled(gi, c):
            what, n = FILL[gi].get(c, (None, 0))
            return n if what == "gate" else None

        def recurrence_act(act, gi):
            v, base = GROUPS[gi]["v"], 16 * gi
            act.wait_ge(s_cum, 4 * gi + 4)
            act.activation(sa_[:, 4 * gi:4 * gi + 4, :], g4[:, :, SEQ:NT], ACT.Exp).then_inc(s_smp, 1)
            if gi:
                act.wait_ge(s_fk, 2 * gi)

            def src(buf, pair):
                return buf[:, pair // 2 % 4, pair % 2 * 256:(pair % 2 + 1) * 256]

            def decays(pair):
                p = pair % 2
                act.wait_ge(s_D, pair + 1)
                act.activation(M[:, p, 0:8, :], M[:, p, 0:8, :], ACT.Abs).then_inc(s_E, 1)
                act.wait_ge(s_E, 5 * pair + 1)
                act.activation(M[:, p, 0:8, :], M[:, p, 0:8, :], ACT.Exp, scale=-1.0).then_inc(s_E, 1)

            def factors(pair):
                p = pair % 2
                since(act, s_o, 2 * pair - 2)
                act.activation(M[:, p, 8, :], src(g4, pair), ACT.Exp).then_inc(s_E, 1)
                act.activation(M[:, p, 9, :], src(k4, pair), ACT.Copy).then_inc(s_E, 1)
                since(act, s_state, 2 * pair - 2)
                act.activation(elast[:, p, :], g4[:, pair // 2 % 4, pair % 2 * 256 + 127:(pair % 2 + 1) * 256:128], ACT.Exp).then_inc(s_E, 1)

            def copy_kd(n):
                act.wait_ge(s_kdt, n + 1)
                since(act, s_u, n - 1)
                act.activation(kdT[:, n % 2, :], ps[:, 2, 0:CH], ACT.Copy).then_inc(s_kdc, 1)

            def square(n):
                act.wait_ge(s_o, n + 1)
                since(act, s_ot, n - 1)
                act.activation(on[n % 2][:, 0:v], ps[:, 4 + n % 2, 0:v], ACT.Square,
                               accum_out=ssum[:, n % 2:n % 2 + 1]).then_inc(s_ss, 1)

            def scale(n):
                act.wait_ge(s_rstd, n + 1)
                act.activation(on[n % 2][:, 0:v], ps[:, 4 + n % 2, 0:v], ACT.Copy,
                               scale=rstd[:, n % 2:n % 2 + 1]).then_inc(s_on, 1)

            def store_state(head):
                act.wait_ge(s_state, 4 * head + 4)
                at = (0, 1024, 1536)[gi] + head % 4 * v
                act.dma_start(st_prompt[:, at:at + v], state[:, 2, 0:v]).then_inc(s_sout, 16)

            for pair in (8 * gi, 8 * gi + 1):
                decays(pair)
                factors(pair)
                if pair == 8 * gi:
                    copy_kd(base)
            for c in range(17):
                even = c % 2 == 0 and 2 <= c <= 12
                if c and filled(gi, c - 1) is not None:
                    gate_act(act, filled(gi, c - 1))
                if c:
                    square(base + c - 1)
                if c + 1 < 16:
                    copy_kd(base + c + 1)
                if even:
                    decays(8 * gi + c // 2 + 1)
                if c:
                    scale(base + c - 1)
                if even:
                    factors(8 * gi + c // 2 + 1)
                if c in (5, 9, 13):
                    store_state(4 * gi + (c - 5) // 4)
            store_state(4 * gi + 3)

        def layer_norm_dve(dve, which):
            base = (LN0, LN1)[which]
            g, b = S(f"ln{which + 1}_g"), S(f"ln{which + 1}_b")

            def wide(v):
                return v.rearrange("p (a t) -> p a t", a=1).broadcast_to([P, KC, v.shape[1]])

            for hf, (lo, hi) in enumerate(halves):
                dve.wait_ge(s_lnp, 4 * which + hf + 1)
                dve.tensor_tensor(X[:, :, lo:hi], X[:, :, lo:hi], wide(ps[:, 2 + hf, 0:HALF]), ALU.subtract).then_inc(s_ln, 1)
            for hf, (lo, hi) in enumerate(halves):
                dve.wait_ge(s_lng, 2 + 2 * which + hf)
                dve.reciprocal(lnr[:, NT + lo:NT + hi], lnr[:, lo:hi]).then_inc(s_ln, 1)
            dve.wait_ge(s_ln, base + 4)
            for hf, (lo, hi) in enumerate(halves):
                dve.tensor_tensor(X[:, :, lo:hi], X[:, :, lo:hi], wide(lnr[:, NT + lo:NT + hi]), ALU.mult).then_inc(s_ln, 1)
            dve.wait_ge(s_ln, base + 6)
            for c in range(KC):
                dve.tensor_scalar(X[:, c, HALF:NT], X[:, c, HALF:NT], g[:, c:c + 1], b[:, c:c + 1], ALU.mult, ALU.add).then_inc(s_ln, 1)
            dve.wait_ge(s_ln, base + 14)
            dve.wait_ge(s_laf, 8 * which + 8)

        @block.sync
        def _(sp):
            sp.dma_start(sml[:, :], small).then_inc(s_small, 16)
            sp.dma_start(cst[:, :], const).then_inc(s_small, 16)
            sp.dma_start(gk2[:, :], wgk2).then_inc(s_small, 16)

            def load(q, slot):
                return sp.dma_start(W[:, slot * 4096:(slot + 1) * 4096], wq[q])

            for q in range(4):
                load(q, q).then_inc(s_w[q], 16)
            sp.dma_start(Xb[:, :], xT).then_inc(s_x, 16)

            def stream(a, b):
                for q in range(a, b):
                    sp.wait_ge(*used(q - 4))
                    load(q, q % 4).then_inc(s_w[q % 4], 16)

            stream(4, 29)
            for b in range(2):
                sp.wait_ge(s_rec, 3)
                sp.dma_start(sin[:, b, :], st_in[b]).then_inc(s_si[b], 16)
            for b in range(DEC):
                sp.wait_ge(s_sn, 12 * (b + 1))
                sp.dma_start(st_out[b], snew[:, b % 2, :]).then_inc(s_so[b % 2], 16)
                if b + 2 < DEC:
                    sp.dma_start(sin[:, b % 2, :], st_in[b + 2]).then_inc(s_si[b % 2], 16)
            for b in range(2):
                sp.wait_ge(s_so[b], 64)
            sp.wait_ge(s_sn2, 6)
            sp.dma_start(Xb[:, :], xT).then_inc(s_x2, 16)
            stream(29, NQ)
            sp.wait_ge(s_p1, 64)
            sp.dma_start(rt, route).then_inc(s_route, 16)
            sp.wait_ge(*used(NQ - 1))
            sp.dma_start(W[:, 3 * 4096:4 * 4096], wexp[NE, :, 0:4096]).then_inc(s_shw, 16)
            sp.wait_ge(s_zero, 1)
            sp.dma_start(h2rows[TRASH:ROWS, :], zrow).then_inc(s_hz, 16)
            sp.dma_start(h2rows[NT:TRASH, :], zrow[0:TRASH - NT, :]).then_inc(s_hz, 16)
            for t in range(TT):
                n = min(P, NT - t * P)
                sp.wait_ge(s_hc, 2 * t + 2)
                sp.dma_start(h2rows[t * P:t * P + n, :], hrow[0:n, t % 2, :]).then_inc(s_hd[t % 2], 16)
            rows_stored(sp)
            sp.dma_start(work[:, 3 * 2048:4 * 2048], wexp[NE, :, 4096:6144]).then_inc(s_shd, 16)
            sp.wait_ge(s_row, 1)
            sp.dma_start(etab_d, ecol).then_inc(s_et, 16)
            sp.wait_ge(s_et, 16)
            sp.dma_start(erow, etab_d[0:MAXT + 4, :].rearrange("t a -> a t")).then_inc(s_et, 16)
            for t in range(TT):
                n = min(P, NT - t * P)
                sp.wait_ge(t_yc, 2 * t + 2)
                sp.dma_start(ffrows[t * P:t * P + n, :], yb[0:n, t % 2, :]).then_inc(t_st[t % 2], 16)
            sp.wait_ge(s_T, 1)
            nq = sp.value_load(qni[0:1, 0:1], min_val=1, max_val=MAXT // 4)

            def load_tile(t, slot, what, sems):
                lo, hi = (0, 4096) if what == "gu" else (4096, 6144)
                e = sp.value_load(eti[0:1, bass.ds(t, 1)], min_val=0, max_val=NE - 1)
                dst = W if what == "gu" else work
                w = hi - lo
                sp.dma_start(dst[:, slot * w:(slot + 1) * w],
                             wexp[bass.ds(e, 1), :, lo:hi].rearrange("a p n -> (a p) n")).then_inc(sems[slot], 16)

            sp.wait_ge(s_eti, 1)
            load_tile(0, 0, "gu", s_gu)
            sp.wait_ge(t_y, 2 * TT)
            sp.wait_ge(s_abp, 40)
            sp.wait_ge(s_T, 2)
            with sp.Fori(0, nq) as i:
                for k in range(4):
                    gate(sp, "sp", s_hh, i * 4 + (k + 2))
                    load_tile(i * 4 + (k + 1), (k + 1) % 4, "gu", s_gu)
                    gate(sp, "sp", s_y, i * 8 + (2 * k + 2))
                    load_tile(i * 4 + k, k, "dn", s_dn)
            gate(sp, "sp", s_add, nq * 64 + 32)
            for t in range(TT):
                n = min(P, NT - t * P)
                sp.dma_start(work[0:n, t * D:(t + 1) * D], ffrows[t * P:t * P + n, :]).then_inc(s_f1, 16)
            sp.wait_ge(s_ln, LN1 + 14)
            sp.wait_ge(s_laf, 16)
            sp.dma_start(yT, Xb[:, :]).then_inc(s_f4, 16)
            sp.wait_ge(s_f4, 16)
            sp.wait_ge(s_sout, 192)

        @block.tensor
        def _(pe):
            pe.wait_ge(s_small, 48)
            pe.wait_ge(s_cs, 1)
            def quad_ready(q):
                pe.wait_ge(s_w[q % 4], 16 * (q // 4 + 1))

            def modulation(first, last):
                for n in range(first, last):
                    q = Q_ADA[n]
                    quad_ready(q)
                    for u in range(4):
                        at = (4 * n + u) * NCOND
                        for c in range(KC):
                            mm = pe.matmul(ps[:, 7, at:at + NCOND], ring[:, q % 4, u, c, :], conds[:, c, :],
                                           start=(c == 0), stop=(c == KC - 1))
                    mm.then_inc(s_wfree, 1)

            modulation(0, 4)
            pe.wait_ge(s_h, 9)

            def gate_proj(n):
                m, lo, hi, bank = gate_unit(n)
                q = Q_G[n // 8]
                quad_ready(q)
                if n < 24:
                    pe.wait_ge(*((s_g3, n) if n else (s_md, 4)))
                elif n > 24:
                    pe.wait_ge(s_g3, n - (n > 25))
                else:
                    pe.wait_ge(s_oc, 48)
                hi = lo + HALF
                for c in range(KC):
                    mm = pe.matmul(ps[:, bank, 0:HALF], ring[:, q % 4, m % 4, c, :], H[:, c, lo:hi],
                                   start=(c == 0), stop=(c == KC - 1))
                mm.then_inc(s_g1, 1)

            def fill(what, n):
                if what == "mod":
                    modulation(n, n + 1)
                else:
                    gate_proj(n)

            n = 0
            for gi, what, a, b in ITEMS:
                g = GROUPS[gi]
                if gi and n == taken(gi - 1, "v"):
                    recurrence_pe(pe, gi - 1, fill)
                    pe.wait_ge(s_pm, 16 * gi)
                bank = n % 2
                if n >= 2:
                    pe.wait_ge(s_zev, n - 1)
                if what == "v":
                    q = (Q_VA + a) if gi == 0 else Q_H[gi - 1][0]
                    rows = min(P, NT - b * P)
                    quad_ready(q)
                    for c in range(KC):
                        mm = pe.matmul(ps[0:rows, bank, :], H[:, c, b * P:b * P + rows], ring[:, q % 4, :, c, :],
                                       start=(c == 0), stop=(c == KC - 1))
                elif what == "gl":
                    w = S("wgk1").rearrange("p (c r) -> p c r", c=KC)
                    for c in range(KC):
                        mm = pe.matmul(ps[0:RANK, bank, 0:HALF], w[:, c, :], H[:, c, halves[b][0]:halves[b][1]],
                                       start=(c == 0), stop=(c == KC - 1))
                elif what == "g":
                    pe.wait_ge(s_zev, 2)
                    mm = pe.matmul(ps[:, bank, 0:HALF], gk2[:, a * P:(a + 1) * P], gkl[:, halves[b][0]:halves[b][1]],
                                   start=True, stop=True)
                else:
                    q = g["qs"] if what == "q" else g["fs"]
                    quad_ready(q)
                    for c in range(KC):
                        mm = pe.matmul(ps[:, bank, 0:HALF], ring[:, q % 4, a, c, :],
                                       H[:, c, halves[b][0]:halves[b][1]], start=(c == 0), stop=(c == KC - 1))
                mm.then_inc(s_z, 1)
                n += 1
            recurrence_pe(pe, 2, fill)
            for n in range(24, 32):
                gate_proj(n)

            def answers(b):
                pe.wait_ge(s_sn, 12 * (b + 1))
                for j in range(16):
                    h = j // 2 if j < 8 else j - 4
                    mm = pe.matmul(ps[:, 4, DEC * j + b:DEC * j + b + 1], snew[:, b % 2, j * P:(j + 1) * P],
                                   sq_[:, h, b:b + 1], start=True, stop=True)
                mm.then_inc(s_sop, 1)

            for b in range(DEC):
                pe.wait_ge(s_vm, b + 1)
                for j in range(4):
                    since(pe, s_sn, 12 * (b - 1) + (2, 4, 8, 12)[j])
                    pe.matmul(ps[:, j, :], ones[0:DEC, :], vm[0:DEC, b % 2, j * 512:(j + 1) * 512],
                              start=True, stop=True).then_inc(s_vb, 1)
                if b:
                    answers(b - 1)
            answers(DEC - 1)
            pe.wait_ge(s_sn2, 2)
            pe.matmul(ps[:, 5, 0:128], ones, oS2.rearrange("p j b -> p (j b)"), start=True, stop=True).then_inc(s_sop, 1)
            pe.wait_ge(s_sn2, 6)
            pe.wait_ge(s_g3, 32)
            n = 0
            for m in range(KC):
                q = Q_P + m
                quad_ready(q)
                for hf, (lo, hi) in enumerate(halves):
                    if n >= 2:
                        pe.wait_ge(s_p3a, 2 * (n - 1))
                    for u, rhs in enumerate((H, oa, H, ob)):
                        for c in range(KC):
                            mm = pe.matmul(ps[:, 4 * hf + u, 0:HALF], ring[:, q % 4, u, c, :], rhs[:, c, lo:hi],
                                           start=(c == 0), stop=(c == KC - 1))
                        mm.then_inc(s_p1, 1)
                    n += 1
            pe.wait_ge(s_p3, 16)
            n = 0
            for q in range(Q_O, NQ):
                quad_ready(q)
                for u in range(4):
                    if n >= 4:
                        pe.wait_ge(s_o2, n - 2)
                        for hf in range(2):
                            mean_pe(pe, n // 2 - 2, hf)
                    for lo, hi in halves:
                        if n >= 2:
                            pe.wait_ge(s_o2, n - 1)
                        for c in range(KC):
                            mm = pe.matmul(ps[:, n % 2, 0:HALF], ring[:, q % 4, u, c, :], mg[:, c, lo:hi],
                                           start=(c == 0), stop=(c == KC - 1))
                        mm.then_inc(s_o1, 1)
                        n += 1
            for c in (KC - 2, KC - 1):
                pe.wait_ge(s_o2, 2 * c + 2)
                for hf in range(2):
                    mean_pe(pe, c, hf)
            variance_pe(pe, 0)
            pe.wait_ge(s_ln, LN1)

            pe.wait_ge(s_route, 16)
            wr = R("w").rearrange("p (c e) -> p c e", c=KC)
            for t in range(TT):
                rows = min(P, NT - t * P)
                for c in range(KC):
                    mm = pe.matmul(ps[0:rows, 0, t * NE:(t + 1) * NE], H[:, c, t * P:t * P + rows], wr[:, c, :],
                                   start=(c == 0), stop=(c == KC - 1))
            mm.then_inc(s_r1, 1)
            for t in range(TT):
                rows = min(P, NT - t * P)
                for hf in range(2):
                    n = 2 * t + hf
                    if n >= 2:
                        pe.wait_ge(s_hc, n - 1)
                    for c in range(4):
                        mm = pe.transpose(ps[0:rows, 1 + n % 2, c * P:(c + 1) * P],
                                          H[:, 4 * hf + c, t * P:t * P + rows], ident)
                    mm.then_inc(s_ht, 1)
            pe.wait_ge(s_msk, 1)
            for t in range(TT):
                rows = min(P, NT - t * P)
                pe.matmul(ps[:, 3, 0:NE], ones[0:rows, :], msk[0:rows, t, :], start=(t == 0), stop=(t == TT - 1))
            for t in range(TT):
                rows = min(P, NT - t * P)
                for t2 in range(t + 1):
                    k = P if t2 < t else rows
                    lhs = ones[0:k, 0:rows] if t2 < t else R("tri")[0:k, 0:rows]
                    mm = pe.matmul(ps[0:rows, 4, t * NE:(t + 1) * NE], lhs, msk[0:k, t2, :],
                                   start=(t2 == 0), stop=(t2 == t))
            mm.then_inc(s_rp, 1)
            def table(n):
                rows = min(P, NT - n // TOPK * P)
                pe.wait_ge(s_ab, 3 * n + 3)
                pe.wait_ge(s_abq, n + 1)
                pe.matmul(ps[0:TS, 5, 0:3 * MAXT], Aoh[0:rows, n % 2, :],
                          Boh[0:rows, n % 2, :, :].rearrange("p c t -> p (c t)"),
                          start=(n == 0), stop=(n == 39)).then_inc(s_abp, 1)

            pe.wait_ge(s_shw, 16)
            pe.wait_ge(s_hc, 2 * TT)
            for n in range(4):
                f, (lo, hi) = n % 2, halves[n // 2]
                if n >= 2:
                    pe.wait_ge(t_sg, 2 * n - 2)
                for k in range(2):
                    for c in range(KC):
                        mm = pe.matmul(ps[:, (1 + k, 6 + k)[f], 0:HALF], GU[:, 3, c, k * FE + f * P:k * FE + (f + 1) * P], H[:, c, lo:hi],
                                       start=(c == 0), stop=(c == KC - 1))
                mm.then_inc(t_hh, 1)
            pe.wait_ge(t_a, 4)
            pe.wait_ge(s_shd, 16)
            for t in range(TT):
                rows = min(P, NT - t * P)
                if t >= 2:
                    pe.wait_ge(t_yc, 2 * t - 2)
                for hf in range(2):
                    for f in range(2):
                        mm = pe.matmul(ps[0:rows, (1, 6)[t % 2] + hf, :], shT[:, f, t * P:t * P + rows],
                                       WD[:, 3, f, hf * 512:(hf + 1) * 512], start=(f == 0), stop=(f == 1))
                    mm.then_inc(t_y, 1)
                for n in range(TOPK * t, TOPK * (t + 1)):
                    table(n)
            pe.wait_ge(s_T, 2)
            pe.wait_ge(t_yc, 2 * TT)
            pe.sem_inc(s_hh, 4)
            pe.sem_inc(s_y, 8)
            pe.sem_inc(s_xt, 4)
            nq = pe.value_load(qni[0:1, 0:1], min_val=1, max_val=MAXT // 4)

            def turn(t, k, gathered):
                gate(pe, "pe", s_ga[k % 2], gathered)
                gate(pe, "pe", s_xc, t * 2 + 2)
                for hf in range(2):
                    for c in range(4):
                        mm = pe.transpose(ps[:, 6 + hf, c * P:(c + 1) * P],
                                          xg[:, k % 2, (4 * hf + c) * P:(4 * hf + c + 1) * P], ident)
                    mm.then_inc(s_xt, 1)

            def gate_up(t, k, loaded):
                gate(pe, "pe", s_xc, t * 2 + 4)
                gate(pe, "pe", s_gu[k % 4], loaded)
                gate(pe, "pe", s_a, t + 1)
                for c in range(KC):
                    mm = pe.matmul(ps[:, k % 2, :], xe[:, k % 2, c, :], GU[:, k % 4, c, :],
                                   start=(c == 0), stop=(c == KC - 1))
                mm.then_inc(s_hh, 1)

            turn(0, 0, 16)
            gate_up(0, 0, 16)
            turn(1, 1, 16)
            with pe.Fori(0, nq) as i:
                for k in range(4):
                    t = i * 4 + k
                    gate(pe, "pe", s_a, i * 4 + (k + 3))
                    gate(pe, "pe", s_ac, t + 1)
                    for f in range(2):
                        mm = pe.transpose(ps[:, 2, f * P:(f + 1) * P], av[:, k % 2, f * P:(f + 1) * P], ident)
                    mm.then_inc(s_at, 1)
                    gate_up(i * 4 + (k + 1), k + 1, i * 16 + (16 if k < 3 else 32))
                    gate(pe, "pe", s_ac, i * 4 + (k + 2))
                    gate(pe, "pe", s_dn[k], i * 16 + 16)
                    for hf in range(2):
                        gate(pe, "pe", s_yc, i * 8 + (2 * k + hf + 1))
                        for f in range(2):
                            mm = pe.matmul(ps[:, 4 + hf, :], aT[:, k % 2, f, :], WD[:, k, f, hf * 512:(hf + 1) * 512],
                                           start=(f == 0), stop=(f == 1))
                        mm.then_inc(s_y, 1)
                    turn(i * 4 + (k + 2), k, i * 32 + 16 * (k // 2 + 2))

            for t in range(TT):
                rows = min(P, NT - t * P)
                pe.wait_ge(s_f1, 16 * TT)
                for hf in range(2):
                    n = 2 * t + hf
                    if n >= 2:
                        pe.wait_ge(s_f3, n - 1)
                    for c in range(4):
                        mm = pe.transpose(ps[:, n % 2, c * P:c * P + rows],
                                          work[0:rows, t * D + (4 * hf + c) * P:t * D + (4 * hf + c + 1) * P],
                                          ident[0:rows, 0:rows])
                    mm.then_inc(s_f2, 1)
            pe.wait_ge(s_f3, 2 * TT)
            for hf in range(2):
                for c in range(KC):
                    mean_pe(pe, c, hf)
            variance_pe(pe, 1)

        @block.scalar
        def _(act):
            act.wait_ge(s_small, 48)
            act.activation(conds, conds, ACT.Silu).then_inc(s_cs, 1)
            act.wait_ge(s_lb, 3)
            act.activation(lbx, lbx, ACT.Exp).then_inc(s_lb, 1)
            n = 0
            for gi, what, a, b in ITEMS:
                g = GROUPS[gi]
                if gi and n == taken(gi - 1, "v"):
                    recurrence_act(act, gi - 1)
                bank = n % 2
                act.wait_ge(s_z, n + 1)
                lo, hi = halves[b] if what != "v" else (0, 0)
                if n == 0:
                    act.wait_ge(s_h, 9)
                if what == "v":
                    rows = min(P, NT - b * P)
                    at = {0: a * 512, 1: 1024, 2: 1536}[gi]
                    dst = V[:, b, a * 512:(a + 1) * 512] if b < 4 else Vs[:, at:at + 512]
                    act.activation(dst, ps[0:rows, bank, :], ACT.Copy).then_inc(s_zev, 1)
                elif what == "gl":
                    act.activation(gkl[:, lo:hi], ps[0:RANK, bank, 0:HALF], ACT.Copy).then_inc(s_zev, 1)
                elif what == "g":
                    act.activation(g4[:, a, lo:hi], ps[:, bank, 0:HALF], ACT.Identity, bias=S("b_gk")[:, a:a + 1]).then_inc(s_zev, 1)
                elif what == "q":
                    if gi == 0:
                        act.activation(q4[:, a, lo:hi], ps[:, bank, 0:HALF], ACT.Copy, scale=P ** -0.5).then_inc(s_zev, 1)
                    else:
                        act.activation(q4[:, a, lo:hi], ps[:, bank, 0:HALF], ACT.Silu).then_inc(s_zev, 1)
                else:
                    if gi == 0:
                        act.activation(k4[:, a, lo:hi], ps[:, bank, 0:HALF], ACT.Copy).then_inc(s_zev, 1)
                    else:
                        act.activation(k4[:, a, lo:hi], ps[:, bank, 0:HALF], ACT.Sigmoid).then_inc(s_zev, 1)
                n += 1
                if what == "g" and (a, b) == (3, 1):
                    tmp_ = view(work, 10336, 4 * NT)
                    act.wait_ge(s_zev, n)
                    act.activation(tmp_, Gb, ACT.Abs).then_inc(s_gk, 1)
                    act.wait_ge(s_gk, 1)
                    act.activation(tmp_, tmp_, ACT.Exp, scale=-1.0).then_inc(s_gk, 1)
                    act.wait_ge(s_gk, 2)
                    act.activation(tmp_, tmp_, ACT.Ln, bias=1.0).then_inc(s_gk, 1)
                if gi and what == "q" and (a, b) == (3, 1):
                    act.wait_ge(s_kf, 4 * gi)
                    act.activation(Gb, Kb, ACT.Ln).then_inc(s_in, 1)
            recurrence_act(act, 2)

            for n in range(24, 32):
                gate_act(act, n)

            for b in range(DEC):
                act.wait_ge(s_si[b % 2], 16 * (b // 2 + 1))
                for h in range(12):
                    lo, hi = (h * GV, (h + 1) * GV) if h < GH else (1024 + (h - 4) * HV, 1024 + (h - 3) * HV)
                    act.activation(sin[:, b % 2, lo:hi], sin[:, b % 2, lo:hi], ACT.Copy, scale=sa_[:, h, b:b + 1]).then_inc(s_sa, 1)

            act.wait_ge(s_sn2, 4)
            act.activation(oms.rearrange("p j b -> p (j b)"), oms.rearrange("p j b -> p (j b)"), ACT.Sqrt).then_inc(s_lng, 1)
            act.wait_ge(s_g3, 32)

            n = 0
            for m in range(KC):
                for hf in range(2):
                    if n >= 2:
                        act.wait_ge(s_p3, n - 1)
                    for u in (0, 2):
                        act.wait_ge(s_p1, 4 * n + u + 1)
                        act.activation(gtmp[:, u // 2 + 2 * hf, :], ps[:, 4 * hf + u, 0:HALF], ACT.Sigmoid).then_inc(s_p2, 1)
                    n += 1
            layer_norm_act(act, 0)
            act.wait_ge(s_r1, 1)
            act.activation(OB[:, 0:4 * NE], ps[:, 0, 0:4 * NE], ACT.Sigmoid).then_inc(s_r2, 1)
            act.activation(scores[0:DEC, 4, :], ps[0:DEC, 0, 4 * NE:5 * NE], ACT.Sigmoid).then_inc(s_r2, 1)
            for t in range(TT):
                rows = min(P, NT - t * P)
                for hf in range(2):
                    n = 2 * t + hf
                    act.wait_ge(s_ht, n + 1)
                    if t >= 2:
                        act.wait_ge(s_hd[t % 2], 16 * (t // 2))
                    act.activation(hrow[0:rows, t % 2, hf * 512:(hf + 1) * 512], ps[0:rows, 1 + n % 2, :], ACT.Copy)\
                       .then_inc(s_hc, 1)
            for n in range(4):
                act.wait_ge(t_hh, n + 1)
                if n >= 1:
                    act.wait_ge(t_a, n)
                for k, fn in enumerate((ACT.Silu, ACT.Copy)):
                    act.activation(shg[:, k, :], ps[:, (1 + k, 6 + k)[n % 2], 0:HALF], fn).then_inc(t_sg, 1)
            act.wait_ge(s_et, 32)
            act.activation(eti[0:1, 0:MAXT + 4], erow, ACT.Copy).then_inc(s_eti, 1)
            for t in range(TT):
                rows = min(P, NT - t * P)
                if t >= 2:
                    act.wait_ge(t_st[t % 2], 16 * (t // 2))
                for hf in range(2):
                    act.wait_ge(t_y, 2 * t + hf + 1)
                    act.activation(yb[0:rows, t % 2, hf * 512:(hf + 1) * 512], ps[0:rows, (1, 6)[t % 2] + hf, :], ACT.Copy)\
                       .then_inc(t_yc, 1)
            act.wait_ge(s_T, 2)
            act.sem_inc(s_xc, 2)
            act.sem_inc(s_ac, 1)
            nq = act.value_load(qni[0:1, 0:1], min_val=1, max_val=MAXT // 4)

            def take_x(t, k):
                gate(act, "act", s_hh, t + 3)
                for hf in range(2):
                    gate(act, "act", s_xt, t * 2 + (5 + hf))
                    act.activation(xe[:, k % 2, 4 * hf:4 * hf + 4, :].rearrange("p c n -> p (c n)"), ps[:, 6 + hf, :],
                                   ACT.Copy).then_inc(s_xc, 1)

            def silu(t, k):
                gate(act, "act", s_hh, t + 5)
                gate(act, "act", s_a, t + 1)
                act.activation(sg[:, k % 2, :], ps[:, k % 2, 0:FE], ACT.Silu).then_inc(s_sg, 1)

            take_x(0, 0)
            silu(0, 0)
            take_x(1, 1)
            with act.Fori(0, nq) as i:
                for k in range(4):
                    gate(act, "act", s_at, i * 4 + (k + 1))
                    gate(act, "act", s_y, i * 8 + (2 * k + 6))
                    act.activation(aT[:, k % 2, :, :].rearrange("p f n -> p (f n)"), ps[:, 2, 0:2 * P], ACT.Copy)\
                       .then_inc(s_ac, 1)
                    silu(i * 4 + (k + 1), k + 1)
                    take_x(i * 4 + (k + 2), k)
            layer_norm_act(act, 1)

        @block.gpsimd
        def _(pool):
            pool.wait_ge(s_small, 48)
            for gi in range(3):
                v, base = GROUPS[gi]["v"], 16 * gi

                def mk(pair):
                    p = pair % 2
                    pool.wait_ge(s_E, 5 * pair + 2)
                    kk = k4[:, pair // 2 % 4, p * 256:(p + 1) * 256]
                    for l in range(LEV):
                        s = CH >> (l + 1)
                        e = M[:, p, l, :].rearrange("p (n s) -> p n s", s=2 * s)[:, :, 0:s]
                        pool.tensor_tensor(e, e, kk.rearrange("p (n s) -> p n s", s=2 * s)[:, :, 0:s], ALU.mult)
                    pool.tensor_tensor(M[:, p, 7, :], M[:, p, 7, :], kk, ALU.mult).then_inc(s_Mk, 1)

                def root(n):
                    ms, rs = ssum[:, n % 2:n % 2 + 1], rstd[:, n % 2:n % 2 + 1]
                    pool.wait_ge(s_ss, n + 1)
                    pool.tensor_scalar(ms, ms, 1.0 / v, EPS, ALU.mult, ALU.add).then_inc(s_rs, 1)
                    pool.wait_ge(s_rs, n + 1)
                    pool.tensor_tensor(rs, ms, C("mhalf"), ALU.pow).then_inc(s_rstd, 1)

                mk(8 * gi)
                mk(8 * gi + 1)
                for c in range(1, 17):
                    root(base + c - 1)
                    if c % 2 == 0 and c <= 12:
                        mk(8 * gi + c // 2 + 1)
            pool.wait_ge(s_zev, len(ITEMS))
            pool.wait_ge(s_rec, 3)
            for b in range(DEC):
                since(pool, s_vb, 4 * (b - 1))
                pool.tensor_scalar(vm[0:DEC, b % 2, :], Vs, ident[0:DEC, b:b + 1], None, ALU.mult).then_inc(s_vm, 1)
            pool.wait_ge(s_ln, LN1)
            pool.memset(zrow, 0.0).then_inc(s_zero, 1)
            for n in range(4):
                lo, hi = halves[n // 2]
                pool.wait_ge(t_sg, 2 * n + 2)
                pool.tensor_tensor(shT[:, n % 2, lo:hi], shg[:, 0, :], shg[:, 1, :], ALU.mult).then_inc(t_a, 1)
            pool.wait_ge(s_slots, 1)
            for n in range(TT * TOPK):
                t, k = n // TOPK, n % TOPK
                if n >= 2:
                    pool.wait_ge(s_abp, n - 1)
                pool.tensor_scalar(Aoh[:, n % 2, :], R("iota")[:, 0:TS], slotk[:, t, k:k + 1], None, ALU.is_equal)\
                    .then_inc(s_abq, 1)
            pool.wait_ge(s_T, 2)
            pool.wait_ge(t_st[0], 48)
            pool.wait_ge(t_st[1], 32)
            rows_stored(pool)
            pool.dma_start(ffrows[TRASH:ROWS, :], zrow).then_inc(s_add, 16)
            pool.dma_start(ffrows[NT:TRASH, :], zrow[0:TRASH - NT, :]).then_inc(s_add, 16)
            pool.wait_ge(s_add, 32)
            nq = pool.value_load(qni[0:1, 0:1], min_val=1, max_val=MAXT // 4)

            def gather(t, k, copied):
                gate(pool, "pool", s_xt, t * 2 + 2)
                pool.tensor_copy(idg[:, k:k + 1], idx_i[:, bass.ds(t, 1)]).then_inc(s_ic, 1)
                gate(pool, "pool", s_ic, copied)
                pool.indirect_dma_start(out=xg[0:TS, k % 2, :], out_offset=None, in_=h2rows,
                                        in_offset=bass.IndirectOffsetOnAxis(ap=idg[0:TS, k:k + 1], axis=0)).then_inc(s_ga[k % 2], 16)

            gather(0, 0, 1)
            gather(1, 1, 2)
            with pool.Fori(0, nq) as i:
                for k in range(4):
                    gather(i * 4 + (k + 2), (k + 2) % 4, i * 8 + (2 * k + 3))
                    gate(pool, "pool", s_add, i * 64 + (16 * k + 32))
                    pool.tensor_copy(ida[:, k:k + 1], idx_i[:, bass.ds(i * 4 + k, 1)]).then_inc(s_ic, 1)
                    gate(pool, "pool", s_yc, i * 8 + (2 * k + 4))
                    gate(pool, "pool", s_ic, i * 8 + (2 * k + 4))
                    pool.indirect_dma_start(out=ffrows, out_offset=bass.IndirectOffsetOnAxis(ap=ida[0:TS, k:k + 1], axis=0),
                                            in_=yb[0:TS, k % 2, :], in_offset=None, compute_op=ALU.add).then_inc(s_add, 16)
            for p in range(2):
                gate(pool, "pool", s_ga[p], nq * 32 + 16)

        @block.vector
        def _(dve):
            dve.wait_ge(s_small, 48)
            lb = S("lb").rearrange("p (r h) -> p r h", r=2)
            def lstep(ins, c=[0]):
                c[0] += 1
                ins.then_inc(s_lb, 1)
                dve.wait_ge(s_lb, c[0])
            lstep(dve.tensor_tensor(lbm, lb[:, 0, :], lb[:, 1, :], ALU.max))
            lstep(dve.tensor_tensor(lbx[:, 0, :], lb[:, 0, :], lbm, ALU.subtract))
            lstep(dve.tensor_tensor(lbx[:, 1, :], lb[:, 1, :], lbm, ALU.subtract))
            def modulation(first, last, scale, done):
                n = last - first
                dve.tensor_tensor(md[:, first:last, :], ps[:, 7, first * NCOND:last * NCOND].rearrange("p (e n) -> p e n", n=NCOND),
                                  S("b_ada")[:, first:last].rearrange("p (e a) -> p e a", a=1).broadcast_to([P, n, NCOND]),
                                  ALU.add).then_inc(s_md, 1)
                dve.wait_ge(s_md, done + 1)
                dve.tensor_scalar(md[:, scale:scale + 8, :], md[:, scale:scale + 8, :], 1.0, None, ALU.add).then_inc(s_md, 1)

            dve.wait_ge(s_wfree, 4)
            modulation(0, 16, SC1, 0)
            dve.wait_ge(s_md, 2)
            dve.wait_ge(s_x, 16)
            for c in range(KC):
                dve.tensor_scalar(H[:, c, 0:SEQ], X[:, c, 0:SEQ], md[:, SC1 + c, 0:1], md[:, SH1 + c, 0:1],
                                  ALU.mult, ALU.add).then_inc(s_h, 1)
            dve.tensor_tensor(H[:, :, SEQ:NT], X[:, :, SEQ:NT], md[:, SC1:SC1 + 8, 1:NCOND], ALU.mult).then_inc(s_md, 1)
            dve.wait_ge(s_md, 3)
            dve.tensor_tensor(H[:, :, SEQ:NT], H[:, :, SEQ:NT], md[:, SH1:SH1 + 8, 1:NCOND], ALU.add).then_inc(s_h, 1)

            for gi in range(3):
                g = GROUPS[gi]
                v, base = g["v"], 16 * gi
                if gi == 0:
                    dve.wait_ge(s_gk, 3)
                    dve.tensor_scalar(Gb, Gb, 0.0, None, ALU.min).then_inc(s_in, 1)
                    dve.wait_ge(s_in, 1)
                    dve.tensor_tensor(Gb, Gb, view(work, 10336, 4 * NT), ALU.subtract).then_inc(s_in, 1)
                    dve.wait_ge(s_in, 2)
                    dve.tensor_scalar(Gb, Gb, 1.0 / 16.0, None, ALU.mult).then_inc(s_in, 1)
                    dve.wait_ge(s_in, 3)
                    dve.wait_ge(s_lb, 4)
                    dve.tensor_tensor(lbm, lbx[:, 0, :], lbx[:, 1, :], ALU.add).then_inc(s_lb, 1)
                    dve.wait_ge(s_lb, 5)
                    dve.reciprocal(lbm, lbm).then_inc(s_lb, 1)
                    dve.wait_ge(s_lb, 6)
                    dve.tensor_tensor(lbt, lbx[:, 0, :], lbm, ALU.mult).then_inc(s_lb, 1)
                    dve.wait_ge(s_lb, 7)
                    dve.tensor_scalar(omlb, lbt, -1.0, 1.0, ALU.mult, ALU.add).then_inc(s_lb, 1)
                    dve.wait_ge(s_lb, 8)
                else:
                    dve.wait_ge(s_zev, taken(gi, "k"))
                    for h in range(4):
                        hd = 4 * (gi - 1) + h
                        dve.tensor_scalar(k4[:, h, :], k4[:, h, :], omlb[:, hd:hd + 1], lbt[:, hd:hd + 1],
                                          ALU.mult, ALU.add).then_inc(s_kf, 1)
                    dve.wait_ge(s_zev, taken(gi, "q"))
                    dve.tensor_scalar(Qb, Qb, P ** -0.5, None, ALU.mult).then_inc(s_fk, 1)
                    dve.wait_ge(s_kf, 4 * gi)
                    dve.wait_ge(s_in, 3 + gi)
                    dve.tensor_scalar(Kb, Kb, -1.0, 1.0, ALU.mult, ALU.add).then_inc(s_fk, 1)
                for h in range(4):
                    dve.tensor_tensor_scan(g4[:, h, :], C("reset"), g4[:, h, :], 0.0, ALU.mult, ALU.add).then_inc(s_cum, 1)
                dve.wait_ge(s_cum, 4 * gi + 4)
                if gi:
                    dve.wait_ge(s_fk, 2 * gi)
                else:
                    dve.wait_ge(s_zev, taken(0, "k"))
                dve.tensor_copy(sq_[:, 4 * gi:4 * gi + 4, :], q4[:, :, SEQ:NT]).then_inc(s_smp, 1)
                dve.tensor_copy(sk_[:, 4 * gi:4 * gi + 4, :], k4[:, :, SEQ:NT]).then_inc(s_smp, 1)

                def diffs(pair):
                    p = pair % 2
                    since(dve, s_sc, 2 * pair - 2)
                    b = g4[:, pair // 2 % 4, p * 256:(p + 1) * 256]
                    for l in range(LEV + 1):
                        w = CH >> l if l < LEV else CH
                        at = w // 2 - 1 if l < LEV else CH - 1
                        bb = b.rearrange("p (n s) -> p n s", s=w)
                        ins = dve.tensor_tensor(M[:, p, l, :].rearrange("p (n s) -> p n s", s=w), bb,
                                                bb[:, :, at:at + 1].broadcast_to([P, 256 // w, w]), ALU.subtract)
                    ins.then_inc(s_D, 1)

                def mq(pair):
                    p = pair % 2
                    qq = q4[:, pair // 2 % 4, p * 256:(p + 1) * 256]
                    dve.wait_ge(s_E, 5 * pair + 2)
                    for l in range(LEV):
                        s = CH >> (l + 1)
                        e = M[:, p, l, :].rearrange("p (n s) -> p n s", s=2 * s)[:, :, s:2 * s]
                        dve.tensor_tensor(e, e, qq.rearrange("p (n s) -> p n s", s=2 * s)[:, :, s:2 * s], ALU.mult)
                    dve.wait_ge(s_E, 5 * pair + 5)
                    dve.tensor_tensor(M[:, p, 8, :], M[:, p, 8, :], qq, ALU.mult).then_inc(s_Mq, 1)

                def mask(n):
                    dve.wait_ge(s_sc, n + 1)
                    since(dve, s_st, n)
                    dve.tensor_tensor(Pm, ps[:, 0:2, :].rearrange("p b t -> p (b t)"), C("masks"), ALU.mult).then_inc(s_pm, 1)
                    dve.wait_ge(s_pm, n + 1)
                    since(dve, s_o, n - 1)
                    dve.tensor_reduce(ST[:, n % 2, :], Pm.rearrange("p (l t) -> p t l", l=8), AX, ALU.add).then_inc(s_st, 1)

                def new_state(n):
                    cc = n % 4
                    dve.wait_ge(s_u, n + 1)
                    dst = state[:, (cc + 1) % 2 if cc < 3 else 2, 0:v]
                    if cc == 3:
                        since(dve, s_sout, n // 4 * 16)
                    else:
                        since(dve, s_o, n)
                    if cc:
                        dve.wait_ge(s_state, n)
                        dve.scalar_tensor_tensor(out=dst, in0=state[:, cc % 2, 0:v], scalar=elast[:, n // 2 % 2, n % 2:n % 2 + 1],
                                                 in1=ps[:, 3, 0:v], op0=ALU.mult, op1=ALU.add).then_inc(s_state, 1)
                    else:
                        dve.tensor_copy(dst, ps[:, 3, 0:v]).then_inc(s_state, 1)

                def take_o(n):
                    nj = v // P
                    h, cc = n // 4 % 4, n % 4
                    dve.wait_ge(s_ot, n + 1)
                    dve.tensor_copy(g["out"][:, h * nj + g["first"]:(h + 1) * nj + g["first"], cc * CH:(cc + 1) * CH],
                                    ps[:, 6, 0:v].rearrange("p (j t) -> p j t", t=CH)).then_inc(s_oc, 1)

                diffs(8 * gi)
                diffs(8 * gi + 1)
                mq(8 * gi)
                mq(8 * gi + 1)
                for c in range(18):
                    if c and filled(gi, c - 1) is not None:
                        gate_mul(dve, filled(gi, c - 1))
                    if c < 16:
                        mask(base + c)
                        new_state(base + c)
                    if c % 2 and c <= 11:
                        diffs(8 * gi + (c + 3) // 2)
                    if c >= 2:
                        take_o(base + c - 2)
                    if c % 2 == 0 and 2 <= c <= 12:
                        mq(8 * gi + c // 2 + 1)
                if gi == 0:
                    dve.wait_ge(s_wfree, 12)
                    modulation(16, 48, SC2, 3)
                dve.wait_ge(s_oc, base + 16)
                dve.sem_inc(s_rec, 1)

            for n in range(24, 32):
                gate_mul(dve, n)
            dve.wait_ge(s_g2, 32)
            for k in range(2):
                a_gates = gdec[:, 0:8, :].rearrange("p (h k) b -> p h k b", k=2)[:, :, k, :]
                dve.tensor_scalar(a_gates, a_gates, S("gla_w")[:, k:k + 1], None, ALU.mult).then_inc(s_g3, 1)
            dve.tensor_scalar(gdec[:, 8:16, :], gdec[:, 8:16, :], S("hgrn_w"), None, ALU.mult).then_inc(s_g3, 1)

            dve.wait_ge(s_smp, 9)
            for b in range(DEC):
                since(dve, s_so[b % 2], 16 * (b // 2))
                since(dve, s_sop, b - 1)
                for h in range(12):
                    lo, hi = (h * GV, (h + 1) * GV) if h < GH else (1024 + (h - 4) * HV, 1024 + (h - 3) * HV)
                    dve.wait_ge(s_vb, 4 * b + lo // 512 + 1)
                    dve.wait_ge(s_sa, 12 * b + h + 1)
                    dve.scalar_tensor_tensor(out=snew[:, b % 2, lo:hi], in0=ps[:, lo // 512, lo % 512:lo % 512 + hi - lo],
                                             scalar=sk_[:, h, b:b + 1], in1=sin[:, b % 2, lo:hi],
                                             op0=ALU.mult, op1=ALU.add).then_inc(s_sn, 1)
            dve.wait_ge(s_sop, 8)
            dve.tensor_copy(oS.rearrange("p j b -> p (j b)"), ps[:, 4, 0:128]).then_inc(s_sn2, 1)
            dve.wait_ge(s_sn2, 1)
            dve.tensor_tensor(oS2, oS, oS, ALU.mult).then_inc(s_sn2, 1)
            dve.wait_ge(s_sop, 9)
            sums = ps[:, 5, 0:128].rearrange("p (j b) -> p j b", b=DEC)
            dve.tensor_copy(oms, sums).then_inc(s_sn2, 1)
            dve.wait_ge(s_sn2, 3)
            pair = oms[:, 0:8, :].rearrange("p (h k) b -> p h k b", k=2)
            both = oS2[:, 0:8, :].rearrange("p (h k) b -> p h k b", k=2)
            for k in range(2):
                ins = dve.tensor_tensor(both[:, :, k, :], pair[:, :, 0, :], pair[:, :, 1, :], ALU.add)
            ins.then_inc(s_mod, 1)
            dve.wait_ge(s_mod, 1)
            dve.tensor_scalar(oms[:, 0:8, :], oS2[:, 0:8, :], 1.0 / GV, EPS, ALU.mult, ALU.add).then_inc(s_mod, 1)
            dve.tensor_scalar(oms[:, 8:16, :], oms[:, 8:16, :], 1.0 / HV, EPS, ALU.mult, ALU.add).then_inc(s_sn2, 1)
            dve.wait_ge(s_mod, 2)
            dve.wait_ge(s_lng, 1)
            dve.reciprocal(oms, oms).then_inc(s_mod, 1)
            dve.wait_ge(s_mod, 3)
            dve.tensor_tensor(oS, oS, oms, ALU.mult).then_inc(s_mod, 1)
            dve.wait_ge(s_mod, 4)
            dve.wait_ge(s_g3, 35)
            dve.tensor_tensor(oa[:, :, SEQ:NT], oS[:, 0:8, :], gdec[:, 0:8, :], ALU.mult).then_inc(s_sn2, 1)
            dve.tensor_tensor(ob[:, :, SEQ:NT], oS[:, 8:16, :], gdec[:, 8:16, :], ALU.mult).then_inc(s_sn2, 1)
            dve.wait_ge(s_sn2, 6)

            dve.wait_ge(s_sout, 192)
            for b in range(2):
                dve.wait_ge(s_so[b], 64)
            n = 0
            for m in range(KC):
                for hf, (lo, hi) in enumerate(halves):
                    dve.wait_ge(s_p2, 2 * n + 2)
                    dve.wait_ge(s_p1, 4 * n + 4)
                    for u in range(2):
                        dve.tensor_tensor(gtmp[:, u + 2 * hf, :], gtmp[:, u + 2 * hf, :], ps[:, 4 * hf + 2 * u + 1, 0:HALF],
                                          ALU.mult).then_inc(s_p3a, 1)
                    dve.wait_ge(s_p3a, 2 * n + 2)
                    dve.tensor_tensor(mg[:, m, lo:hi], gtmp[:, 2 * hf, :], gtmp[:, 1 + 2 * hf, :], ALU.add).then_inc(s_p3, 1)
                    n += 1
            dve.wait_ge(s_x2, 16)
            dve.tensor_scalar(Xb[:, :], Xb[:, :], ALPHA, None, ALU.mult).then_inc(s_fx, 1)
            dve.wait_ge(s_fx, 1)
            for m in range(KC):
                for hf, (lo, hi) in enumerate(halves):
                    n = 2 * m + hf
                    dve.wait_ge(s_o1, n + 1)
                    w = min(hi, SEQ) - lo
                    ins = dve.scalar_tensor_tensor(out=X[:, m, lo:lo + w], in0=ps[:, n % 2, 0:w], scalar=md[:, G1 + m, 0:1],
                                                   in1=X[:, m, lo:lo + w], op0=ALU.mult, op1=ALU.add)
                    if hi > SEQ:
                        dec = view(tiny, 200, DEC)
                        dve.tensor_tensor(dec, ps[:, n % 2, w:w + DEC], md[:, G1 + m, 1:NCOND], ALU.mult).then_inc(s_fx, 1)
                        dve.wait_ge(s_fx, m + 2)
                        ins = dve.tensor_tensor(X[:, m, SEQ:NT], X[:, m, SEQ:NT], dec, ALU.add)
                    ins.then_inc(s_o2, 1)
            dve.wait_ge(s_o2, 16)
            layer_norm_dve(dve, 0)
            for c in range(KC):
                dve.tensor_scalar(H[:, c, 0:SEQ], X[:, c, 0:SEQ], md[:, SC2 + c, 0:1], md[:, SH2 + c, 0:1],
                                  ALU.mult, ALU.add).then_inc(s_ln, 1)
            dve.tensor_tensor(H[:, :, SEQ:NT], X[:, :, SEQ:NT], md[:, SC2:SC2 + 8, 1:NCOND], ALU.mult).then_inc(s_ln, 1)
            dve.wait_ge(s_ln, LN1 - 1)
            dve.tensor_tensor(H[:, :, SEQ:NT], H[:, :, SEQ:NT], md[:, SH2:SH2 + 8, 1:NCOND], ALU.add).then_inc(s_ln, 1)

            dve.wait_ge(s_ln, LN1)
            dve.tensor_scalar(Xb[:, :], Xb[:, :], ALPHA, None, ALU.mult).then_inc(s_fx, 1)

            count = [0]

            def step(ins):
                ins.then_inc(s_rv, 1)
                count[0] += 1
                return ins

            def settled():
                dve.wait_ge(s_rv, count[0])

            dve.wait_ge(s_route, 16)
            dve.wait_ge(s_r2, 2)
            grouped = "p t (g k) -> p (t g) k"
            step(dve.tensor_tensor(biased, scores, R("bias").rearrange("p (a e) -> p a e", a=1).broadcast_to([P, TT, NE]), ALU.add))
            settled()
            for t in range(TT):
                for g in range(NG):
                    step(dve.max(g8[:, t, g, :], biased[:, t, g * 8:(g + 1) * 8]))
            settled()
            step(dve.tensor_tensor(grp, g8[:, :, :, 0], g8[:, :, :, 1], ALU.add))
            settled()
            for t in range(TT):
                step(dve.max(top[:, t, :], grp[:, t, :]))
            settled()
            for t in range(TT):
                step(dve.max_index(ui[:, t, :], top[:, t, :], grp[:, t, :]))
            settled()
            step(dve.tensor_copy(idxf, ui))
            settled()
            g4h = view(work, 0, TT * TOPG * NG, "p (t k g) -> p t k g", t=TT, k=TOPG)
            step(dve.tensor_tensor(g4h, R("group").rearrange("p (a b g) -> p a b g", a=1, b=1).broadcast_to([P, TT, TOPG, NG]),
                                   idxf[:, :, 0:TOPG].rearrange("p t (k a) -> p t k a", a=1).broadcast_to([P, TT, TOPG, NG]),
                                   ALU.is_equal))
            settled()
            step(dve.tensor_reduce(gm, g4h.rearrange("p t k g -> p t g k"), AX, ALU.add))
            settled()
            gmf = gm.rearrange("p t g -> p (t g)")
            gmx = gm.rearrange("p t (g a) -> p (t g) a", a=1)
            step(dve.tensor_tensor(tmp.rearrange(grouped, k=8), biased.rearrange(grouped, k=8),
                                   gmx.broadcast_to([P, TT * NG, 8]), ALU.mult))
            settled()
            step(dve.tensor_scalar(gmf, gmf, -1.0, BIG, ALU.add, ALU.mult))
            settled()
            step(dve.tensor_tensor(tmp.rearrange(grouped, k=8), tmp.rearrange(grouped, k=8),
                                   gmx.broadcast_to([P, TT * NG, 8]), ALU.add))
            settled()
            for t in range(TT):
                step(dve.max(top[:, t, :], tmp[:, t, :]))
            settled()
            for t in range(TT):
                step(dve.max_index(ui[:, t, :], top[:, t, :], tmp[:, t, :]))
            settled()
            step(dve.tensor_copy(idxf, ui))
            settled()
            step(dve.tensor_tensor(oh, R("iota")[:, 0:NE].rearrange("p (a b e) -> p a b e", a=1, b=1).broadcast_to([P, TT, TOPK, NE]),
                                   idxf.rearrange("p t (k a) -> p t k a", a=1).broadcast_to([P, TT, TOPK, NE]), ALU.is_equal))
            settled()
            dve.tensor_reduce(msk, oh.rearrange("p t k e -> p t e k"), AX, ALU.add).then_inc(s_msk, 1)
            dve.wait_ge(s_msk, 1)
            step(dve.tensor_tensor(tmp, scores, msk, ALU.mult))
            settled()
            step(dve.tensor_reduce(gsum, tmp, AX, ALU.add))
            settled()
            step(dve.reciprocal(gsum, gsum))
            settled()
            step(dve.tensor_scalar(gsum, gsum, RSCALE, None, ALU.mult))
            settled()
            step(dve.tensor_tensor(gates, scores, gsum.rearrange("p (t a) -> p t a", a=1).broadcast_to([P, TT, NE]), ALU.mult))
            dve.wait_ge(s_rp, 1)
            step(dve.tensor_copy(cnt, ps[:, 3, 0:NE]))
            settled()
            step(dve.tensor_scalar(nti, cnt, 0.0, None, ALU.is_gt))
            settled()
            for k in range(1, -(-NT // TS)):
                step(dve.scalar_tensor_tensor(out=nti, in0=cnt, scalar=float(TS * k), in1=nti, op0=ALU.is_gt, op1=ALU.add))
                settled()
            step(dve.tensor_tensor_scan(incl, ones[:, 0:NE], nti, 0.0, ALU.mult, ALU.add))
            settled()
            step(dve.tensor_scalar(cmp_, incl, R("part"), None, ALU.is_le))
            step(dve.tensor_tensor(excl, incl, nti, ALU.subtract))
            settled()
            step(dve.tensor_reduce(ecol, cmp_, AX, ALU.add))
            settled()
            dve.tensor_scalar(ecol, ecol, float(NE - 1), None, ALU.min).then_inc(s_row, 1)
            step(dve.tensor_scalar(cmp_[:, 0:MAXT // 4], R("quads"), incl[:, NE - 1:NE], None, ALU.is_lt))
            settled()
            step(dve.tensor_reduce(quadn, cmp_[:, 0:MAXT // 4], AX, ALU.add))
            settled()
            dve.tensor_copy(qni[0:1, 0:1], quadn[0:1, :]).then_inc(s_T, 1)
            for t, r in ((slice(0, 4), P), (slice(4, 5), DEC)):
                n = t.stop - t.start
                step(dve.scalar_tensor_tensor(out=pos[0:r, t, :], in0=excl[0:r, :].rearrange("p (a e) -> p a e", a=1).broadcast_to([r, n, NE]),
                                              scalar=float(TS), op0=ALU.mult, op1=ALU.add,
                                              in1=ps[0:r, 4, t.start * NE:t.stop * NE].rearrange("p (t e) -> p t e", t=n)))
            settled()
            for dst, src in ((posk, pos), (gk, gates)):
                step(dve.tensor_tensor(prod, oh, src.rearrange("p t (a e) -> p t a e", a=1).broadcast_to([P, TT, TOPK, NE]), ALU.mult))
                settled()
                step(dve.tensor_reduce(dst, prod, AX, ALU.add))
                settled()
            step(dve.tensor_copy(posi, posk.rearrange("p t k -> p (t k)")))
            settled()
            step(dve.tensor_scalar(hi_i, posi, 7, None, ALU.arith_shift_right))
            settled()
            tile_, slot_, pos_ = (v.rearrange("p t k -> p (t k)") for v in (tilek, slotk, posk))
            step(dve.tensor_copy(tile_, hi_i))
            settled()
            dve.scalar_tensor_tensor(out=slot_, in0=tile_, scalar=-float(TS), in1=pos_, op0=ALU.mult, op1=ALU.add).then_inc(s_slots, 1)
            n = 0
            for t in range(TT):
                for k in range(TOPK):
                    if n >= 2:
                        dve.wait_ge(s_abp, n - 1)
                    tile = tilek[:, t, k:k + 1]
                    upto = R("iota")[:, 0:MAXT]
                    dve.tensor_scalar(Boh[:, n % 2, 0, :], upto, tile, R("token")[:, t:t + 1], ALU.is_equal, ALU.mult).then_inc(s_ab, 1)
                    dve.tensor_scalar(Boh[:, n % 2, 1, :], upto, tile, gk[:, t, k:k + 1], ALU.is_equal, ALU.mult).then_inc(s_ab, 1)
                    dve.tensor_scalar(Boh[:, n % 2, 2, :], upto, tile, None, ALU.is_equal).then_inc(s_ab, 1)
                    n += 1
            dve.wait_ge(s_abp, 40)
            tok, gat, use = (ps[0:TS, 5, c * MAXT:(c + 1) * MAXT] for c in range(3))
            step(dve.tensor_copy(gtabs[0:TS, 0:MAXT], gat))
            step(dve.memset(gtabs[:, MAXT:MAXT + 4], 0.0))
            step(dve.memset(idxt[:, MAXT:MAXT + 4], 1.0))
            step(dve.tensor_scalar(idxt[0:TS, 0:MAXT], use, -1.0, 1.0, ALU.mult, ALU.add))
            settled()
            step(dve.tensor_scalar(idxt[0:TS, :], idxt[0:TS, :], R("trash")[0:TS, :], None, ALU.mult))
            settled()
            step(dve.tensor_tensor(idxt[0:TS, 0:MAXT], idxt[0:TS, 0:MAXT], tok, ALU.add))
            settled()
            dve.tensor_copy(idx_i[0:TS, :], idxt[0:TS, :]).then_inc(s_T, 1)

            dve.sem_inc(s_a, 2)
            dve.sem_inc(s_yc, 2)
            dve.wait_ge(s_T, 2)
            nq = dve.value_load(qni[0:1, 0:1], min_val=1, max_val=MAXT // 4)

            def gated(t, k, copied):
                dve.tensor_copy(gcol[:, k % 4:k % 4 + 1], gtabs[:, bass.ds(t, 1)]).then_inc(s_gc, 1)
                gate(dve, "dve", s_gc, copied)
                gate(dve, "dve", s_sg, t + 1)
                dve.scalar_tensor_tensor(out=av[:, k % 2, :], in0=ps[:, k % 2, FE:2 * FE], scalar=gcol[:, k % 4:k % 4 + 1],
                                         in1=sg[:, k % 2, :], op0=ALU.mult, op1=ALU.mult).then_inc(s_a, 1)

            gated(0, 0, 1)
            with dve.Fori(0, nq) as i:
                for k in range(4):
                    gated(i * 4 + (k + 1), k + 1, i * 4 + (k + 2))
                    gate(dve, "dve", s_add, i * 64 + (16 * k + 16))
                    for hf in range(2):
                        gate(dve, "dve", s_y, i * 8 + (2 * k + hf + 9))
                        dve.tensor_copy(yb[:, k % 2, hf * 512:(hf + 1) * 512], ps[:, 4 + hf, :]).then_inc(s_yc, 1)

            for t in range(TT):
                rows = min(P, NT - t * P)
                for hf in range(2):
                    n = 2 * t + hf
                    dve.wait_ge(s_f2, n + 1)
                    if t < 4:
                        for c in range(4):
                            m = 4 * hf + c
                            ins = dve.scalar_tensor_tensor(out=X[:, m, t * P:(t + 1) * P], in0=ps[:, n % 2, c * P:(c + 1) * P],
                                                           scalar=md[:, G2 + m, 0:1], in1=X[:, m, t * P:(t + 1) * P],
                                                           op0=ALU.mult, op1=ALU.add)
                    else:
                        four = slice(4 * hf, 4 * hf + 4)
                        dec = view(tiny, 184 + 32 * hf, 4 * DEC, "p (c b) -> p c b", c=4)
                        dve.tensor_tensor(dec, ps[:, n % 2, :].rearrange("p (c t) -> p c t", c=4)[:, :, 0:DEC],
                                          md[:, G2 + 4 * hf:G2 + 4 * hf + 4, 1:NCOND], ALU.mult).then_inc(s_fy, 1)
                        dve.wait_ge(s_fy, hf + 1)
                        ins = dve.tensor_tensor(X[:, four, SEQ:NT], X[:, four, SEQ:NT], dec, ALU.add)
                    ins.then_inc(s_f3, 1)
            dve.wait_ge(s_f3, 2 * TT)
            layer_norm_dve(dve, 1)


def kernel(**inputs):
    import concourse.bacc as bacc
    from concourse.bass_utils import run_bass_kernel_spmd as run

    a = {k: np.asarray(v) for k, v in inputs.items()}

    def rows(x):
        return x.reshape(-1, KC, P).transpose(2, 1, 0)

    def blocks(w):
        return w.reshape(KC, P, -1, P).transpose(2, 1, 0, 3).reshape(-1, P, KC * P)

    xT = rows(np.concatenate([a["x_prompt"][0], a["x_sample"][:, 0]])).reshape(P, KC * NT)
    w_in = a["w_in"][0]
    cuts = np.cumsum([0, 512, 512, 1024, 1024, 16, 1024, 1024, 1024, 1024, 1024, 1024])
    qa, ka, va, ga, gk, qb, fb, ib, gb, ua, ub = (w_in[:, cuts[i]:cuts[i + 1]] for i in range(11))
    B = blocks
    merge = np.stack([B(ua), B(a["w_proj_a"][0]), B(ub), B(a["w_proj_b"][0])], 1).reshape(4 * KC, P, KC * P)
    ada = B(a["w_ada"][0]).reshape(3, 4 * 4, P, KC * P)
    wq = np.concatenate([ada[0], B(qa), B(ka), B(va), ada[1], ada[2],
                         B(fb[:, :512]), B(qb[:, :512]), B(ib[:, :512]), B(ga),
                         B(fb[:, 512:]), B(qb[:, 512:]), B(ib[:, 512:]), B(gb), merge, B(a["w_out"][0])])
    wq = wq.reshape(NQ, 4, P, KC * P).transpose(0, 2, 1, 3).reshape(NQ, P, 4 * KC * P)
    col = lambda x: x.reshape(-1, P).T
    small = np.concatenate([
        rows(np.concatenate([a["c_prompt"], a["c_sample"]])).reshape(P, -1), col(a["b_ada"][0]), col(a["b_gk"][0]),
        col(a["hgrn_lb"]), col(a["gla_norm_w"][0]), col(a["hgrn_norm_w"][0]), col(a["ln1_g"][0]), col(a["ln1_b"][0]),
        col(a["ln2_g"][0]), col(a["ln2_b"][0]), gk.reshape(KC, P, RANK).transpose(1, 0, 2).reshape(P, -1)], 1)
    const, route = constants()
    at, n = ROUTE["bias"]
    route[:, at:at + n] = np.broadcast_to(a["router_bias"][0], (P, NE))
    at, n = ROUTE["w"]
    route[:, at:at + n] = a["w_router"][0].reshape(KC, P, NE).transpose(1, 0, 2).reshape(P, -1)

    def expert(g, u, d):
        gu = np.concatenate([g.reshape(-1, KC, P, FE), u.reshape(-1, KC, P, FE)], 3)
        return np.concatenate([gu.transpose(0, 2, 1, 3).reshape(-1, P, 4096),
                               d.reshape(-1, 2, P, D).transpose(0, 2, 1, 3).reshape(-1, P, 2048)], 2)

    wexp = np.concatenate([expert(a["w_exp_gate"][0], a["w_exp_up"][0], a["w_exp_down"][0]),
                           expert(a["w_sh_gate"], a["w_sh_up"], a["w_sh_down"])])
    st_in = np.concatenate([a["state_gla"][0].transpose(0, 2, 1, 3).reshape(DEC, P, GH * GV),
                            a["state_hgrn"][0].transpose(0, 2, 1, 3).reshape(DEC, P, HH * HV)], 2)
    ins = dict(xT=xT, small=small, wgk2=a["w_gk2"][0], const=const, route=route, wq=wq, wexp=wexp, st_in=st_in)
    ins = {k: np.ascontiguousarray(v) for k, v in ins.items()}

    nc = bacc.Bacc("TRN2", target_bir_lowering=False, num_devices=1)
    aps = {k: nc.dram_tensor(k, v.shape, F32, kind="ExternalInput").ap() for k, v in ins.items()}
    outs = dict(yT=(P, KC * NT), st_prompt=(P, 2048), st_out=(DEC, P, 2048))
    aps.update({k: nc.dram_tensor(k, s, F32, kind="ExternalOutput").ap() for k, s in outs.items()})
    decoder_step(nc, **aps)
    r = run(nc, [ins], core_ids=[0]).results[0]
    y = r["yT"].reshape(P, KC, NT).transpose(2, 1, 0).reshape(NT, D)
    sp, so = r["st_prompt"], r["st_out"]
    gla = lambda s: s[..., :1024].reshape(-1, P, GH, GV).transpose(0, 2, 1, 3)[None]
    hgrn = lambda s: s[..., 1024:].reshape(-1, P, HH, HV).transpose(0, 2, 1, 3)[None]
    c = np.ascontiguousarray
    return (c(y[None, :SEQ]), c(y[SEQ:, None]), c(gla(sp[None])), c(hgrn(sp[None])), c(gla(so)), c(hgrn(so)))
```

```python
from contextlib import ExitStack

import numpy as np
import concourse.bass as bass
from concourse import mybir

P = 128
D = 1024
KC = D // P
SEQ = 512
DEC = 8
NT = SEQ + DEC
HALF = NT // 2
CH = 128
NCH = SEQ // CH
LEV = 7
GH, GV = 4, 256
HH, HV = 8, 128
RANK = 16
NE, NG, TOPG, TOPK = 64, 8, 4, 8
FE = 256
TT = 5
TS = 128
MAXT = 96
TRASH = TT * P
ROWS = TRASH + P
ALPHA = 2.0 ** 0.25
EPS = 1e-5
RSCALE = 2.5
NCOND = 1 + DEC
BIG = 1e30
assert MAXT % 4 == 0 and MAXT >= NT * TOPK // TS + NE - 1 and TS == 1 << 7


F32 = mybir.dt.float32
I32 = mybir.dt.int32
U32 = mybir.dt.uint32
ALU = mybir.AluOpType
ACT = mybir.ActivationFunctionType
AX = mybir.AxisListType.X

Q_ADA = [0, 1, 2, 3, 8, 9, 10, 11, 12, 13, 14, 15]
Q_QA, Q_KA, Q_VA = 4, 5, 6
Q_H = [(18, 17, 16), (23, 22, 21)]
Q_G = [19, 20, 24, 25]
Q_P, Q_O = 26, 34
NQ = 36

def columns(widths):
    at, out = 0, {}
    for name, w in widths:
        out[name] = (at, w)
        at += w
    return out, at

SMALL, NSMALL = columns([("cond", KC * NCOND), ("b_ada", 48), ("b_gk", GH), ("lb", 2 * HH), ("gla_w", 2),
                         ("hgrn_w", 1), ("ln1_g", KC), ("ln1_b", KC), ("ln2_g", KC), ("ln2_b", KC),
                         ("wgk1", KC * RANK)])
CONST, NCONST = columns([("ident", P), ("ones", P), ("mean", P), ("masks", 8 * P), ("reset", NT), ("mhalf", 1), ("eps", 1)])
ROUTE, NROUTE = columns([("tri", P), ("iota", P), ("group", NG), ("quads", MAXT // 4), ("part", 1),
                         ("trash", 1), ("token", TT), ("bias", NE), ("w", KC * NE)])


def constants():
    c = np.zeros((P, NCONST), np.float32)
    def put(table, arr, name, v):
        a, w = table[name]
        arr[:, a:a + w] = v
    j, i = np.arange(P)[:, None], np.arange(P)[None, :]
    put(CONST, c, "ident", np.eye(P))
    put(CONST, c, "ones", 1.0)
    put(CONST, c, "mean", 1.0 / D)
    masks = []
    for l in range(LEV):
        s = CH >> (l + 1)
        masks.append((j // (2 * s) == i // (2 * s)) & (j % (2 * s) < s) & (i % (2 * s) >= s))
    masks.append(j == i)
    put(CONST, c, "masks", np.stack(masks, 1).reshape(P, 8 * P))
    t = np.arange(NT)
    put(CONST, c, "reset", ((t % CH != 0) & (t < SEQ))[None, :])
    put(CONST, c, "mhalf", -0.5)
    put(CONST, c, "eps", EPS)
    r = np.zeros((P, NROUTE), np.float32)
    put(ROUTE, r, "tri", j < i)
    put(ROUTE, r, "iota", i)
    put(ROUTE, r, "group", np.arange(NG)[None, :])
    put(ROUTE, r, "quads", 4 * np.arange(MAXT // 4)[None, :])
    put(ROUTE, r, "part", j)
    put(ROUTE, r, "trash", TRASH + j)
    put(ROUTE, r, "token", j + P * np.arange(TT)[None, :])
    return c, r


def decoder_step(nc, xT, small, wgk2, const, route, wq, wexp, st_in, yT, st_prompt, st_out):
    with ExitStack() as ctx:
        def sb(name, n, dt=F32, p=P):
            return ctx.enter_context(nc.sbuf_tensor(name, [p, n], dt))

        def sem(name):
            return ctx.enter_context(nc.semaphore(name))

        h2rows = nc.dram_tensor("h2rows", [ROWS, D], F32, kind="Internal").ap()
        ffrows = nc.dram_tensor("ffrows", [ROWS, D], F32, kind="Internal").ap()
        etab_d = nc.dram_tensor("etab", [P, 1], F32, kind="Internal").ap()

        W = sb("W", 4 * 4096)
        Xb = sb("Xb", KC * NT)
        Hb = sb("Hb", KC * NT)
        OA = sb("OA", KC * NT)
        OB = sb("OB", KC * NT)
        work = sb("work", 16480)
        cst = sb("cst", NCONST)
        sml = sb("sml", NSMALL)
        side = sb("side", 2 * HALF)
        mod = sb("mod", 48 * NCOND)
        tiny = sb("tiny", 256)
        ints = sb("ints", 256, I32)
        ps = ctx.enter_context(nc.psum_tensor("ps", [P, 8, 512], F32))

        def view(buf, first, n, pattern=None, **kw):
            v = buf[:, first:first + n]
            return v.rearrange(pattern, **kw) if pattern else v

        def C(name):
            a, w = CONST[name]
            return cst[:, a:a + w]

        def S(name):
            a, w = SMALL[name]
            return sml[:, a:a + w]

        ident, ones = C("ident"), C("ones")
        gk2 = side[0:RANK, 0:GH * P]
        gb = side[:, :].rearrange("p (b t) -> p b t", b=2)
        ring = W[:, :].rearrange("p (s u c m) -> p s u c m", s=4, u=4, c=KC)
        X = Xb[:, :].rearrange("p (c t) -> p c t", c=KC)
        H = Hb[:, :].rearrange("p (c t) -> p c t", c=KC)
        oa = OA[:, :].rearrange("p (c t) -> p c t", c=KC)
        ob = OB[:, :].rearrange("p (c t) -> p c t", c=KC)
        md = mod[:, :].rearrange("p (e n) -> p e n", n=NCOND)
        SH1, SC1, G1, SH2, SC2, G2 = range(0, 48, 8)
        conds = S("cond").rearrange("p (c n) -> p c n", c=KC)
        V = view(work, 0, 4096, "p (t n) -> p t n", t=NCH)
        Qb, Kb, Gb = (view(work, 4096 + k * 4 * NT, 4 * NT) for k in range(3))
        q4, k4, g4 = (v.rearrange("p (h t) -> p h t", h=4) for v in (Qb, Kb, Gb))
        M = view(work, 10336, 5120, "p (b l t) -> p b l t", b=2, l=10)
        state = view(work, 15456, 768, "p (b v) -> p b v", b=3)
        Vs = Xb[0:DEC, 0:2048]
        sq_, sk_, sa_ = (view(Xb, 2048 + 96 * k, 96, "p (h b) -> p h b", b=DEC) for k in range(3))
        Pm = view(Xb, 2336, 1024)
        ST = view(Xb, 3360, 256, "p (b t) -> p b t", b=2)
        kdT = view(Xb, 3616, 256, "p (b t) -> p b t", b=2)
        gkl = Xb[0:RANK, 3640:3640 + NT]
        on = (view(work, 16224, 256), view(Xb, 3872, 256))
        gdec = view(tiny, 64, 16 * DEC, "p (j b) -> p j b", b=DEC)
        elast = view(tiny, 0, 4, "p (b c) -> p b c", b=2)
        ssum = view(tiny, 4, 2)
        rstd = view(tiny, 6, 2)
        lbt = view(tiny, 16, 8)
        omlb = view(tiny, 24, 8)
        halfw = view(tiny, 8, 3)
        lbx = view(tiny, 40, 16, "p (r h) -> p r h", r=2)
        lbm = view(tiny, 56, 8)

        s_small, s_x, s_x2, s_route = sem("small_loaded"), sem("x_loaded"), sem("x_again"), sem("route_loaded")
        s_w = [sem(f"quad_loaded_{k}") for k in range(4)]
        s_wfree = sem("quad_used")
        s_cs = sem("cond_silu")
        s_mr, s_mt = sem("mod_rows_copied"), sem("mod_rows_turned")
        s_md, s_mod, s_h = sem("modulation"), sem("sample_sums"), sem("h_ready")
        s_z, s_zev = sem("proj_done"), sem("proj_taken")
        s_lb = sem("lb_steps")
        s_gk = sem("gk_steps")
        s_kf, s_fk = sem("forget_ready"), sem("hgrn_k_ready")
        s_in, s_cum = sem("gates_in"), sem("cumsum_done")
        s_D, s_E, s_Mq, s_Mk = sem("diff_done"), sem("exp_done"), sem("mq_done"), sem("mk_done")
        s_kdt, s_kdc = sem("kd_transposed"), sem("kd_copied")
        s_sc, s_pm, s_st = sem("scores_done"), sem("scores_masked"), sem("scores_summed")
        s_o, s_ss, s_rs, s_rstd = sem("o_done"), sem("o_squares"), sem("o_ms"), sem("o_rstd")
        s_on, s_ot, s_oc = sem("o_scaled"), sem("o_transposed"), sem("o_copied")
        s_u, s_state, s_sout = sem("update_done"), sem("state_done"), sem("state_stored")
        s_rec = sem("group_done")
        s_smp = sem("sample_saved")
        paced = {e: sem(f"paced_{e}") for e in ("sp", "pe", "act", "dve", "pool")}

        def gate(eng, name, s, value):
            eng.wait_ge(s, value)
            eng.sem_inc(paced[name], 1)

        s_si = [sem(f"state_loaded_{b}") for b in range(4)]
        s_so = [sem("sout0"), sem("sout1")]
        s_vb, s_sa, s_sn, s_sop = sem("v_bcast"), sem("s_scaled"), sem("s_new"), sem("s_o")
        s_sn2 = sem("sample_norm")
        s_g1, s_g2, s_g3, s_g5 = sem("gate_proj"), sem("gate_tanh"), sem("gate_value"), sem("gate_applied")
        s_hw = sem("half_weights")
        s_p1, s_p2, s_p3, s_p3a = sem("merge_proj"), sem("merge_act"), sem("merged"), sem("merge_parts")
        s_o1, s_o2 = sem("out_proj"), sem("resid")
        s_ln = sem("ln_steps")
        s_lnp = sem("ln_sums")
        s_lna = sem("ln_squares")
        s_lng, s_laf = sem("deviation"), sem("ln_affine")
        s_r1, s_r2, s_rv = sem("router_proj"), sem("router_sigmoid"), sem("route_steps")
        s_rp = sem("route_counts")
        s_ab, s_abq, s_abp = sem("tile_onehots"), sem("slot_onehots"), sem("onehots_used")
        s_slots, s_eti = sem("slots_ready"), sem("tile_experts")
        s_row, s_et, s_T = sem("etab_stored"), sem("etab_back"), sem("etab_ready")
        s_ht, s_hc, s_hd = sem("h2_transposed"), sem("h2_copied"), [sem("h2_stored_0"), sem("h2_stored_1")]
        s_zero, s_hz = sem("zeroed"), sem("zeros_stored")
        s_shw, s_shd = sem("shared_gu"), sem("shared_down")
        s_gu = [sem(f"gu_loaded_{k}") for k in range(4)]
        s_dn = [sem(f"dn_loaded_{k}") for k in range(4)]
        s_ic, s_gc, s_xt, s_xc = sem("idx_col"), sem("gate_col"), sem("x_transposed"), sem("x_copied")
        s_hh, s_sg, s_a, s_at, s_ac = sem("hidden"), sem("hidden_silu"), sem("act_ready"), sem("act_transposed"), sem("act_copied")
        s_y, s_yc, s_add = sem("y_done"), sem("y_copied"), sem("y_added")
        s_ga = [sem(f"gathered_{b}") for b in range(4)]
        t_hh, t_sg, t_a = sem("sh_hidden"), sem("sh_factors"), sem("sh_act")
        t_y, t_yc, t_st = sem("sh_y"), sem("sh_y_copied"), [sem("sh_stored_0"), sem("sh_stored_1")]
        s_f1 = [sem(f"ff_loaded_{t}") for t in range(TT)]
        s_f2, s_f3, s_f4 = sem("ff_transposed"), sem("ff_resid"), sem("y_stored")
        s_fx, s_fy, s_msk = sem("x_scaled"), sem("decode_resid"), sem("mask_ready")

        block = ctx.enter_context(nc.Block())

        R0 = KC * NT - NROUTE - 8
        assert R0 > 2900
        rt = view(OB, R0, NROUTE)

        def R(name):
            a, w = ROUTE[name]
            return rt[:, a:a + w]

        scores = view(OB, 0, TT * NE, "p (t e) -> p t e", t=TT)
        biased = view(OB, 320, TT * NE, "p (t e) -> p t e", t=TT)
        msk = view(OB, 640, TT * NE, "p (t e) -> p t e", t=TT)
        pos = view(OB, 960, TT * NE, "p (t e) -> p t e", t=TT)
        gates = view(OB, 1280, TT * NE, "p (t e) -> p t e", t=TT)
        tmp = view(OB, 1600, TT * NE, "p (t e) -> p t e", t=TT)
        g8 = view(OB, 1920, TT * NG * 8, "p (t g k) -> p t g k", t=TT, g=NG)
        grp = view(OB, 2240, TT * NG, "p (t g) -> p t g", t=TT)
        gm = view(OB, 2280, TT * NG, "p (t g) -> p t g", t=TT)
        top = view(OB, 2320, TT * 8, "p (t k) -> p t k", t=TT)
        idxf = view(OB, 2360, TT * 8, "p (t k) -> p t k", t=TT)
        posk = view(OB, 2400, TT * 8, "p (t k) -> p t k", t=TT)
        gk = view(OB, 2440, TT * 8, "p (t k) -> p t k", t=TT)
        tilek = view(OB, 2480, TT * 8, "p (t k) -> p t k", t=TT)
        slotk = view(OB, 2520, TT * 8, "p (t k) -> p t k", t=TT)
        cnt = view(OB, 2560, NE)
        nti = view(OB, 2624, NE)
        incl = view(OB, 2688, NE)
        excl = view(OB, 2752, NE)
        cmp_ = view(OB, 2816, NE)
        gsum = view(tiny, 32, TT)
        ecol = view(tiny, 37, 1)
        erow = tiny[0:1, 64:64 + MAXT + 4]
        ui = ints[:, 0:TT * 8].bitcast(U32).rearrange("p (t k) -> p t k", t=TT)
        posi = ints[:, 40:80]
        hi_i = ints[:, 80:120]
        idxt = view(OB, 2880, MAXT + 4)
        assert 2880 + MAXT + 4 <= R0
        quadn = tiny[:, 180:181]
        oh = view(work, 0, TT * 8 * NE, "p (t k e) -> p t k e", t=TT, k=8)
        prod = view(work, 2560, TT * 8 * NE, "p (t k e) -> p t k e", t=TT, k=8)
        Aoh = view(work, 5120, 4 * TS, "p (b s) -> p b s", b=4)
        Boh = view(work, 14336, 4 * 3 * MAXT, "p (b c t) -> p b c t", b=4, c=3)
        hrow = view(work, 6400, 2 * D, "p (b d) -> p b d", b=2)
        zrow = view(work, 8448, D)
        assert 8448 + D <= 10240
        WD = view(work, 0, 8192, "p (s f d) -> p s f d", s=4, f=2)
        GU = W[:, :].rearrange("p (s c f) -> p s c f", s=4, c=KC)
        xg = [view(work, 8192, D), view(work, 9216, D), view(OB, 0, D), view(OB, D, D)]
        xe = view(work, 10240, 2 * KC * TS, "p (b c n) -> p b c n", b=2, c=KC)
        yb = view(work, 12288, 2048, "p (b d) -> p b d", b=2)
        av = view(work, 14336, 512, "p (b f) -> p b f", b=2)
        aT = view(work, 14848, 512, "p (b f n) -> p b f n", b=2, f=2)
        sg = view(work, 15360, 512, "p (b f) -> p b f", b=2)
        shT = view(work, 10240, 2 * NT, "p (f t) -> p f t", f=2)
        shg = view(work, 11280, 2 * HALF, "p (k t) -> p k t", k=2)
        idx_i = view(work, 15872, MAXT + 4).bitcast(I32)
        gtabs = view(work, 15984, MAXT + 4)
        eti = work[0:1, 16096:16096 + MAXT + 4].bitcast(I32)
        qni = view(work, 16208, 1).bitcast(I32)
        idg = view(work, 16212, 4).bitcast(I32)
        ida = view(work, 16216, 4).bitcast(I32)
        gcol = view(work, 16220, 4)

        LSQ = view(work, 0, KC * NT, "p (c t) -> p c t", c=KC)
        lnr = view(work, 4160, 2 * NT)
        mg = [view(work, at, KC * HALF, "p (c t) -> p c t", c=KC) for at in (13840, 6000)]
        gtmp = view(work, 12800, 4 * HALF, "p (b t) -> p b t", b=4)
        sin = view(work, 0, 8192, "p (b n) -> p b n", b=4)
        snew = view(work, 8192, 4096, "p (b n) -> p b n", b=2)
        oS = view(work, 12288, 128, "p (j b) -> p j b", b=DEC)
        oS2 = view(work, 12416, 128, "p (j b) -> p j b", b=DEC)
        oms = view(work, 12544, 128, "p (j b) -> p j b", b=DEC)

        GROUPS = [dict(heads=GH, v=GV, out=oa, first=0, kind="gla", qs=Q_QA, fs=Q_KA),
                  dict(heads=4, v=HV, out=ob, first=0, kind="hgrn", qs=Q_H[0][1], fs=Q_H[0][2]),
                  dict(heads=4, v=HV, out=ob, first=4, kind="hgrn", qs=Q_H[1][1], fs=Q_H[1][2])]
        halves = [(0, HALF), (HALF, NT)]

        def z_items():
            out = []
            for gi in range(3):
                def heads(what):
                    return [(gi, what, h, hf) for h in range(4) for hf in range(2)]

                if gi == 0:
                    out += [(gi, "gl", 0, hf) for hf in range(2)] + heads("g") + heads("q") + heads("k")
                else:
                    out += heads("k") + heads("q")
                for b in range(2 if gi == 0 else 1):
                    out += [(gi, "v", b, t) for t in range(TT)]
            return out

        ITEMS = z_items()


        def rows_stored(eng):
            eng.wait_ge(s_hd[0], 48)
            eng.wait_ge(s_hd[1], 32)
            eng.wait_ge(s_hz, 32)

        def used(q):
            if q in Q_ADA:
                return s_wfree, Q_ADA.index(q) + 1
            if q in Q_G:
                return s_g1, 1 + max(n for n, u in enumerate(UNITS) if u[0] == q)
            if q < Q_P:
                n, last = 0, 0
                for gi, what, a, b in ITEMS:
                    n += 1
                    own = {"v": (Q_VA + a) if gi == 0 else Q_H[gi - 1][0], "q": GROUPS[gi]["qs"],
                           "k": GROUPS[gi]["fs"]}.get(what)
                    if own == q:
                        last = n
                return s_z, last
            if q < Q_O:
                return s_p1, 4 * (1 + max(n for n, (m, hf) in enumerate(MERGE) if m == q - Q_P))
            return s_o1, 8 * (q - Q_O + 1)

        def taken(gi, what):
            return 1 + max(n for n, it in enumerate(ITEMS) if it[:2] == (gi, what))

        def since(eng, s, value):
            if value > 0:
                eng.wait_ge(s, value)

        UNITS = [(Q_G[m // 4], m, hf, False) for m in range(8) for hf in range(2)]
        for c in range(16):
            m, hf = c // 4, c % 2
            UNITS.append((Q_G[2], m, hf, False) if c % 4 >= 2 else (Q_G[3], 4 + m, hf, True))

        def gate_unit(n):
            q, m, hf, before = UNITS[n]
            lo, hi = halves[hf]
            return q, m, lo, min(hi, SEQ), (7, 5)[n % 2]

        def mod_rows(n):
            return view(work, 512 * n, 512)[0:NCOND, :] if n < 4 else side[0:NCOND, 0:512]

        def mod_bank(n):
            return 6 + n % 2 if n < 4 else 7

        MERGE = [(m, 0) for m in range(4)] + [(m, 1) for m in range(4)] + [(m, hf) for m in range(4, KC) for hf in range(2)]
        decode = [("B", 0)] + [x for b in range(1, DEC) for x in (("B", b), ("A", b - 1))] + [("A", DEC - 1)]
        ORDER = []
        for k in range(12):
            ORDER.append(("P", k))
            for _ in range(2 if k % 3 == 0 else 1):
                ORDER.append(decode.pop(0))
        ORDER += [("N1", 0), ("P", 12), ("S", 0), ("N2", 0)] + [("P", k) for k in range(13, 4 * len(MERGE))]
        assert not decode

        FILL = [[("mod", 8 + c) for c in range(16)], [("gate", c) for c in range(16)], [("gate", 16 + c) for c in range(16)]]

        LN0, LN1 = 0, 24

        def mean_pe(pe, c, hf):
            lo, hi = halves[hf]
            mm = pe.matmul(ps[:, 2 + hf, 0:HALF], C("mean"), X[:, c, lo:hi], start=(c == 0), stop=(c == KC - 1))
            if c == KC - 1:
                mm.then_inc(s_lnp, 1)

        def variance_pe(pe, which):
            for hf, (lo, hi) in enumerate(halves):
                pe.wait_ge(s_lna, 2 * which + hf + 1)
                for c in range(KC):
                    mm = pe.matmul(ps[:, 4 + hf, 0:HALF], C("mean"), LSQ[:, c, lo:hi], start=(c == 0), stop=(c == KC - 1))
                mm.then_inc(s_lnp, 1)

        def recurrence_pe(pe, gi, fill, last):
            v, base = GROUPS[gi]["v"], 16 * gi

            def scores_of(n):
                pair, p, c, h, cc = n // 2, n // 2 % 2, n % 2, n // 4 % 4, n % 4
                col_ = slice(c * CH, (c + 1) * CH)
                pe.wait_ge(s_Mk, pair + 1)
                pe.wait_ge(s_Mq, pair + 1)
                since(pe, s_kdc, n)
                pe.transpose(ps[:, 2, 0:CH], M[:, p, 7, col_], ident).then_inc(s_kdt, 1)
                since(pe, s_pm, n)
                for l in range(LEV):
                    pe.matmul(ps[:, l // 4, (l % 4) * CH:(l % 4 + 1) * CH], M[:, p, l, col_], M[:, p, l, col_],
                              start=True, stop=True)
                pe.matmul(ps[:, 1, 3 * CH:4 * CH], M[:, p, 9, col_], q4[:, h, cc * CH:(cc + 1) * CH],
                          start=True, stop=True).then_inc(s_sc, 1)

            def values(n):
                return V[:, n % 4, n // 4 % 4 * v:(n // 4 % 4 + 1) * v]

            def update(n):
                pe.wait_ge(s_kdc, n + 1)
                since(pe, s_state, n)
                pe.matmul(ps[:, 3, 0:v], kdT[:, n % 2, :], values(n), start=True, stop=True).then_inc(s_u, 1)

            def output(n):
                o = ps[:, 4, 0:v]
                pe.wait_ge(s_st, n + 1)
                since(pe, s_on, n)
                mm = pe.matmul(o, ST[:, n % 2, :], values(n), start=True, stop=(n % 4 == 0))
                if n % 4:
                    pe.wait_ge(s_state, n)
                    mm = pe.matmul(o, M[:, n // 2 % 2, 8, n % 2 * CH:(n % 2 + 1) * CH], state[:, n % 4 % 2, 0:v],
                                   start=False, stop=True)
                mm.then_inc(s_o, 1)

            def turn(n):
                pe.wait_ge(s_on, n + 1)
                since(pe, s_oc, n)
                for j in range(v // P):
                    mm = pe.transpose(ps[:, 6, j * P:(j + 1) * P], on[n % 2][:, j * P:(j + 1) * P], ident)
                mm.then_inc(s_ot, 1)

            pe.wait_ge(s_zev, taken(gi, "v"))
            scores_of(base)
            for c in range(17):
                if c < 16:
                    update(base + c)
                    fill(*FILL[gi][c])
                if c + 1 < 16:
                    scores_of(base + c + 1)
                if c < 16:
                    output(base + c)
                if c:
                    turn(base + c - 1)
            if gi == 0:
                last()

        def layer_norm_act(act, which):
            base = (LN0, LN1)[which]
            g, b = S(f"ln{which + 1}_g"), S(f"ln{which + 1}_b")
            for hf, (lo, hi) in enumerate(halves):
                act.wait_ge(s_ln, base + 1 + hf)
                act.activation(LSQ[:, :, lo:hi], X[:, :, lo:hi], ACT.Square).then_inc(s_lna, 1)
            for hf, (lo, hi) in enumerate(halves):
                act.wait_ge(s_lnp, 4 * which + hf + 3)
                act.activation(lnr[:, lo:hi], ps[:, 4 + hf, 0:HALF], ACT.Sqrt, bias=C("eps")).then_inc(s_lng, 1)
            act.wait_ge(s_ln, base + 4)
            for c in range(KC):
                act.activation(X[:, c, 0:HALF], X[:, c, 0:HALF], ACT.Identity, scale=g[:, c:c + 1],
                               bias=b[:, c:c + 1]).then_inc(s_laf, 1)

        def gate_tanh(act, n):
            q, m, lo, hi, bank = gate_unit(n)
            act.wait_ge(s_g1, n + 1)
            since(act, s_g5, min(n - 1, 16))
            since(act, s_g3, n - 1)
            act.activation(gb[:, n % 2, :], ps[:, bank, 0:HALF], ACT.Tanh, scale=0.5).then_inc(s_g2, 1)

        def gate_value(dve, n):
            q, m, lo, hi, bank = gate_unit(n)
            g, half, before = gb[:, n % 2, :], UNITS[n][2], UNITS[n][3]
            dve.wait_ge(s_g2, n + 1)
            if n < 16:
                dve.scalar_tensor_tensor(out=g, in0=g, scalar=1.0, in1=ps[:, bank, 0:HALF],
                                         op0=ALU.add, op1=ALU.mult).then_inc(s_g3, 1)
                return
            o = ob[:, m, lo:hi]
            if half:
                dve.tensor_scalar(gdec[:, 8 + m, :], g[:, hi - lo:HALF], 1.0, None, ALU.add)
            if before:
                dve.tensor_scalar(o, g[:, 0:hi - lo], 1.0, None, ALU.add).then_inc(s_g3, 1)
            else:
                dve.scalar_tensor_tensor(out=o, in0=g[:, 0:hi - lo], scalar=1.0, in1=o, op0=ALU.add, op1=ALU.mult).then_inc(s_g3, 1)

        def gate_apply(pool, n):
            q, m, lo, hi, bank = gate_unit(n)
            o, g = oa[:, m, lo:hi], gb[:, n % 2, :]
            pool.wait_ge(s_g3, n + 1)
            if UNITS[n][2]:
                pool.tensor_copy(gdec[:, m, :], g[:, hi - lo:HALF])
            pool.tensor_tensor(o, o, g[:, 0:hi - lo], ALU.mult).then_inc(s_g5, 1)

        def filled(gi, c):
            what, n = FILL[gi][c]
            return n if what == "gate" else None

        def src(buf, pair):
            return buf[:, pair // 2 % 4, pair % 2 * 256:(pair % 2 + 1) * 256]

        def decays(act, pair):
            p = pair % 2
            act.wait_ge(s_D, pair + 1)
            act.activation(M[:, p, 0:8, :], M[:, p, 0:8, :], ACT.Abs).then_inc(s_E, 1)
            act.wait_ge(s_E, 5 * pair + 1)
            act.activation(M[:, p, 0:8, :], M[:, p, 0:8, :], ACT.Exp, scale=-1.0).then_inc(s_E, 1)

        def factors(act, pair):
            p = pair % 2
            since(act, s_o, 2 * pair - 2)
            act.activation(M[:, p, 8, :], src(g4, pair), ACT.Exp).then_inc(s_E, 1)
            act.activation(M[:, p, 9, :], src(k4, pair), ACT.Copy).then_inc(s_E, 1)
            since(act, s_state, 2 * pair - 2)
            act.activation(elast[:, p, :], g4[:, pair // 2 % 4, pair % 2 * 256 + 127:(pair % 2 + 1) * 256:128], ACT.Exp).then_inc(s_E, 1)

        def first_factors(act, gi, k):
            if k == 0:
                act.wait_ge(s_cum, 4 * gi + 4)
                act.activation(sa_[:, 4 * gi:4 * gi + 4, :], g4[:, :, SEQ:NT], ACT.Exp).then_inc(s_smp, 1)
                since(act, s_fk, 2 * gi)
            decays(act, 8 * gi + k)
            factors(act, 8 * gi + k)

        def recurrence_act(act, gi, copy_rows):
            v, base = GROUPS[gi]["v"], 16 * gi

            def copy_kd(n):
                act.wait_ge(s_kdt, n + 1)
                since(act, s_u, n - 1)
                act.activation(kdT[:, n % 2, :], ps[:, 2, 0:CH], ACT.Copy).then_inc(s_kdc, 1)

            def square(n):
                act.wait_ge(s_o, n + 1)
                since(act, s_ot, n - 1)
                act.activation(on[n % 2][:, 0:v], ps[:, 4, 0:v], ACT.Square,
                               accum_out=ssum[:, n % 2:n % 2 + 1]).then_inc(s_ss, 1)

            def scale(n):
                act.wait_ge(s_rstd, n + 1)
                act.activation(on[n % 2][:, 0:v], ps[:, 4, 0:v], ACT.Copy,
                               scale=rstd[:, n % 2:n % 2 + 1]).then_inc(s_on, 1)

            def store_state(head):
                act.wait_ge(s_state, 4 * head + 4)
                at = (0, 1024, 1536)[gi] + head % 4 * v
                act.dma_start(st_prompt[:, at:at + v], state[:, 2, 0:v]).then_inc(s_sout, 16)

            copy_kd(base)
            for c in range(17):
                even = c % 2 == 0 and 2 <= c <= 12
                if gi == 0 and c % 2 == 0 and c:
                    copy_rows(3 + c // 2)
                if c:
                    square(base + c - 1)
                if c and gi:
                    gate_tanh(act, filled(gi, c - 1))
                if c:
                    scale(base + c - 1)
                if even:
                    decays(act, 8 * gi + c // 2 + 1)
                if c + 1 < 16:
                    copy_kd(base + c + 1)
                if even:
                    factors(act, 8 * gi + c // 2 + 1)
                if c in (5, 9, 13):
                    store_state(4 * gi + (c - 5) // 4)
            store_state(4 * gi + 3)

        def layer_norm_dve(dve, which):
            base = (LN0, LN1)[which]
            g, b = S(f"ln{which + 1}_g"), S(f"ln{which + 1}_b")

            def wide(v):
                return v.rearrange("p (a t) -> p a t", a=1).broadcast_to([P, KC, v.shape[1]])

            for hf, (lo, hi) in enumerate(halves):
                dve.wait_ge(s_lnp, 4 * which + hf + 1)
                dve.tensor_tensor(X[:, :, lo:hi], X[:, :, lo:hi], wide(ps[:, 2 + hf, 0:HALF]), ALU.subtract).then_inc(s_ln, 1)
            for hf, (lo, hi) in enumerate(halves):
                dve.wait_ge(s_lng, 2 + 2 * which + hf)
                dve.reciprocal(lnr[:, NT + lo:NT + hi], lnr[:, lo:hi]).then_inc(s_ln, 1)
                dve.wait_ge(s_ln, base + 3 + 2 * hf)
                dve.tensor_tensor(X[:, :, lo:hi], X[:, :, lo:hi], wide(lnr[:, NT + lo:NT + hi]), ALU.mult).then_inc(s_ln, 1)
            dve.wait_ge(s_ln, base + 6)
            for c in range(KC):
                dve.tensor_scalar(X[:, c, HALF:NT], X[:, c, HALF:NT], g[:, c:c + 1], b[:, c:c + 1], ALU.mult, ALU.add).then_inc(s_ln, 1)
            dve.wait_ge(s_ln, base + 14)
            dve.wait_ge(s_laf, 8 * which + 8)

        @block.sync
        def _(sp):
            sp.dma_start(sml[:, :], small).then_inc(s_small, 16)
            sp.dma_start(cst[:, :], const).then_inc(s_small, 16)
            sp.dma_start(gk2[:, :], wgk2).then_inc(s_small, 16)

            def load(q, slot):
                return sp.dma_start(W[:, slot * 4096:(slot + 1) * 4096], wq[q])

            for q in range(4):
                load(q, q).then_inc(s_w[q], 16)
            sp.dma_start(Xb[:, :], xT).then_inc(s_x, 16)

            def stream(a, b):
                for q in range(a, b):
                    sp.wait_ge(*used(q - 4))
                    load(q, q % 4).then_inc(s_w[q % 4], 16)

            stream(4, 28)
            sp.wait_ge(s_rec, 3)
            for b in range(4):
                sp.dma_start(sin[:, b, :], st_in[b]).then_inc(s_si[b], 16)
            stream(28, 30)
            for b in range(DEC):
                sp.wait_ge(s_sn, 12 * (b + 1))
                if b + 4 < DEC:
                    sp.dma_start(sin[:, b % 4, :], st_in[b + 4]).then_inc(s_si[b % 4], 16)
                sp.dma_start(st_out[b], snew[:, b % 2, :]).then_inc(s_so[b % 2], 16)
            for b in range(2):
                sp.wait_ge(s_so[b], 64)
            sp.wait_ge(s_sn2, 6)
            sp.dma_start(Xb[:, :], xT).then_inc(s_x2, 16)
            stream(30, NQ)
            sp.wait_ge(s_p1, 64)
            sp.dma_start(rt, route).then_inc(s_route, 16)
            sp.wait_ge(*used(NQ - 1))
            sp.dma_start(W[:, 3 * 4096:4 * 4096], wexp[NE, :, 0:4096]).then_inc(s_shw, 16)
            sp.wait_ge(s_zero, 1)
            sp.dma_start(h2rows[TRASH:ROWS, :], zrow).then_inc(s_hz, 16)
            sp.dma_start(h2rows[NT:TRASH, :], zrow[0:TRASH - NT, :]).then_inc(s_hz, 16)
            for t in range(TT):
                n = min(P, NT - t * P)
                sp.wait_ge(s_hc, 2 * t + 2)
                sp.dma_start(h2rows[t * P:t * P + n, :], hrow[0:n, t % 2, :]).then_inc(s_hd[t % 2], 16)
            rows_stored(sp)
            sp.dma_start(work[:, 3 * 2048:4 * 2048], wexp[NE, :, 4096:6144]).then_inc(s_shd, 16)
            sp.wait_ge(s_row, 1)
            sp.dma_start(etab_d, ecol).then_inc(s_et, 16)
            sp.wait_ge(s_et, 16)
            sp.dma_start(erow, etab_d[0:MAXT + 4, :].rearrange("t a -> a t")).then_inc(s_et, 16)

            def load_tile(t, slot, what, sems):
                lo, hi = (0, 4096) if what == "gu" else (4096, 6144)
                at = slice(t, t + 1) if isinstance(t, int) else bass.ds(t, 1)
                e = sp.value_load(eti[0:1, at], min_val=0, max_val=NE - 1)
                dst = W if what == "gu" else work
                w = hi - lo
                sp.dma_start(dst[:, slot * w:(slot + 1) * w],
                             wexp[bass.ds(e, 1), :, lo:hi].rearrange("a p n -> (a p) n")).then_inc(sems[slot], 16)

            sp.wait_ge(s_T, 1)
            nq = sp.value_load(qni[0:1, 0:1], min_val=1, max_val=MAXT // 4)
            sp.wait_ge(s_eti, 1)
            for t in range(3):
                load_tile(t, t, "gu", s_gu)
            for t in range(TT):
                n = min(P, NT - t * P)
                sp.wait_ge(t_yc, 2 * t + 2)
                sp.dma_start(ffrows[t * P:t * P + n, :], yb[0:n, t % 2, :]).then_inc(t_st[t % 2], 16)
            sp.wait_ge(s_ga[0], 16)
            sp.wait_ge(s_abp, 40)
            for k in range(4):
                if k >= 2:
                    if k == 3:
                        sp.wait_ge(s_hh, 5)
                        sp.wait_ge(t_y, 2 * TT)
                    if k == 2:
                        sp.wait_ge(t_hh, 4)
                    load_tile(k + 1, (k + 1) % 4, "gu", s_gu)
                load_tile(k, k, "dn", s_dn)
            with sp.Fori(1, nq) as i:
                for k in range(4):
                    gate(sp, "sp", s_hh, i * 4 + (k + 2))
                    load_tile(i * 4 + (k + 1), (k + 1) % 4, "gu", s_gu)
                    gate(sp, "sp", s_y, i * 8 + (2 * k + 2))
                    load_tile(i * 4 + k, k, "dn", s_dn)
            gate(sp, "sp", s_add, nq * 64 + 32)
            for t in range(TT):
                n = min(P, NT - t * P)
                sp.dma_start(work[0:n, t * D:(t + 1) * D], ffrows[t * P:t * P + n, :]).then_inc(s_f1[t], 16)
            for k, (done, count) in enumerate(((s_laf, 16), (s_ln, LN1 + 14))):
                lo, hi = halves[k]
                sp.wait_ge(done, count)
                sp.dma_start(yT.rearrange("p (c t) -> p c t", c=KC)[:, :, lo:hi], X[:, :, lo:hi]).then_inc(s_f4, 16)
            sp.wait_ge(s_f4, 32)
            sp.wait_ge(s_sout, 192)

        @block.tensor
        def _(pe):
            pe.wait_ge(s_small, 48)
            pe.wait_ge(s_cs, 1)
            def quad_ready(q):
                pe.wait_ge(s_w[q % 4], 16 * (q // 4 + 1))

            def mod_proj(n, chunks):
                q = Q_ADA[n]
                quad_ready(q)
                if 0 in chunks:
                    since(pe, s_mr, n - 1 if n < 4 else n)
                for c in chunks:
                    mm = pe.matmul(ps[0:NCOND, mod_bank(n), :], conds[:, c, :], ring[:, q % 4, :, c, :],
                                   start=(c == 0), stop=(c == KC - 1))
                if c == KC - 1:
                    mm.then_inc(s_wfree, 1)

            def mod_turn(n):
                pe.wait_ge(s_mr, n + 1)
                for u in range(4):
                    at = (4 * n + u) * NCOND
                    mm = pe.transpose(ps[:, 5, at:at + NCOND], mod_rows(n)[:, u * P:(u + 1) * P], ident[0:NCOND, 0:NCOND])
                mm.then_inc(s_mt, 1)

            for n in range(4):
                mod_proj(n, range(KC))
                if n:
                    mod_turn(n - 1)
            mod_turn(3)
            pe.wait_ge(s_h, 9)

            def gate_proj(n):
                q, m, lo, hi, bank = gate_unit(n)
                quad_ready(q)
                if n == 0:
                    pe.wait_ge(s_md, 4)
                since(pe, s_g3, n - 1)
                for c in range(KC):
                    mm = pe.matmul(ps[:, bank, 0:HALF], ring[:, q % 4, m % 4, c, :], H[:, c, lo:lo + HALF],
                                   start=(c == 0), stop=(c == KC - 1))
                mm.then_inc(s_g1, 1)

            def fill(what, n):
                if what == "mod":
                    half = n % 2
                    if n > 8 and not half:
                        mod_turn(n // 2 - 1)
                    mod_proj(n // 2, range(4 * half, 4 * half + 4))
                else:
                    gate_proj(n)

            n = 0
            for gi, what, a, b in ITEMS:
                g = GROUPS[gi]
                if gi and n == taken(gi - 1, "v"):
                    recurrence_pe(pe, gi - 1, fill, lambda: mod_turn(11))
                    pe.wait_ge(s_pm, 16 * gi)
                bank = n % 2
                if n >= 2:
                    pe.wait_ge(s_zev, n - 1)
                if what == "v":
                    q = (Q_VA + a) if gi == 0 else Q_H[gi - 1][0]
                    rows = min(P, NT - b * P)
                    quad_ready(q)
                    for c in range(KC):
                        mm = pe.matmul(ps[0:rows, bank, :], H[:, c, b * P:b * P + rows], ring[:, q % 4, :, c, :],
                                       start=(c == 0), stop=(c == KC - 1))
                elif what == "gl":
                    w = S("wgk1").rearrange("p (c r) -> p c r", c=KC)
                    for c in range(KC):
                        mm = pe.matmul(ps[0:RANK, bank, 0:HALF], w[:, c, :], H[:, c, halves[b][0]:halves[b][1]],
                                       start=(c == 0), stop=(c == KC - 1))
                elif what == "g":
                    pe.wait_ge(s_zev, 2)
                    mm = pe.matmul(ps[:, bank, 0:HALF], gk2[:, a * P:(a + 1) * P], gkl[:, halves[b][0]:halves[b][1]],
                                   start=True, stop=True)
                else:
                    q = g["qs"] if what == "q" else g["fs"]
                    quad_ready(q)
                    for c in range(KC):
                        mm = pe.matmul(ps[:, bank, 0:HALF], ring[:, q % 4, a, c, :],
                                       H[:, c, halves[b][0]:halves[b][1]], start=(c == 0), stop=(c == KC - 1))
                mm.then_inc(s_z, 1)
                n += 1
            recurrence_pe(pe, 2, fill, None)
            pe.wait_ge(s_zev, len(ITEMS))
            pe.wait_ge(s_oc, 48)
            def answers(b):
                pe.wait_ge(s_sn, 12 * (b + 1))
                for j in range(16):
                    h = j // 2 if j < 8 else j - 4
                    mm = pe.matmul(ps[:, 4, DEC * j + b:DEC * j + b + 1], snew[:, b % 2, j * P:(j + 1) * P],
                                   sq_[:, h, b:b + 1], start=True, stop=True)
                mm.then_inc(s_sop, 1)

            def spread(b):
                for j in range(4):
                    since(pe, s_sn, 12 * (b - 1) + (2, 4, 8, 12)[j])
                    pe.matmul(ps[:, j, :], ident[0:DEC, b:b + 1].broadcast_to([DEC, P]), Vs[:, j * 512:(j + 1) * 512],
                              start=True, stop=True).then_inc(s_vb, 1)

            def product(k):
                n, u = k // 4, k % 4
                m, hf = MERGE[n]
                lo, hi = halves[hf]
                quad_ready(Q_P + m)
                if hf:
                    pe.wait_ge(s_sn2, 6)
                if k >= 3:
                    last = k - 3
                    pe.wait_ge(s_p3a if last % 2 else s_p2, last // 2 + 1)
                for c in range(KC):
                    mm = pe.matmul(ps[:, 5 + k % 3, 0:HALF], ring[:, (Q_P + m) % 4, u, c, :], (H, oa, H, ob)[u][:, c, lo:hi],
                                   start=(c == 0), stop=(c == KC - 1))
                mm.then_inc(s_p1, 1)

            pe.wait_ge(s_g5, 16)
            pe.wait_ge(s_g3, 32)
            for what, k in ORDER:
                if what == "B":
                    spread(k)
                elif what == "A":
                    answers(k)
                elif what == "P":
                    product(k)
                elif what == "S":
                    pe.wait_ge(s_sn2, 2)
                    pe.matmul(ps[:, 4, 128:256], ones, oS2.rearrange("p j b -> p (j b)"), start=True, stop=True).then_inc(s_sop, 1)
            pe.wait_ge(s_p3, 16)
            n = 0
            for q in range(Q_O, NQ):
                quad_ready(q)
                for u in range(4):
                    if n >= 4:
                        pe.wait_ge(s_o2, n - 2)
                        for hf in range(2):
                            mean_pe(pe, n // 2 - 2, hf)
                    for lo, hi in halves:
                        if n >= 2:
                            pe.wait_ge(s_o2, n - 1)
                        for c in range(KC):
                            mm = pe.matmul(ps[:, n % 2, 0:HALF], ring[:, q % 4, u, c, :], mg[n % 2][:, c, :],
                                           start=(c == 0), stop=(c == KC - 1))
                        mm.then_inc(s_o1, 1)
                        n += 1
            for c in (KC - 2, KC - 1):
                pe.wait_ge(s_o2, 2 * c + 2)
                for hf in range(2):
                    mean_pe(pe, c, hf)
            variance_pe(pe, 0)
            pe.wait_ge(s_ln, LN1)

            pe.wait_ge(s_route, 16)
            wr = R("w").rearrange("p (c e) -> p c e", c=KC)
            for t in range(TT):
                rows = min(P, NT - t * P)
                for c in range(KC):
                    mm = pe.matmul(ps[0:rows, 0, t * NE:(t + 1) * NE], H[:, c, t * P:t * P + rows], wr[:, c, :],
                                   start=(c == 0), stop=(c == KC - 1))
            mm.then_inc(s_r1, 1)
            def shared(n):
                f, (lo, hi) = n % 2, halves[n // 2]
                if n >= 2:
                    pe.wait_ge(t_sg, 2 * n - 2)
                for k in range(2):
                    for c in range(KC):
                        mm = pe.matmul(ps[:, (1 + k, 6 + k)[f], 0:HALF], GU[:, 3, c, k * FE + f * P:k * FE + (f + 1) * P], H[:, c, lo:hi],
                                       start=(c == 0), stop=(c == KC - 1))
                mm.then_inc(t_hh, 1)

            pe.wait_ge(s_shw, 16)
            shared(0)
            shared(1)
            pe.wait_ge(s_msk, 1)
            for t in range(TT):
                rows = min(P, NT - t * P)
                pe.matmul(ps[:, 3, 0:NE], ones[0:rows, :], msk[0:rows, t, :], start=(t == 0), stop=(t == TT - 1))
            for t in range(TT):
                rows = min(P, NT - t * P)
                for t2 in range(t + 1):
                    k = P if t2 < t else rows
                    lhs = ones[0:k, 0:rows] if t2 < t else R("tri")[0:k, 0:rows]
                    mm = pe.matmul(ps[0:rows, 4, t * NE:(t + 1) * NE], lhs, msk[0:k, t2, :],
                                   start=(t2 == 0), stop=(t2 == t))
            mm.then_inc(s_rp, 1)
            pe.wait_ge(s_r2, 2)
            for t in range(TT):
                rows = min(P, NT - t * P)
                for hf in range(2):
                    n = 2 * t + hf
                    if n >= 2:
                        pe.wait_ge(s_hc, n - 1)
                    for c in range(4):
                        mm = pe.transpose(ps[0:rows, 5 * (n % 2), c * P:(c + 1) * P],
                                          H[:, 4 * hf + c, t * P:t * P + rows], ident)
                    mm.then_inc(s_ht, 1)
            shared(2)
            shared(3)
            pe.wait_ge(s_hc, 2 * TT)
            def table(n):
                rows = min(P, NT - n // TOPK * P)
                pe.wait_ge(s_ab, 3 * n + 3)
                pe.wait_ge(s_abq, n + 1)
                pe.matmul(ps[0:TS, 5, 0:3 * MAXT], Aoh[0:rows, n % 4, :],
                          Boh[0:rows, n % 4, :, :].rearrange("p c t -> p (c t)"),
                          start=(n == 0), stop=(n == 39)).then_inc(s_abp, 1)

            pe.sem_inc(s_hh, 4)
            pe.sem_inc(s_y, 8)
            pe.sem_inc(s_xt, 8)
            pe.wait_ge(t_a, 4)
            pe.wait_ge(s_shd, 16)
            for t in range(TT):
                rows = min(P, NT - t * P)
                if t >= 2:
                    pe.wait_ge(t_yc, 2 * t - 2)
                for hf in range(2):
                    for f in range(2):
                        mm = pe.matmul(ps[0:rows, (1, 6)[t % 2] + hf, :], shT[:, f, t * P:t * P + rows],
                                       WD[:, 3, f, hf * 512:(hf + 1) * 512], start=(f == 0), stop=(f == 1))
                    mm.then_inc(t_y, 1)
                for n in range(10 * t, min(10 * t + 10, TT * TOPK)):
                    table(n)
            pe.wait_ge(s_T, 2)
            pe.wait_ge(t_yc, 2 * TT)
            nq = pe.value_load(qni[0:1, 0:1], min_val=1, max_val=MAXT // 4)

            def turn(t, k, gathered):
                gate(pe, "pe", s_ga[k % 4], gathered)
                gate(pe, "pe", s_xc, t * 2 + 2)
                for hf in range(2):
                    for c in range(4):
                        mm = pe.transpose(ps[:, 6 + hf, c * P:(c + 1) * P],
                                          xg[k % 4][:, (4 * hf + c) * P:(4 * hf + c + 1) * P], ident)
                    mm.then_inc(s_xt, 1)

            def gate_up(t, k, loaded):
                gate(pe, "pe", s_xc, t * 2 + 4)
                gate(pe, "pe", s_gu[k % 4], loaded)
                gate(pe, "pe", s_a, t + 1)
                for c in range(KC):
                    mm = pe.matmul(ps[:, k % 2, :], xe[:, k % 2, c, :], GU[:, k % 4, c, :],
                                   start=(c == 0), stop=(c == KC - 1))
                mm.then_inc(s_hh, 1)

            turn(0, 0, 16)
            gate_up(0, 0, 16)
            turn(1, 1, 16)
            with pe.Fori(0, nq) as i:
                for k in range(4):
                    t = i * 4 + k
                    gate(pe, "pe", s_a, i * 4 + (k + 3))
                    gate(pe, "pe", s_ac, t + 1)
                    for f in range(2):
                        mm = pe.transpose(ps[:, 2, f * P:(f + 1) * P], av[:, k % 2, f * P:(f + 1) * P], ident)
                    mm.then_inc(s_at, 1)
                    gate_up(i * 4 + (k + 1), k + 1, i * 16 + (16 if k < 3 else 32))
                    turn(i * 4 + (k + 2), (k + 2) % 4, i * 16 + 16 * ((k + 2) // 4 + 1))
                    gate(pe, "pe", s_ac, i * 4 + (k + 2))
                    gate(pe, "pe", s_dn[k], i * 16 + 16)
                    for hf in range(2):
                        gate(pe, "pe", s_yc, i * 8 + (2 * k + hf + 1))
                        for f in range(2):
                            mm = pe.matmul(ps[:, 4 + hf, :], aT[:, k % 2, f, :], WD[:, k, f, hf * 512:(hf + 1) * 512],
                                           start=(f == 0), stop=(f == 1))
                        mm.then_inc(s_y, 1)

            for t in range(TT):
                rows = min(P, NT - t * P)
                pe.wait_ge(s_f1[t], 16)
                for hf in range(2):
                    n = 2 * t + hf
                    if n >= 2:
                        pe.wait_ge(s_f3, n - 1)
                    for c in range(4):
                        mm = pe.transpose(ps[:, n % 2, c * P:c * P + rows],
                                          work[0:rows, t * D + (4 * hf + c) * P:t * D + (4 * hf + c + 1) * P],
                                          ident[0:rows, 0:rows])
                    mm.then_inc(s_f2, 1)
                if t == 3:
                    pe.wait_ge(s_f3, 6)
                    for c in range(KC):
                        mean_pe(pe, c, 0)
            pe.wait_ge(s_f3, 2 * TT)
            for c in range(KC):
                mean_pe(pe, c, 1)
            variance_pe(pe, 1)

        @block.scalar
        def _(act):
            act.wait_ge(s_small, 48)
            act.activation(conds, conds, ACT.Silu).then_inc(s_cs, 1)
            def copy_rows(n):
                act.wait_ge(s_wfree, n + 1)
                if n > 4:
                    act.wait_ge(s_mt, n)
                elif n == 4:
                    act.wait_ge(s_zev, taken(0, "g"))
                    act.wait_ge(s_z, taken(0, "g"))
                act.activation(mod_rows(n), ps[0:NCOND, mod_bank(n), :], ACT.Copy).then_inc(s_mr, 1)

            for n in range(4):
                copy_rows(n)
            act.wait_ge(s_lb, 3)
            act.activation(lbx, lbx, ACT.Exp).then_inc(s_lb, 1)
            n = 0
            for gi, what, a, b in ITEMS:
                g = GROUPS[gi]
                if gi and n == taken(gi - 1, "v"):
                    recurrence_act(act, gi - 1, copy_rows)
                bank = n % 2
                act.wait_ge(s_z, n + 1)
                lo, hi = halves[b] if what != "v" else (0, 0)
                if n == 0:
                    act.wait_ge(s_h, 9)
                if what == "v":
                    rows = min(P, NT - b * P)
                    at = {0: a * 512, 1: 1024, 2: 1536}[gi]
                    dst = V[:, b, a * 512:(a + 1) * 512] if b < 4 else Vs[:, at:at + 512]
                    act.activation(dst, ps[0:rows, bank, :], ACT.Copy).then_inc(s_zev, 1)
                elif what == "gl":
                    act.activation(gkl[:, lo:hi], ps[0:RANK, bank, 0:HALF], ACT.Copy).then_inc(s_zev, 1)
                elif what == "g":
                    act.activation(g4[:, a, lo:hi], ps[:, bank, 0:HALF], ACT.Identity, bias=S("b_gk")[:, a:a + 1]).then_inc(s_zev, 1)
                elif what == "q":
                    if gi == 0:
                        act.activation(q4[:, a, lo:hi], ps[:, bank, 0:HALF], ACT.Copy, scale=P ** -0.5).then_inc(s_zev, 1)
                    else:
                        act.activation(q4[:, a, lo:hi], ps[:, bank, 0:HALF], ACT.Silu).then_inc(s_zev, 1)
                else:
                    if gi == 0:
                        act.activation(k4[:, a, lo:hi], ps[:, bank, 0:HALF], ACT.Copy).then_inc(s_zev, 1)
                    else:
                        act.activation(k4[:, a, lo:hi], ps[:, bank, 0:HALF], ACT.Sigmoid).then_inc(s_zev, 1)
                n += 1
                if what == "v" and a == (gi == 0) and b in (1, 2):
                    first_factors(act, gi, b - 1)
                if what == "g" and (a, b) == (3, 1):
                    tmp_ = view(work, 10336, 4 * NT)
                    act.wait_ge(s_zev, n)
                    act.activation(tmp_, Gb, ACT.Abs).then_inc(s_gk, 1)
                    act.wait_ge(s_gk, 1)
                    act.activation(tmp_, tmp_, ACT.Exp, scale=-1.0).then_inc(s_gk, 1)
                    act.wait_ge(s_gk, 2)
                    act.activation(tmp_, tmp_, ACT.Ln, bias=1.0).then_inc(s_gk, 1)
                if gi and what == "q" and (a, b) == (3, 1):
                    act.wait_ge(s_kf, 4 * gi)
                    act.activation(Gb, Kb, ACT.Ln).then_inc(s_in, 1)
            recurrence_act(act, 2, copy_rows)

            def decay(b):
                act.wait_ge(s_si[b % 4], 16 * (b // 4 + 1))
                for h in range(12):
                    lo, hi = (h * GV, (h + 1) * GV) if h < GH else (1024 + (h - 4) * HV, 1024 + (h - 3) * HV)
                    act.activation(sin[:, b % 4, lo:hi], sin[:, b % 4, lo:hi], ACT.Copy, scale=sa_[:, h, b:b + 1]).then_inc(s_sa, 1)

            def open_gate(k):
                n, u = k // 4, k % 4
                act.wait_ge(s_p1, k + 1)
                if u == 0:
                    since(act, s_p3, n - 1)
                act.activation(gtmp[:, u // 2 + 2 * (n % 2), :], ps[:, 5 + k % 3, 0:HALF], ACT.Sigmoid).then_inc(s_p2, 1)

            for what, k in ORDER:
                if what == "B":
                    decay(k)
                elif what == "P" and k % 2 == 0:
                    open_gate(k)
                elif what == "N2":
                    act.wait_ge(s_sn2, 4)
                    act.activation(oms.rearrange("p j b -> p (j b)"), oms.rearrange("p j b -> p (j b)"), ACT.Sqrt).then_inc(s_lng, 1)

            layer_norm_act(act, 0)
            act.wait_ge(s_r1, 1)
            act.activation(OB[:, 0:4 * NE], ps[:, 0, 0:4 * NE], ACT.Sigmoid).then_inc(s_r2, 1)
            act.activation(scores[0:DEC, 4, :], ps[0:DEC, 0, 4 * NE:5 * NE], ACT.Sigmoid).then_inc(s_r2, 1)
            def factors_of(n):
                act.wait_ge(t_hh, n + 1)
                if n >= 1:
                    act.wait_ge(t_a, n)
                for k, fn in enumerate((ACT.Silu, ACT.Copy)):
                    act.activation(shg[:, k, :], ps[:, (1 + k, 6 + k)[n % 2], 0:HALF], fn).then_inc(t_sg, 1)

            factors_of(0)
            factors_of(1)
            for t in range(TT):
                rows = min(P, NT - t * P)
                for hf in range(2):
                    n = 2 * t + hf
                    act.wait_ge(s_ht, n + 1)
                    if t >= 2:
                        act.wait_ge(s_hd[t % 2], 16 * (t // 2))
                    act.activation(hrow[0:rows, t % 2, hf * 512:(hf + 1) * 512], ps[0:rows, 5 * (n % 2), :], ACT.Copy)\
                       .then_inc(s_hc, 1)
            factors_of(2)
            factors_of(3)
            act.wait_ge(s_et, 32)
            act.activation(eti[0:1, 0:MAXT + 4], erow, ACT.Copy).then_inc(s_eti, 1)
            for t in range(TT):
                rows = min(P, NT - t * P)
                if t >= 2:
                    act.wait_ge(t_st[t % 2], 16 * (t // 2))
                for hf in range(2):
                    act.wait_ge(t_y, 2 * t + hf + 1)
                    act.activation(yb[0:rows, t % 2, hf * 512:(hf + 1) * 512], ps[0:rows, (1, 6)[t % 2] + hf, :], ACT.Copy)\
                       .then_inc(t_yc, 1)
            act.wait_ge(s_T, 2)
            act.sem_inc(s_xc, 2)
            act.sem_inc(s_ac, 1)
            nq = act.value_load(qni[0:1, 0:1], min_val=1, max_val=MAXT // 4)

            def take_x(t, k):
                gate(act, "act", s_hh, t + 3)
                for hf in range(2):
                    gate(act, "act", s_xt, t * 2 + (9 + hf))
                    act.activation(xe[:, k % 2, 4 * hf:4 * hf + 4, :].rearrange("p c n -> p (c n)"), ps[:, 6 + hf, :],
                                   ACT.Copy).then_inc(s_xc, 1)

            def silu(t, k):
                gate(act, "act", s_hh, t + 5)
                gate(act, "act", s_a, t + 1)
                act.activation(sg[:, k % 2, :], ps[:, k % 2, 0:FE], ACT.Silu).then_inc(s_sg, 1)

            take_x(0, 0)
            silu(0, 0)
            take_x(1, 1)
            with act.Fori(0, nq) as i:
                for k in range(4):
                    gate(act, "act", s_at, i * 4 + (k + 1))
                    gate(act, "act", s_y, i * 8 + (2 * k + 6))
                    act.activation(aT[:, k % 2, :, :].rearrange("p f n -> p (f n)"), ps[:, 2, 0:2 * P], ACT.Copy)\
                       .then_inc(s_ac, 1)
                    silu(i * 4 + (k + 1), k + 1)
                    take_x(i * 4 + (k + 2), k)
            layer_norm_act(act, 1)

        @block.gpsimd
        def _(pool):
            pool.wait_ge(s_small, 48)
            for gi in range(3):
                v, base = GROUPS[gi]["v"], 16 * gi

                def mk(pair):
                    p = pair % 2
                    pool.wait_ge(s_E, 5 * pair + 2)
                    kk = k4[:, pair // 2 % 4, p * 256:(p + 1) * 256]
                    for l in range(LEV):
                        s = CH >> (l + 1)
                        e = M[:, p, l, :].rearrange("p (n s) -> p n s", s=2 * s)[:, :, 0:s]
                        pool.tensor_tensor(e, e, kk.rearrange("p (n s) -> p n s", s=2 * s)[:, :, 0:s], ALU.mult)
                    pool.tensor_tensor(M[:, p, 7, :], M[:, p, 7, :], kk, ALU.mult).then_inc(s_Mk, 1)

                def root(n):
                    ms, rs = ssum[:, n % 2:n % 2 + 1], rstd[:, n % 2:n % 2 + 1]
                    pool.wait_ge(s_ss, n + 1)
                    pool.tensor_scalar(ms, ms, 1.0 / v, EPS, ALU.mult, ALU.add).then_inc(s_rs, 1)
                    pool.wait_ge(s_rs, n + 1)
                    pool.tensor_tensor(rs, ms, C("mhalf"), ALU.pow).then_inc(s_rstd, 1)

                mk(8 * gi)
                mk(8 * gi + 1)
                if gi == 1:
                    pool.wait_ge(s_oc, 16)
                for c in range(1, 17):
                    root(base + c - 1)
                    if gi == 1:
                        gate_apply(pool, filled(gi, c - 1))
                    if c % 2 == 0 and c <= 12:
                        mk(8 * gi + c // 2 + 1)
            pool.wait_ge(s_ln, LN1)
            pool.memset(zrow, 0.0).then_inc(s_zero, 1)
            pool.wait_ge(s_zero, 1)
            pool.dma_start(ffrows[TRASH:ROWS, :], zrow).then_inc(s_add, 16)
            pool.dma_start(ffrows[NT:TRASH, :], zrow[0:TRASH - NT, :]).then_inc(s_add, 16)
            for n in range(4):
                lo, hi = halves[n // 2]
                pool.wait_ge(t_sg, 2 * n + 2)
                pool.tensor_tensor(shT[:, n % 2, lo:hi], shg[:, 0, :], shg[:, 1, :], ALU.mult).then_inc(t_a, 1)
            pool.wait_ge(s_slots, 1)
            for n in range(TT * TOPK):
                t, k = n // TOPK, n % TOPK
                if n >= 4:
                    pool.wait_ge(s_abp, n - 3)
                pool.tensor_scalar(Aoh[:, n % 4, :], R("iota")[:, 0:TS], slotk[:, t, k:k + 1], None, ALU.is_equal)\
                    .then_inc(s_abq, 1)
            pool.wait_ge(s_T, 2)
            rows_stored(pool)
            pool.wait_ge(s_add, 32)
            nq = pool.value_load(qni[0:1, 0:1], min_val=1, max_val=MAXT // 4)

            def gather(t, k, copied):
                gate(pool, "pool", s_xt, t * 2 + 2)
                pool.tensor_copy(idg[:, k:k + 1], idx_i[:, bass.ds(t, 1)]).then_inc(s_ic, 1)
                gate(pool, "pool", s_ic, copied)
                pool.indirect_dma_start(out=xg[k % 4], out_offset=None, in_=h2rows,
                                        in_offset=bass.IndirectOffsetOnAxis(ap=idg[0:TS, k:k + 1], axis=0)).then_inc(s_ga[k % 4], 16)

            gather(0, 0, 1)
            gather(1, 1, 2)
            gather(2, 2, 3)
            pool.wait_ge(t_st[0], 48)
            pool.wait_ge(t_st[1], 32)
            with pool.Fori(0, nq) as i:
                for k in range(4):
                    gather(i * 4 + (k + 3), (k + 3) % 4, i * 8 + (2 * k + 4))
                    gate(pool, "pool", s_add, i * 64 + (16 * k + 32))
                    pool.tensor_copy(ida[:, k:k + 1], idx_i[:, bass.ds(i * 4 + k, 1)]).then_inc(s_ic, 1)
                    gate(pool, "pool", s_yc, i * 8 + (2 * k + 4))
                    gate(pool, "pool", s_ic, i * 8 + (2 * k + 5))
                    pool.indirect_dma_start(out=ffrows, out_offset=bass.IndirectOffsetOnAxis(ap=ida[0:TS, k:k + 1], axis=0),
                                            in_=yb[0:TS, k % 2, :], in_offset=None, compute_op=ALU.add).then_inc(s_add, 16)
            for p in range(4):
                gate(pool, "pool", s_ga[p], nq * 16 + (16 if p < 3 else 0))

        @block.vector
        def _(dve):
            dve.wait_ge(s_small, 48)
            lb = S("lb").rearrange("p (r h) -> p r h", r=2)
            def lstep(ins, c=[0]):
                c[0] += 1
                ins.then_inc(s_lb, 1)
                dve.wait_ge(s_lb, c[0])
            for k, name in ((0, "gla_w"), (2, "hgrn_w")):
                w = S(name)
                dve.tensor_scalar(halfw[:, k:k + w.shape[1]], w, 0.5, None, ALU.mult).then_inc(s_hw, 1)
            dve.wait_ge(s_hw, 2)
            lstep(dve.tensor_tensor(lbm, lb[:, 0, :], lb[:, 1, :], ALU.max))
            lstep(dve.tensor_tensor(lbx[:, 0, :], lb[:, 0, :], lbm, ALU.subtract))
            lstep(dve.tensor_tensor(lbx[:, 1, :], lb[:, 1, :], lbm, ALU.subtract))
            def modulation(first, last, scale, done):
                n = last - first
                dve.tensor_tensor(md[:, first:last, :], ps[:, 5, first * NCOND:last * NCOND].rearrange("p (e n) -> p e n", n=NCOND),
                                  S("b_ada")[:, first:last].rearrange("p (e a) -> p e a", a=1).broadcast_to([P, n, NCOND]),
                                  ALU.add).then_inc(s_md, 1)
                dve.wait_ge(s_md, done + 1)
                dve.tensor_scalar(md[:, scale:scale + 8, :], md[:, scale:scale + 8, :], 1.0, None, ALU.add).then_inc(s_md, 1)

            dve.wait_ge(s_mt, 4)
            modulation(0, 16, SC1, 0)
            dve.wait_ge(s_md, 2)
            dve.wait_ge(s_x, 16)
            for c in range(KC):
                dve.tensor_scalar(H[:, c, 0:SEQ], X[:, c, 0:SEQ], md[:, SC1 + c, 0:1], md[:, SH1 + c, 0:1],
                                  ALU.mult, ALU.add).then_inc(s_h, 1)
            dve.tensor_tensor(H[:, :, SEQ:NT], X[:, :, SEQ:NT], md[:, SC1:SC1 + 8, 1:NCOND], ALU.mult).then_inc(s_md, 1)
            dve.wait_ge(s_md, 3)
            dve.tensor_tensor(H[:, :, SEQ:NT], H[:, :, SEQ:NT], md[:, SH1:SH1 + 8, 1:NCOND], ALU.add).then_inc(s_h, 1)

            for gi in range(3):
                g = GROUPS[gi]
                v, base = g["v"], 16 * gi
                if gi == 0:
                    dve.wait_ge(s_gk, 3)
                    dve.tensor_scalar(Gb, Gb, 0.0, None, ALU.min).then_inc(s_in, 1)
                    dve.wait_ge(s_in, 1)
                    dve.tensor_tensor(Gb, Gb, view(work, 10336, 4 * NT), ALU.subtract).then_inc(s_in, 1)
                    dve.wait_ge(s_in, 2)
                    dve.tensor_scalar(Gb, Gb, 1.0 / 16.0, None, ALU.mult).then_inc(s_in, 1)
                    dve.wait_ge(s_in, 3)
                    dve.wait_ge(s_lb, 4)
                    dve.tensor_tensor(lbm, lbx[:, 0, :], lbx[:, 1, :], ALU.add).then_inc(s_lb, 1)
                    dve.wait_ge(s_lb, 5)
                    dve.reciprocal(lbm, lbm).then_inc(s_lb, 1)
                    dve.wait_ge(s_lb, 6)
                    dve.tensor_tensor(lbt, lbx[:, 0, :], lbm, ALU.mult).then_inc(s_lb, 1)
                    dve.wait_ge(s_lb, 7)
                    dve.tensor_scalar(omlb, lbt, -1.0, 1.0, ALU.mult, ALU.add).then_inc(s_lb, 1)
                    dve.wait_ge(s_lb, 8)
                else:
                    dve.wait_ge(s_zev, taken(gi, "k"))
                    for h in range(4):
                        hd = 4 * (gi - 1) + h
                        dve.tensor_scalar(k4[:, h, :], k4[:, h, :], omlb[:, hd:hd + 1], lbt[:, hd:hd + 1],
                                          ALU.mult, ALU.add).then_inc(s_kf, 1)
                    dve.wait_ge(s_zev, taken(gi, "q"))
                    dve.tensor_scalar(Qb, Qb, P ** -0.5, None, ALU.mult).then_inc(s_fk, 1)
                    dve.wait_ge(s_kf, 4 * gi)
                    dve.wait_ge(s_in, 3 + gi)
                    dve.tensor_scalar(Kb, Kb, -1.0, 1.0, ALU.mult, ALU.add).then_inc(s_fk, 1)
                for h in range(4):
                    dve.tensor_tensor_scan(g4[:, h, :], C("reset"), g4[:, h, :], 0.0, ALU.mult, ALU.add).then_inc(s_cum, 1)
                dve.wait_ge(s_cum, 4 * gi + 4)
                if gi:
                    dve.wait_ge(s_fk, 2 * gi)
                else:
                    dve.wait_ge(s_zev, taken(0, "k"))
                dve.tensor_copy(sq_[:, 4 * gi:4 * gi + 4, :], q4[:, :, SEQ:NT]).then_inc(s_smp, 1)
                dve.tensor_copy(sk_[:, 4 * gi:4 * gi + 4, :], k4[:, :, SEQ:NT]).then_inc(s_smp, 1)

                def diffs(pair):
                    p = pair % 2
                    since(dve, s_sc, 2 * pair - 2)
                    b = g4[:, pair // 2 % 4, p * 256:(p + 1) * 256]
                    for l in range(LEV + 1):
                        w = CH >> l if l < LEV else CH
                        at = w // 2 - 1 if l < LEV else CH - 1
                        bb = b.rearrange("p (n s) -> p n s", s=w)
                        ins = dve.tensor_tensor(M[:, p, l, :].rearrange("p (n s) -> p n s", s=w), bb,
                                                bb[:, :, at:at + 1].broadcast_to([P, 256 // w, w]), ALU.subtract)
                    ins.then_inc(s_D, 1)

                def mq(pair):
                    p = pair % 2
                    qq = q4[:, pair // 2 % 4, p * 256:(p + 1) * 256]
                    dve.wait_ge(s_E, 5 * pair + 2)
                    for l in range(LEV):
                        s = CH >> (l + 1)
                        e = M[:, p, l, :].rearrange("p (n s) -> p n s", s=2 * s)[:, :, s:2 * s]
                        dve.tensor_tensor(e, e, qq.rearrange("p (n s) -> p n s", s=2 * s)[:, :, s:2 * s], ALU.mult)
                    dve.wait_ge(s_E, 5 * pair + 5)
                    dve.tensor_tensor(M[:, p, 8, :], M[:, p, 8, :], qq, ALU.mult).then_inc(s_Mq, 1)

                def mask(n):
                    dve.wait_ge(s_sc, n + 1)
                    since(dve, s_st, n)
                    dve.tensor_tensor(Pm, ps[:, 0:2, :].rearrange("p b t -> p (b t)"), C("masks"), ALU.mult).then_inc(s_pm, 1)
                    dve.wait_ge(s_pm, n + 1)
                    since(dve, s_o, n - 1)
                    dve.tensor_reduce(ST[:, n % 2, :], Pm.rearrange("p (l t) -> p t l", l=8), AX, ALU.add).then_inc(s_st, 1)

                def new_state(n):
                    cc = n % 4
                    dve.wait_ge(s_u, n + 1)
                    dst = state[:, (cc + 1) % 2 if cc < 3 else 2, 0:v]
                    if cc == 3:
                        since(dve, s_sout, n // 4 * 16)
                    else:
                        since(dve, s_o, n)
                    if cc:
                        dve.wait_ge(s_state, n)
                        dve.scalar_tensor_tensor(out=dst, in0=state[:, cc % 2, 0:v], scalar=elast[:, n // 2 % 2, n % 2:n % 2 + 1],
                                                 in1=ps[:, 3, 0:v], op0=ALU.mult, op1=ALU.add).then_inc(s_state, 1)
                    else:
                        dve.tensor_copy(dst, ps[:, 3, 0:v]).then_inc(s_state, 1)

                def take_o(n):
                    nj = v // P
                    h, cc = n // 4 % 4, n % 4
                    dve.wait_ge(s_ot, n + 1)
                    dst = g["out"][:, h * nj + g["first"]:(h + 1) * nj + g["first"], cc * CH:(cc + 1) * CH]
                    o = ps[:, 6, 0:v].rearrange("p (j t) -> p j t", t=CH)
                    if gi == 0:
                        for j in range(2):
                            ins = dve.tensor_scalar(dst[:, j, :], o[:, j, :], halfw[:, j:j + 1], None, ALU.mult)
                        ins.then_inc(s_oc, 1)
                    elif gi == 1:
                        dve.tensor_scalar(dst, o, halfw[:, 2:3], None, ALU.mult).then_inc(s_oc, 1)
                    else:
                        dve.wait_ge(s_g3, 16 + 4 * h + 1 + cc // 2)
                        dve.scalar_tensor_tensor(out=dst[:, 0, :], in0=o[:, 0, :], scalar=halfw[:, 2:3], in1=dst[:, 0, :],
                                                 op0=ALU.mult, op1=ALU.mult).then_inc(s_oc, 1)

                diffs(8 * gi)
                diffs(8 * gi + 1)
                mq(8 * gi)
                mq(8 * gi + 1)
                for c in range(18):
                    if c >= 2:
                        take_o(base + c - 2)
                    if c < 16:
                        mask(base + c)
                        new_state(base + c)
                    if gi and 1 <= c <= 16:
                        gate_value(dve, filled(gi, c - 1))
                    if c % 2 and c <= 11:
                        diffs(8 * gi + (c + 3) // 2)
                    if c % 2 == 0 and 2 <= c <= 12:
                        mq(8 * gi + c // 2 + 1)
                if gi == 0:
                    dve.wait_ge(s_mt, 12)
                    modulation(16, 48, SC2, 3)
                dve.wait_ge(s_oc, base + 16)
                dve.sem_inc(s_rec, 1)

            dve.wait_ge(s_g5, 16)
            dve.wait_ge(s_g3, 32)
            for k in range(2):
                a_gates = gdec[:, 0:8, :].rearrange("p (h k) b -> p h k b", k=2)[:, :, k, :]
                dve.tensor_scalar(a_gates, a_gates, halfw[:, k:k + 1], None, ALU.mult).then_inc(s_hw, 1)
            dve.tensor_scalar(gdec[:, 8:16, :], gdec[:, 8:16, :], halfw[:, 2:3], None, ALU.mult).then_inc(s_hw, 1)

            dve.wait_ge(s_smp, 9)
            dve.wait_ge(s_sout, 192)

            def new_states(b):
                since(dve, s_so[b % 2], 16 * (b // 2))
                since(dve, s_sop, b - 1)
                for h in range(12):
                    lo, hi = (h * GV, (h + 1) * GV) if h < GH else (1024 + (h - 4) * HV, 1024 + (h - 3) * HV)
                    dve.wait_ge(s_vb, 4 * b + lo // 512 + 1)
                    dve.wait_ge(s_sa, 12 * b + h + 1)
                    dve.scalar_tensor_tensor(out=snew[:, b % 2, lo:hi], in0=ps[:, lo // 512, lo % 512:lo % 512 + hi - lo],
                                             scalar=sk_[:, h, b:b + 1], in1=sin[:, b % 4, lo:hi],
                                             op0=ALU.mult, op1=ALU.add).then_inc(s_sn, 1)
            def norm_first():
                dve.wait_ge(s_sop, 8)
                dve.tensor_copy(oS.rearrange("p j b -> p (j b)"), ps[:, 4, 0:128]).then_inc(s_sn2, 1)
                dve.wait_ge(s_sn2, 1)
                dve.tensor_tensor(oS2, oS, oS, ALU.mult).then_inc(s_sn2, 1)

            def norm_rest():
                dve.wait_ge(s_sop, 9)
                sums = ps[:, 4, 128:256].rearrange("p (j b) -> p j b", b=DEC)
                dve.tensor_copy(oms, sums).then_inc(s_sn2, 1)
                dve.wait_ge(s_sn2, 3)
                pair = oms[:, 0:8, :].rearrange("p (h k) b -> p h k b", k=2)
                both = oS2[:, 0:8, :].rearrange("p (h k) b -> p h k b", k=2)
                for k in range(2):
                    ins = dve.tensor_tensor(both[:, :, k, :], pair[:, :, 0, :], pair[:, :, 1, :], ALU.add)
                ins.then_inc(s_mod, 1)
                dve.wait_ge(s_mod, 1)
                dve.tensor_scalar(oms[:, 0:8, :], oS2[:, 0:8, :], 1.0 / GV, EPS, ALU.mult, ALU.add).then_inc(s_mod, 1)
                dve.tensor_scalar(oms[:, 8:16, :], oms[:, 8:16, :], 1.0 / HV, EPS, ALU.mult, ALU.add).then_inc(s_sn2, 1)
                dve.wait_ge(s_mod, 2)
                dve.wait_ge(s_lng, 1)
                dve.reciprocal(oms, oms).then_inc(s_mod, 1)
                dve.wait_ge(s_mod, 3)
                dve.tensor_tensor(oS, oS, oms, ALU.mult).then_inc(s_mod, 1)
                dve.wait_ge(s_mod, 4)
                dve.wait_ge(s_hw, 5)
                dve.tensor_tensor(oa[:, :, SEQ:NT], oS[:, 0:8, :], gdec[:, 0:8, :], ALU.mult).then_inc(s_sn2, 1)
                dve.tensor_tensor(ob[:, :, SEQ:NT], oS[:, 8:16, :], gdec[:, 8:16, :], ALU.mult).then_inc(s_sn2, 1)
                dve.wait_ge(s_sn2, 6)

            def merged(k):
                n, u = k // 4, k % 4
                m, hf = MERGE[n]
                g = gtmp[:, u // 2 + 2 * (n % 2), :]
                dve.wait_ge(s_p2, k // 2 + 1)
                dve.wait_ge(s_p1, k + 1)
                dve.tensor_tensor(g, g, ps[:, 5 + k % 3, 0:HALF], ALU.mult).then_inc(s_p3a, 1)
                if u == 3:
                    if n == 4:
                        for b in range(2):
                            dve.wait_ge(s_so[b], 64)
                    dve.wait_ge(s_p3a, 2 * n + 2)
                    dve.tensor_tensor(mg[hf][:, m, :], gtmp[:, 2 * (n % 2), :], gtmp[:, 1 + 2 * (n % 2), :], ALU.add).then_inc(s_p3, 1)

            for what, k in ORDER:
                if what == "B":
                    new_states(k)
                elif what == "P" and k % 2:
                    merged(k)
                elif what == "N1":
                    norm_first()
                elif what == "N2":
                    norm_rest()
            dve.wait_ge(s_x2, 16)
            dve.tensor_scalar(Xb[:, :], Xb[:, :], ALPHA, None, ALU.mult).then_inc(s_fx, 1)
            dve.wait_ge(s_fx, 1)
            for m in range(KC):
                for hf, (lo, hi) in enumerate(halves):
                    n = 2 * m + hf
                    dve.wait_ge(s_o1, n + 1)
                    w = min(hi, SEQ) - lo
                    ins = dve.scalar_tensor_tensor(out=X[:, m, lo:lo + w], in0=ps[:, n % 2, 0:w], scalar=md[:, G1 + m, 0:1],
                                                   in1=X[:, m, lo:lo + w], op0=ALU.mult, op1=ALU.add)
                    if hi > SEQ:
                        dec = view(tiny, 200, DEC)
                        dve.tensor_tensor(dec, ps[:, n % 2, w:w + DEC], md[:, G1 + m, 1:NCOND], ALU.mult).then_inc(s_fx, 1)
                        dve.wait_ge(s_fx, m + 2)
                        ins = dve.tensor_tensor(X[:, m, SEQ:NT], X[:, m, SEQ:NT], dec, ALU.add)
                    ins.then_inc(s_o2, 1)
            dve.wait_ge(s_o2, 16)
            layer_norm_dve(dve, 0)
            for c in range(KC):
                dve.tensor_scalar(H[:, c, 0:SEQ], X[:, c, 0:SEQ], md[:, SC2 + c, 0:1], md[:, SH2 + c, 0:1],
                                  ALU.mult, ALU.add).then_inc(s_ln, 1)
            dve.tensor_tensor(H[:, :, SEQ:NT], X[:, :, SEQ:NT], md[:, SC2:SC2 + 8, 1:NCOND], ALU.mult).then_inc(s_ln, 1)
            dve.wait_ge(s_ln, LN1 - 1)
            dve.tensor_tensor(H[:, :, SEQ:NT], H[:, :, SEQ:NT], md[:, SH2:SH2 + 8, 1:NCOND], ALU.add).then_inc(s_ln, 1)

            dve.wait_ge(s_ln, LN1)
            dve.tensor_scalar(Xb[:, :], Xb[:, :], ALPHA, None, ALU.mult).then_inc(s_fx, 1)

            count = [0]

            def step(ins):
                ins.then_inc(s_rv, 1)
                count[0] += 1
                return ins

            def settled():
                dve.wait_ge(s_rv, count[0])

            dve.wait_ge(s_route, 16)
            dve.wait_ge(s_r2, 2)
            grouped = "p t (g k) -> p (t g) k"
            step(dve.tensor_tensor(biased, scores, R("bias").rearrange("p (a e) -> p a e", a=1).broadcast_to([P, TT, NE]), ALU.add))
            settled()
            for t in range(TT):
                for g in range(NG):
                    step(dve.max(g8[:, t, g, :], biased[:, t, g * 8:(g + 1) * 8]))
            settled()
            step(dve.tensor_tensor(grp, g8[:, :, :, 0], g8[:, :, :, 1], ALU.add))
            settled()
            for t in range(TT):
                step(dve.max(top[:, t, :], grp[:, t, :]))
            settled()
            for t in range(TT):
                step(dve.max_index(ui[:, t, :], top[:, t, :], grp[:, t, :]))
            settled()
            step(dve.tensor_copy(idxf, ui))
            settled()
            g4h = view(work, 0, TT * TOPG * NG, "p (t k g) -> p t k g", t=TT, k=TOPG)
            step(dve.tensor_tensor(g4h, R("group").rearrange("p (a b g) -> p a b g", a=1, b=1).broadcast_to([P, TT, TOPG, NG]),
                                   idxf[:, :, 0:TOPG].rearrange("p t (k a) -> p t k a", a=1).broadcast_to([P, TT, TOPG, NG]),
                                   ALU.is_equal))
            settled()
            step(dve.tensor_reduce(gm, g4h.rearrange("p t k g -> p t g k"), AX, ALU.add))
            settled()
            gmf = gm.rearrange("p t g -> p (t g)")
            gmx = gm.rearrange("p t (g a) -> p (t g) a", a=1)
            step(dve.tensor_tensor(tmp.rearrange(grouped, k=8), biased.rearrange(grouped, k=8),
                                   gmx.broadcast_to([P, TT * NG, 8]), ALU.mult))
            settled()
            step(dve.tensor_scalar(gmf, gmf, -1.0, BIG, ALU.add, ALU.mult))
            settled()
            step(dve.tensor_tensor(tmp.rearrange(grouped, k=8), tmp.rearrange(grouped, k=8),
                                   gmx.broadcast_to([P, TT * NG, 8]), ALU.add))
            settled()
            for t in range(TT):
                step(dve.max(top[:, t, :], tmp[:, t, :]))
            settled()
            for t in range(TT):
                step(dve.max_index(ui[:, t, :], top[:, t, :], tmp[:, t, :]))
            settled()
            step(dve.tensor_copy(idxf, ui))
            settled()
            step(dve.tensor_tensor(oh, R("iota")[:, 0:NE].rearrange("p (a b e) -> p a b e", a=1, b=1).broadcast_to([P, TT, TOPK, NE]),
                                   idxf.rearrange("p t (k a) -> p t k a", a=1).broadcast_to([P, TT, TOPK, NE]), ALU.is_equal))
            settled()
            dve.tensor_reduce(msk, oh.rearrange("p t k e -> p t e k"), AX, ALU.add).then_inc(s_msk, 1)
            dve.wait_ge(s_msk, 1)
            step(dve.tensor_tensor(tmp, scores, msk, ALU.mult))
            settled()
            step(dve.tensor_reduce(gsum, tmp, AX, ALU.add))
            settled()
            step(dve.reciprocal(gsum, gsum))
            settled()
            step(dve.tensor_scalar(gsum, gsum, RSCALE, None, ALU.mult))
            settled()
            step(dve.tensor_tensor(gates, scores, gsum.rearrange("p (t a) -> p t a", a=1).broadcast_to([P, TT, NE]), ALU.mult))
            dve.wait_ge(s_rp, 1)
            step(dve.tensor_copy(cnt, ps[:, 3, 0:NE]))
            settled()
            step(dve.tensor_scalar(nti, cnt, 0.0, None, ALU.is_gt))
            settled()
            for k in range(1, -(-NT // TS)):
                step(dve.scalar_tensor_tensor(out=nti, in0=cnt, scalar=float(TS * k), in1=nti, op0=ALU.is_gt, op1=ALU.add))
                settled()
            step(dve.tensor_tensor_scan(incl, ones[:, 0:NE], nti, 0.0, ALU.mult, ALU.add))
            settled()
            step(dve.tensor_scalar(cmp_, incl, R("part"), None, ALU.is_le))
            step(dve.tensor_tensor(excl, incl, nti, ALU.subtract))
            settled()
            step(dve.tensor_reduce(ecol, cmp_, AX, ALU.add))
            settled()
            dve.tensor_scalar(ecol, ecol, float(NE - 1), None, ALU.min).then_inc(s_row, 1)
            step(dve.tensor_scalar(cmp_[:, 0:MAXT // 4], R("quads"), incl[:, NE - 1:NE], None, ALU.is_lt))
            settled()
            step(dve.tensor_reduce(quadn, cmp_[:, 0:MAXT // 4], AX, ALU.add))
            settled()
            dve.tensor_copy(qni[0:1, 0:1], quadn[0:1, :]).then_inc(s_T, 1)
            for t, r in ((slice(0, 4), P), (slice(4, 5), DEC)):
                n = t.stop - t.start
                step(dve.scalar_tensor_tensor(out=pos[0:r, t, :], in0=excl[0:r, :].rearrange("p (a e) -> p a e", a=1).broadcast_to([r, n, NE]),
                                              scalar=float(TS), op0=ALU.mult, op1=ALU.add,
                                              in1=ps[0:r, 4, t.start * NE:t.stop * NE].rearrange("p (t e) -> p t e", t=n)))
            settled()
            for dst, src in ((posk, pos), (gk, gates)):
                step(dve.tensor_tensor(prod, oh, src.rearrange("p t (a e) -> p t a e", a=1).broadcast_to([P, TT, TOPK, NE]), ALU.mult))
                settled()
                step(dve.tensor_reduce(dst, prod, AX, ALU.add))
                settled()
            step(dve.tensor_copy(posi, posk.rearrange("p t k -> p (t k)")))
            settled()
            step(dve.tensor_scalar(hi_i, posi, 7, None, ALU.arith_shift_right))
            settled()
            tile_, slot_, pos_ = (v.rearrange("p t k -> p (t k)") for v in (tilek, slotk, posk))
            step(dve.tensor_copy(tile_, hi_i))
            settled()
            dve.scalar_tensor_tensor(out=slot_, in0=tile_, scalar=-float(TS), in1=pos_, op0=ALU.mult, op1=ALU.add).then_inc(s_slots, 1)
            n = 0
            for t in range(TT):
                for k in range(TOPK):
                    if n >= 4:
                        dve.wait_ge(s_abp, n - 3)
                    tile = tilek[:, t, k:k + 1]
                    upto = R("iota")[:, 0:MAXT]
                    dve.tensor_scalar(Boh[:, n % 4, 0, :], upto, tile, R("token")[:, t:t + 1], ALU.is_equal, ALU.mult).then_inc(s_ab, 1)
                    dve.tensor_scalar(Boh[:, n % 4, 1, :], upto, tile, gk[:, t, k:k + 1], ALU.is_equal, ALU.mult).then_inc(s_ab, 1)
                    dve.tensor_scalar(Boh[:, n % 4, 2, :], upto, tile, None, ALU.is_equal).then_inc(s_ab, 1)
                    n += 1
            dve.wait_ge(s_abp, 40)
            tok, gat, use = (ps[0:TS, 5, c * MAXT:(c + 1) * MAXT] for c in range(3))
            step(dve.tensor_copy(gtabs[0:TS, 0:MAXT], gat))
            step(dve.memset(gtabs[:, MAXT:MAXT + 4], 0.0))
            step(dve.memset(idxt[:, MAXT:MAXT + 4], 1.0))
            step(dve.tensor_scalar(idxt[0:TS, 0:MAXT], use, -1.0, 1.0, ALU.mult, ALU.add))
            settled()
            step(dve.tensor_scalar(idxt[0:TS, :], idxt[0:TS, :], R("trash")[0:TS, :], None, ALU.mult))
            settled()
            step(dve.tensor_tensor(idxt[0:TS, 0:MAXT], idxt[0:TS, 0:MAXT], tok, ALU.add))
            settled()
            dve.tensor_copy(idx_i[0:TS, :], idxt[0:TS, :]).then_inc(s_T, 1)

            dve.wait_ge(t_st[0], 48)
            dve.wait_ge(t_st[1], 32)
            dve.sem_inc(s_a, 2)
            dve.sem_inc(s_yc, 2)
            dve.wait_ge(s_T, 2)
            nq = dve.value_load(qni[0:1, 0:1], min_val=1, max_val=MAXT // 4)

            def gated(t, k, copied):
                dve.tensor_copy(gcol[:, k % 4:k % 4 + 1], gtabs[:, bass.ds(t, 1)]).then_inc(s_gc, 1)
                gate(dve, "dve", s_gc, copied)
                gate(dve, "dve", s_sg, t + 1)
                dve.scalar_tensor_tensor(out=av[:, k % 2, :], in0=ps[:, k % 2, FE:2 * FE], scalar=gcol[:, k % 4:k % 4 + 1],
                                         in1=sg[:, k % 2, :], op0=ALU.mult, op1=ALU.mult).then_inc(s_a, 1)

            gated(0, 0, 1)
            with dve.Fori(0, nq) as i:
                for k in range(4):
                    gated(i * 4 + (k + 1), k + 1, i * 4 + (k + 2))
                    gate(dve, "dve", s_add, i * 64 + (16 * k + 16))
                    for hf in range(2):
                        gate(dve, "dve", s_y, i * 8 + (2 * k + hf + 9))
                        dve.tensor_copy(yb[:, k % 2, hf * 512:(hf + 1) * 512], ps[:, 4 + hf, :]).then_inc(s_yc, 1)

            for t in range(TT):
                rows = min(P, NT - t * P)
                for hf in range(2):
                    n = 2 * t + hf
                    dve.wait_ge(s_f2, n + 1)
                    if t < 4:
                        for c in range(4):
                            m = 4 * hf + c
                            ins = dve.scalar_tensor_tensor(out=X[:, m, t * P:(t + 1) * P], in0=ps[:, n % 2, c * P:(c + 1) * P],
                                                           scalar=md[:, G2 + m, 0:1], in1=X[:, m, t * P:(t + 1) * P],
                                                           op0=ALU.mult, op1=ALU.add)
                    else:
                        four = slice(4 * hf, 4 * hf + 4)
                        dec = view(tiny, 184 + 32 * hf, 4 * DEC, "p (c b) -> p c b", c=4)
                        dve.tensor_tensor(dec, ps[:, n % 2, :].rearrange("p (c t) -> p c t", c=4)[:, :, 0:DEC],
                                          md[:, G2 + 4 * hf:G2 + 4 * hf + 4, 1:NCOND], ALU.mult).then_inc(s_fy, 1)
                        dve.wait_ge(s_fy, hf + 1)
                        ins = dve.tensor_tensor(X[:, four, SEQ:NT], X[:, four, SEQ:NT], dec, ALU.add)
                    ins.then_inc(s_f3, 1)
            dve.wait_ge(s_f3, 2 * TT)
            layer_norm_dve(dve, 1)


def kernel(**inputs):
    import concourse.bacc as bacc
    from concourse.bass_utils import run_bass_kernel_spmd as run

    a = {k: np.asarray(v) for k, v in inputs.items()}

    def rows(x):
        return x.reshape(-1, KC, P).transpose(2, 1, 0)

    def blocks(w):
        return w.reshape(KC, P, -1, P).transpose(2, 1, 0, 3).reshape(-1, P, KC * P)

    xT = rows(np.concatenate([a["x_prompt"][0], a["x_sample"][:, 0]])).reshape(P, KC * NT)
    w_in = a["w_in"][0]
    cuts = np.cumsum([0, 512, 512, 1024, 1024, 16, 1024, 1024, 1024, 1024, 1024, 1024])
    qa, ka, va, ga, gk, qb, fb, ib, gb, ua, ub = (w_in[:, cuts[i]:cuts[i + 1]] for i in range(11))
    B = blocks
    merge = np.stack([B(ua), B(a["w_proj_a"][0]), B(ub), B(a["w_proj_b"][0])], 1).reshape(4 * KC, P, KC * P)
    ada = B(a["w_ada"][0]).reshape(3, 4 * 4, P, KC * P)
    wq = np.concatenate([ada[0], B(qa), B(ka), B(va), ada[1], ada[2],
                         B(fb[:, :512]), B(qb[:, :512]), B(ib[:, :512]), B(ga),
                         B(fb[:, 512:]), B(qb[:, 512:]), B(ib[:, 512:]), B(gb), merge, B(a["w_out"][0])])
    wq = wq.reshape(NQ, 4, P, KC * P).transpose(0, 2, 1, 3).reshape(NQ, P, 4 * KC * P)
    col = lambda x: x.reshape(-1, P).T
    small = np.concatenate([
        rows(np.concatenate([a["c_prompt"], a["c_sample"]])).reshape(P, -1), col(a["b_ada"][0]), col(a["b_gk"][0]),
        col(a["hgrn_lb"]), col(a["gla_norm_w"][0]), col(a["hgrn_norm_w"][0]), col(a["ln1_g"][0]), col(a["ln1_b"][0]),
        col(a["ln2_g"][0]), col(a["ln2_b"][0]), gk.reshape(KC, P, RANK).transpose(1, 0, 2).reshape(P, -1)], 1)
    const, route = constants()
    at, n = ROUTE["bias"]
    route[:, at:at + n] = np.broadcast_to(a["router_bias"][0], (P, NE))
    at, n = ROUTE["w"]
    route[:, at:at + n] = a["w_router"][0].reshape(KC, P, NE).transpose(1, 0, 2).reshape(P, -1)

    def expert(g, u, d):
        gu = np.concatenate([g.reshape(-1, KC, P, FE), u.reshape(-1, KC, P, FE)], 3)
        return np.concatenate([gu.transpose(0, 2, 1, 3).reshape(-1, P, 4096),
                               d.reshape(-1, 2, P, D).transpose(0, 2, 1, 3).reshape(-1, P, 2048)], 2)

    wexp = np.concatenate([expert(a["w_exp_gate"][0], a["w_exp_up"][0], a["w_exp_down"][0]),
                           expert(a["w_sh_gate"], a["w_sh_up"], a["w_sh_down"])])
    st_in = np.concatenate([a["state_gla"][0].transpose(0, 2, 1, 3).reshape(DEC, P, GH * GV),
                            a["state_hgrn"][0].transpose(0, 2, 1, 3).reshape(DEC, P, HH * HV)], 2)
    ins = dict(xT=xT, small=small, wgk2=a["w_gk2"][0], const=const, route=route, wq=wq, wexp=wexp, st_in=st_in)
    ins = {k: np.ascontiguousarray(v) for k, v in ins.items()}

    nc = bacc.Bacc("TRN2", target_bir_lowering=False, num_devices=1)
    aps = {k: nc.dram_tensor(k, v.shape, F32, kind="ExternalInput").ap() for k, v in ins.items()}
    outs = dict(yT=(P, KC * NT), st_prompt=(P, 2048), st_out=(DEC, P, 2048))
    aps.update({k: nc.dram_tensor(k, s, F32, kind="ExternalOutput").ap() for k, s in outs.items()})
    decoder_step(nc, **aps)
    r = run(nc, [ins], core_ids=[0]).results[0]
    y = r["yT"].reshape(P, KC, NT).transpose(2, 1, 0).reshape(NT, D)
    sp, so = r["st_prompt"], r["st_out"]
    gla = lambda s: s[..., :1024].reshape(-1, P, GH, GV).transpose(0, 2, 1, 3)[None]
    hgrn = lambda s: s[..., 1024:].reshape(-1, P, HH, HV).transpose(0, 2, 1, 3)[None]
    c = np.ascontiguousarray
    return (c(y[None, :SEQ]), c(y[SEQ:, None]), c(gla(sp[None])), c(hgrn(sp[None])), c(gla(so)), c(hgrn(so)))
```
